# Optimizing a Trainium2 kernel written in Bass

```python
import math
import jax, jax.numpy as jnp
from jax import lax
import numpy as np

D_MODEL = 1024
BATCH = 1
SEQ = 512
DEPTH = 2

N_EVEN = (DEPTH + 1) // 2
N_ODD = DEPTH // 2
A_HEADS = 8
A_HEAD_DIM = 64
IDX_HEADS = 4
IDX_DIM = 64
TOPK_MAX = 256
Q_BLOCK = 128
B_HEADS = 4
B_DK = 64
B_DV = 128
GLA_RANK = 16
GLA_TAU = 16.0
GLA_CHUNK = 64
C_WIDTH = D_MODEL
CONV_WIDTH = 31
REL_BUCKETS = 32
REL_MAX_EXACT = 16
REL_MAX_DIST = 128
EPS = 1e-6

A_W = A_HEADS * A_HEAD_DIM
B_KW = B_HEADS * B_DK
B_VW = B_HEADS * B_DV
EVEN_SPLIT = [A_W, A_W, A_W, A_W,
              IDX_HEADS * IDX_DIM, IDX_DIM, IDX_HEADS,
              B_KW, B_KW, B_VW, B_VW, GLA_RANK]
EVEN_COLS = int(sum(EVEN_SPLIT))
ODD_SPLIT = [C_WIDTH, C_WIDTH, C_WIDTH]
ODD_COLS = int(sum(ODD_SPLIT))
MIX_W = A_W + B_VW

kernel_name = "hybrid_dsa_gla_conformer_block"

def _split(x, sizes):
    return jnp.split(x, [int(v) for v in np.cumsum(sizes)[:-1]], axis=-1)

def rmsnorm(x, g):
    xf = x.astype(jnp.float32)
    y = xf * lax.rsqrt(jnp.mean(xf * xf, axis=-1, keepdims=True) + EPS)
    return (y * g.astype(jnp.float32)).astype(x.dtype)

def layernorm(x, g, b):
    xf = x.astype(jnp.float32)
    mu = jnp.mean(xf, axis=-1, keepdims=True)
    var = jnp.mean(jnp.square(xf - mu), axis=-1, keepdims=True)
    y = (xf - mu) * lax.rsqrt(var + EPS)
    return (y * g.astype(jnp.float32) + b.astype(jnp.float32)).astype(x.dtype)

def t5_bucket(dist):
    dist = jnp.maximum(dist, 0)
    is_small = dist < REL_MAX_EXACT
    d = jnp.maximum(dist, 1).astype(jnp.float32)
    large = REL_MAX_EXACT + (jnp.log(d / REL_MAX_EXACT)
                             / math.log(REL_MAX_DIST / REL_MAX_EXACT)
                             * (REL_BUCKETS - REL_MAX_EXACT)).astype(jnp.int32)
    large = jnp.minimum(large, REL_BUCKETS - 1)
    return jnp.where(is_small, dist, large)

def dsa_attention(q, k, v, q_idx, k_idx, w_idx, rel_bias, top_k):
    B, S, H, Dh = q.shape
    n_blocks = S // Q_BLOCK
    s_pos = jnp.arange(S, dtype=jnp.int32)
    scale = Dh ** -0.5
    idx_scale = (IDX_DIM ** -0.5) * (IDX_HEADS ** -0.5)

    def block(i):
        t0 = i * Q_BLOCK
        t = t0 + jnp.arange(Q_BLOCK, dtype=jnp.int32)
        qi = lax.dynamic_slice_in_dim(q_idx, t0, Q_BLOCK, axis=1)
        wi = lax.dynamic_slice_in_dim(w_idx, t0, Q_BLOCK, axis=1)
        qa = lax.dynamic_slice_in_dim(q, t0, Q_BLOCK, axis=1)
        sc = jax.nn.relu(jnp.einsum('bqhd,bsd->bqhs', qi, k_idx).astype(jnp.float32))
        score = jnp.einsum('bqh,bqhs->bqs', wi.astype(jnp.float32), sc) * idx_scale
        score = jnp.where(s_pos[None, None, :] <= t[None, :, None], score, -jnp.inf)
        _, sel = lax.top_k(score, top_k)
        valid = sel <= t[None, :, None]
        ks = jax.vmap(lambda a, ii: a[ii])(k, sel)
        vs = jax.vmap(lambda a, ii: a[ii])(v, sel)
        logits = jnp.einsum('bqhd,bqkhd->bhqk', qa, ks).astype(jnp.float32) * scale
        bias = rel_bias.astype(jnp.float32)[t5_bucket(t[None, :, None] - sel)]
        logits = logits + jnp.transpose(bias, (0, 3, 1, 2))
        logits = jnp.where(valid[:, None, :, :], logits, -jnp.inf)
        p = jax.nn.softmax(logits, axis=-1).astype(vs.dtype)
        return jnp.einsum('bhqk,bqkhd->bqhd', p, vs)

    out = lax.map(block, jnp.arange(n_blocks, dtype=jnp.int32))
    return jnp.transpose(out, (1, 0, 2, 3, 4)).reshape(B, S, H, Dh)

def gla(q, k, v, log_a):
    B, S, H, DK = q.shape
    DV = v.shape[-1]
    C = GLA_CHUNK
    N = S // C

    def to_chunks(t):
        return jnp.transpose(t.astype(jnp.float32).reshape(B, N, C, H, t.shape[-1]),
                             (1, 0, 3, 2, 4))

    qc = to_chunks(q) * (DK ** -0.5)
    kc, vc = to_chunks(k), to_chunks(v)
    bc = jnp.cumsum(to_chunks(log_a), axis=-2)
    causal = jnp.tril(jnp.ones((C, C), dtype=bool))

    def step(state, inp):
        qi, ki, vi, bi = inp
        o_inter = jnp.einsum('bhcd,bhde->bhce', qi * jnp.exp(bi), state)
        diff = bi[:, :, :, None, :] - bi[:, :, None, :, :]
        decay = jnp.exp(jnp.where(causal[None, None, :, :, None], diff, -jnp.inf))
        att = jnp.einsum('bhid,bhjd,bhijd->bhij', qi, ki, decay)
        o_intra = jnp.einsum('bhij,bhje->bhie', att, vi)
        b_last = bi[:, :, -1:, :]
        new_state = (jnp.exp(b_last[:, :, 0, :])[..., None] * state
                     + jnp.einsum('bhjd,bhje->bhde', ki * jnp.exp(b_last - bi), vi))
        return new_state, o_inter + o_intra

    s0 = jnp.zeros((B, H, DK, DV), jnp.float32)
    _, out = lax.scan(step, s0, (qc, kc, vc, bc))
    return jnp.transpose(out, (1, 0, 3, 2, 4)).reshape(B, S, H, DV)

def causal_depthwise_conv(u, w, b):
    Cc = u.shape[-1]
    y = lax.conv_general_dilated(
        u, w.astype(u.dtype)[:, None, :], window_strides=(1,),
        padding=[(CONV_WIDTH - 1, 0)],
        dimension_numbers=('NWC', 'WIO', 'NWC'), feature_group_count=Cc)
    return y + b.astype(u.dtype)

def setup_inputs(seed: int = 0) -> dict:
    key = jax.random.key(seed)
    ks = jax.random.split(key, 20)
    f32 = jnp.float32
    nrm = lambda k, shape, s: jax.random.normal(k, shape, f32) * s
    return {
        "x": nrm(ks[0], (BATCH, SEQ, D_MODEL), 1.0),
        "rel_bias": nrm(ks[1], (REL_BUCKETS, A_HEADS), 0.5),
        "norm_even": 1.0 + nrm(ks[2], (N_EVEN, D_MODEL), 0.02),
        "w_in_even": nrm(ks[3], (N_EVEN, D_MODEL, EVEN_COLS), D_MODEL ** -0.5),
        "w_gla_lr": nrm(ks[4], (N_EVEN, GLA_RANK, B_KW), GLA_RANK ** -0.5),
        "b_gla_lr": nrm(ks[5], (N_EVEN, B_KW), 0.1),
        "gla_norm": 1.0 + nrm(ks[6], (N_EVEN, B_DV), 0.02),
        "w_out_even": nrm(ks[7], (N_EVEN, MIX_W, D_MODEL), MIX_W ** -0.5),
        "norm_odd": 1.0 + nrm(ks[8], (N_ODD, D_MODEL), 0.02),
        "w_in_odd": nrm(ks[9], (N_ODD, D_MODEL, ODD_COLS), D_MODEL ** -0.5),
        "conv_w": nrm(ks[10], (N_ODD, CONV_WIDTH, C_WIDTH), CONV_WIDTH ** -0.5),
        "conv_b": nrm(ks[11], (N_ODD, C_WIDTH), 0.02),
        "conv_ln_g": 1.0 + nrm(ks[12], (N_ODD, C_WIDTH), 0.02),
        "conv_ln_b": nrm(ks[13], (N_ODD, C_WIDTH), 0.02),
        "w_out_odd": nrm(ks[14], (N_ODD, C_WIDTH, D_MODEL), C_WIDTH ** -0.5),
        "norm_f": 1.0 + nrm(ks[15], (D_MODEL,), 0.02),
    }

def reference(x, rel_bias, norm_even, w_in_even, w_gla_lr, b_gla_lr, gla_norm,
              w_out_even, norm_odd, w_in_odd, conv_w, conv_b, conv_ln_g,
              conv_ln_b, w_out_odd, norm_f):
    B, S, _ = x.shape
    top_k = min(TOPK_MAX, S // 4)
    for layer in range(DEPTH):
        if layer % 2 == 0:
            i = layer // 2
            h = rmsnorm(x, norm_even[i])
            proj = h @ w_in_even[i]
            (qa, ka, va, ga, qi, ki, wi, qb, kb, vb, gb, lr) = _split(proj, EVEN_SPLIT)
            o_a = dsa_attention(
                qa.reshape(B, S, A_HEADS, A_HEAD_DIM),
                ka.reshape(B, S, A_HEADS, A_HEAD_DIM),
                va.reshape(B, S, A_HEADS, A_HEAD_DIM),
                qi.reshape(B, S, IDX_HEADS, IDX_DIM), ki, wi, rel_bias, top_k)
            o_a = o_a.reshape(B, S, A_W) * jax.nn.silu(ga)
            z = lr @ w_gla_lr[i] + b_gla_lr[i]
            log_a = jax.nn.log_sigmoid(z.astype(jnp.float32)) / GLA_TAU
            o_b = gla(qb.reshape(B, S, B_HEADS, B_DK),
                      kb.reshape(B, S, B_HEADS, B_DK),
                      vb.reshape(B, S, B_HEADS, B_DV),
                      log_a.reshape(B, S, B_HEADS, B_DK))
            o_b = o_b * lax.rsqrt(jnp.mean(o_b * o_b, axis=-1, keepdims=True) + EPS)
            o_b = (o_b * gla_norm[i].astype(jnp.float32)).astype(x.dtype)
            o_b = o_b.reshape(B, S, B_VW) * jax.nn.silu(gb)
            x = x + jnp.concatenate([o_a, o_b], axis=-1) @ w_out_even[i]
        else:
            j = layer // 2
            h = rmsnorm(x, norm_odd[j])
            proj = h @ w_in_odd[j]
            val, glu_g, gate = _split(proj, ODD_SPLIT)
            u = val * jax.nn.sigmoid(glu_g)
            u = causal_depthwise_conv(u, conv_w[j], conv_b[j])
            u = jax.nn.silu(layernorm(u, conv_ln_g[j], conv_ln_b[j]))
            x = x + (u * jax.nn.silu(gate)) @ w_out_odd[j]
    return rmsnorm(x, norm_f)


_drawn_inputs = setup_inputs


def setup_inputs(seed=0):
    import zlib

    import numpy as np

    out = dict(_drawn_inputs(seed))
    spreads = {}
    factors = {'norm_even': 2.949,
     'b_gla_lr': 2.97,
     'gla_norm': 6.568,
     'norm_odd': 6.336,
     'conv_b': 4.409,
     'conv_ln_g': 7.643,
     'conv_ln_b': 8.0,
     'norm_f': 2.864}
    for name, (base, spread) in spreads.items():
        noise = np.random.default_rng([zlib.crc32(name.encode()), seed]).standard_normal(out[name].shape)
        drawn = base * np.exp(spread * noise) if base else spread * noise
        out[name] = __import__('jax').numpy.asarray(drawn.astype(out[name].dtype))
    for name, factor in factors.items():
        out[name] = (out[name] * factor).astype(out[name].dtype)
    return out
```

```python
from contextlib import ExitStack

import concourse.bass as bass
from concourse import mybir

F32 = mybir.dt.float32
F32R = mybir.dt.float32r
BF16 = mybir.dt.bfloat16
I32 = mybir.dt.int32
U8 = mybir.dt.uint8
ALU = mybir.AluOpType
ACT = mybir.ActivationFunctionType
AX = mybir.AxisListType

P = 128
D = 1024
S = 512
KC = D // P
TB = S // P
EPS = 1e-6
AH, AD = 8, 64
IH, ID = 4, 64
BH, DK, DV = 4, 64, 128
RANK = 16
TAU = 16.0
TOPK = min(256, S // 4)
CW = 31
NB, MAXEX, MAXD = 32, 16, 128
NEG = -1.0e30
HIDDEN = -2.0e38
TAKEN = -3.0e38

C_QA, C_KA, C_VA, C_GA = 0, 512, 1024, 1536
C_QI = 2048
C_KI = C_QI + IH * ID
C_WI = C_KI + ID
C_QB = C_WI + IH
C_KB = C_QB + BH * DK
C_VB = C_KB + BH * DK
C_GB = C_VB + BH * DV
C_LR = C_GB + BH * DV


def bucket_starts():
    import math
    first = {}
    for d in range(S):
        if d < MAXEX:
            b = d
        else:
            b = min(NB - 1, MAXEX + int(math.log(d / MAXEX) / math.log(MAXD / MAXEX) * (NB - MAXEX) + 1e-6))
        first.setdefault(b, d)
    return [first[b] for b in range(NB)]


def plan_slots():
    a = lambda m, c: ("a", (0,), [(0, m, c, 256)])
    b = lambda m, c, ks: [("b", ks[0:4], [(0, m, c, 512)]), ("b", ks[4:8], [(0, m, c, 512)])]
    up = tuple(range(KC))
    s = [a("e", C_QI),
         ("a", (0,), [(0, "e", C_KI, ID), (ID, "e", C_KI, ID), (128, "e", C_LR, RANK), (144, "e", C_WI, IH)]),
         a("e", C_QB), a("e", C_KB)]
    s += b("e", C_VB, up)
    s += [a("e", C_QA), a("e", C_QA + 256), a("e", C_KA), a("e", C_KA + 256)]
    s += b("e", C_VA, up) + b("e", C_GA, up) + b("e", C_GB, up)
    s += b("oe", 0, up) + b("oe", 512, up)
    vg = lambda c: ("a", (0,), [(0, "o", c * P, P), (P, "o", D + c * P, P)])
    gate = lambda n: a("o", 2 * D + n * 256)
    s += [vg(0), vg(1), gate(0), vg(2), vg(3), gate(1), vg(4), vg(5), gate(2), vg(6), vg(7), gate(3)]
    s += b("oo", 0, up) + b("oo", 512, up)
    return s


def hybrid_trunk(nc, x, rel_bias, norm_even, w_in_even, w_gla_lr, b_gla_lr, gla_norm, w_out_even,
                 norm_odd, w_in_odd, conv_w, conv_b, conv_ln_g, conv_ln_b, w_out_odd, norm_f, out):
    SLOTS = plan_slots()
    NS = len(SLOTS)
    WSRC = {"e": w_in_even[0], "oe": w_out_even[0], "o": w_in_odd[0], "oo": w_out_odd[0]}
    S_VB, S_QA, S_KA, S_VA, S_GA, S_GB, S_OE, S_ODD, S_OO = 4, 6, 8, 10, 12, 14, 16, 20, 32
    FIRST, evac_by = {}, []
    CHUNK, GATE = {}, {}
    for j, (kind, ks, pieces) in enumerate(SLOTS):
        if kind == "a":
            FIRST[j] = len(evac_by)
            if S_ODD <= j < S_OO:
                c0 = pieces[0][2]
                if c0 < D:
                    CHUNK[j] = c0 // P
                    evac_by += ["val", "act"]
                else:
                    GATE[j] = (c0 - 2 * D) // P
                    evac_by += ["act", "act"]
            else:
                evac_by += ["act", "act"]
        elif j % 2 == 0:
            FIRST[j] = FIRST[j + 1] = len(evac_by)
            evac_by += ["residual" if j >= S_OE else "act"] * TB

    def evacs_through(g, who):
        return sum(1 for e in evac_by[:g + 1] if e == who)

    raw_full, n_in = {}, [0, 0]
    for j, (_, ks, pieces) in enumerate(SLOTS):
        n_in[j % 2] += 16 * len(pieces)
        raw_full[j] = n_in[j % 2]

    ctx = ExitStack()
    with ctx:
        def sb(name, shape, dt=F32):
            return ctx.enter_context(nc.sbuf_tensor(name, shape, dt))

        def sem(name):
            return ctx.enter_context(nc.semaphore(name))

        w_raw = [sb(f"w_raw{i}", [P, 2048]) for i in range(2)]
        w_hi = [sb(f"w_hi{i}", [P, 2048], F32R) for i in range(3)]
        w_lo = [sb(f"w_lo{i}", [P, 2048], F32R) for i in range(3)]
        hT_hi = sb("hT_hi", [P, KC, S], F32R)
        hT_lo = sb("hT_lo", [P, KC, S], F32R)
        r_x = sb("r_x", [P, 4096])
        r_oa = sb("r_oa", [P, 2048])
        r_ob = sb("r_ob", [P, 2048])
        r_qa = sb("r_qa", [P, 2048])
        r_ka = sb("r_ka", [P, 2048])
        r_va = sb("r_va", [P, 2048])
        r_vb = sb("r_vb", [P, 2048])
        r_qkb = sb("r_qkb", [P, 2048])
        r_g = sb("r_g", [P, 4096])
        r_att = sb("r_att", [P, 2048])
        neg_mask = sb("neg_mask", [P, 1280], BF16)
        ident = sb("ident", [P, P])
        ident_bf = sb("ident_bf", [P, P], BF16)
        ones = sb("ones", [P, P])
        level_mask = sb("level_mask", [P, 6, P], U8)
        NROW = CW + 5
        pvec = sb("pvec", [P, KC, NROW])
        pb3 = sb("pb3", [P, 4])
        small_rows = sb("small_rows", [3, P])
        rel_rows = sb("rel_rows", [AH, NB])
        w_lr = sb("w_lr", [RANK, BH * DK])
        lwT = sb("lwT", [RANK + IH, S])
        wi = sb("wi", [P, TB, IH])
        stat = sb("stat", [P, 16])
        rstd = sb("rstd", [P, 16])
        minus_half = sb("minus_half", [P, 16])
        top8 = sb("top8", [P, 8])
        row_max = sb("row_max", [P, TB * AH])
        neg_max = sb("neg_max", [P, TB * AH])
        row_sum = sb("row_sum", [P, TB * AH])
        row_inv = sb("row_inv", [P, TB * AH])
        chunk_decay = sb("chunk_decay", [P, 2, TB])
        state = sb("state", [P, TB, 2 * DV])

        x_t = r_x[:].rearrange("p (t d) -> p t d", t=TB)
        bias_tab = r_x[:].rearrange("p (h u) -> p h u", h=AH)
        oa = r_oa[:].rearrange("p (t d) -> p t d", t=TB)
        ob = r_ob[:].rearrange("p (t d) -> p t d", t=TB)
        qaT = r_qa[:].rearrange("p (c t) -> p c t", c=4)
        kaT = r_ka[:].rearrange("p (c t) -> p c t", c=4)
        va = r_va[:].rearrange("p (t d) -> p t d", t=TB)
        vb = r_vb[:].rearrange("p (t d) -> p t d", t=TB)
        qbT = r_qkb[:, 0:1024]
        kbT = r_qkb[:, 1024:2048]
        gate_a = r_qkb[:].rearrange("p (t d) -> p t d", t=TB)
        gate_b = vb
        qiT = r_qa[:, 0:1024].rearrange("p (c t) -> p c t", c=2)
        kiT = r_qa[:, 1024:1536]
        relu_b = [r_ka[:, 512 * i:512 * i + 512] for i in range(4)]
        score = {tb: r_va[:, o:o + P * (tb + 1)] for tb, o in ((1, 0), (2, 256), (3, 640))}
        MASK_AT = (0, 128, 384, 768)
        bsum = r_ob[:, 0:1024]
        lin = [r_g[:, 1024 * i:1024 * (i + 1)] for i in range(4)]
        q_dec = r_oa[:, 0:1024]
        k_rows = r_oa[:, 1024:1792].rearrange("p (t c) -> p t c", t=3)
        attn = r_att[:].rearrange("p (g i) -> p g i", g=BH * TB)
        param_rows = r_att[:, 0:D]
        junk = r_att[:, D:2 * D]
        iota_i = r_vb[:, 0:128].bitcast(I32)
        iota_p = r_vb[:, 128:256].bitcast(I32)
        ixor = r_vb[:, 256:384].bitcast(I32)
        ixor_up = r_vb[:, 384:512].bitcast(I32)
        ishift = r_vb[:, 512:640].bitcast(I32)
        bias_rev = r_vb[0:AH, 1024:1664]
        logit = [r_g[:, 512 * i:512 * i + 512] for i in (0, 1)]
        prob = [r_g[:, 1024 + 512 * i:1536 + 512 * i] for i in (0, 1)]
        probT = [r_g[:, 2048 + 512 * i:2560 + 512 * i] for i in (0, 1)]
        sq_b = [r_g[:, 3072 + 512 * i:3584 + 512 * i] for i in (0, 1)]
        conv_y = lambda c: (r_oa if c < 4 else r_ob)[:, 512 * (c % 4):512 * (c % 4) + 512]
        PADW = S + CW - 1
        upad = [r_va[:, 576 * i:576 * i + PADW] for i in range(3)]
        sgl = [r_vb[:, 512 * i:512 * i + 512] for i in (0, 1)]
        ln_rstd = r_vb[:, 1024:1536]
        m_f32 = [r_g[:, 512 * i:512 * i + 512] for i in range(2)]
        ln_sq = [r_qkb[:, 512 * i:512 * i + 512] for i in (0, 1)]
        gate_s = lambda c: (r_qa if c < 4 else r_ka)[:, 512 * (c % 4):512 * (c % 4) + 512]
        nf_row = r_att[:, 0:D]
        sq_junk = r_att[:, D:2 * D]
        ROW_NE, ROW_NO, ROW_CB, ROW_LG, ROW_LB = CW, CW + 1, CW + 2, CW + 3, CW + 4

        def hx(tb, c):
            return (oa if c < 4 else ob)[:, tb, P * (c % 4):P * (c % 4) + P]

        bank = [ctx.enter_context(nc.psum_tensor(f"bank{i}", [P, 512], F32)) for i in range(8)]

        x_in = [sem(f"x_in{t}") for t in range(TB)]
        params_in = sem("params_in")
        rel_in = sem("rel_in")
        raw_in = [sem(f"raw_in{i}") for i in range(2)]
        table_in = sem("table_in")
        x_again = sem("x_again")
        nf_in = sem("nf_in")
        out_done = sem("out_done")
        pool_const = sem("pool_const")
        pool_chain = sem("pool_chain")
        hi_ready = sem("hi_ready")
        lo_ready = sem("lo_ready")
        squares = sem("squares")
        var_ready = sem("var_ready")
        rstd_ready = sem("rstd_ready")
        normed = sem("normed")
        params_T = sem("params_T")
        pvec_ready = sem("pvec_ready")
        rev_ready = sem("rev_ready")
        xor_ready = sem("xor_ready")
        hT_in_bank = sem("hT_in_bank")
        hT_hi_ready = sem("hT_hi_ready")
        hT_ready = sem("hT_ready")
        half_used = sem("half_used")
        group_done = sem("group_done")
        act_emptied = sem("act_emptied")
        dve_emptied = sem("dve_emptied")
        wi_T = sem("wi_T")
        wi_ready = sem("wi_ready")
        z_done = sem("z_done")
        z_added = sem("z_added")
        softplus = sem("softplus")
        bsum_ready = sem("bsum_ready")
        idx_done = sem("idx_done")
        relu_ready = sem("relu_ready")
        score_step = sem("score_step")
        masks_ready = sem("masks_ready")
        causal_ready = sem("causal_ready")
        mask_ready = sem("mask_ready")
        act_chain = sem("act_chain")
        dve_chain = sem("dve_chain")
        diff_ready = sem("diff_ready")
        exp_ready = sem("exp_ready")
        operand_ready = sem("operand_ready")
        fill_done = sem("fill_done")
        fill_emptied = sem("fill_emptied")
        ob_squared = sem("ob_squared")
        ob_summed = sem("ob_summed")
        ob_var = sem("ob_var")
        ob_rstd = sem("ob_rstd")
        att_zero = sem("att_zero")
        qk_done = sem("qk_done")
        logit_ready = sem("logit_ready")
        max_ready = sem("max_ready")
        prob_ready = sem("prob_ready")
        probT_done = sem("probT_done")
        probT_ready = sem("probT_ready")
        pv_done = sem("pv_done")
        oa_emptied = sem("oa_emptied")
        gates_silu = sem("gates_silu")
        mixed = sem("mixed")
        sig_ready = sem("sig_ready")
        u_ready = sem("u_ready")
        conv_done = sem("conv_done")
        mean_done = sem("mean_done")
        centred = sem("centred")
        lnsq_ready = sem("lnsq_ready")
        lnsq_used = sem("lnsq_used")
        std_ready = sem("std_ready")
        scaled = sem("scaled")
        ln_silu = sem("ln_silu")
        m_ready = sem("m_ready")
        y_ready = sem("y_ready")

        LEVELS = [64, 32, 16, 8, 4, 2, 1]
        ITEMS = ["k"] + LEVELS
        ITEM_STEP = {6: ["k"], 7: [64], 8: [32, 16], 9: [8, 4], 10: [2, 1]}
        ITEM_NO = {it: n for n, it in enumerate(ITEMS)}
        FILLS = ["k0", "k1"] + [(lv, h) for lv in LEVELS for h in range(BH)] + [(0, h) for h in range(BH)]
        OB_FILLS = [f"ob{t}{par}" for t in range(TB) for par in range(2)]
        FILLS += ["kv0", "kv1", "kv2"] + OB_FILLS
        FILL_NO = {f: n for n, f in enumerate(FILLS)}
        FILL_AT = {}
        for s_, its in ITEM_STEP.items():
            for half, it in enumerate(its):
                FILL_AT[(s_, half if len(its) == 2 else 1)] = ["k0", "k1"] if it == "k" else [(it, h) for h in range(BH)]
        FILL_AT[(11, 0)] = [(0, h) for h in range(BH)] + ["kv0", "kv1", "kv2"]
        FILL_AT[(11, 1)] = OB_FILLS
        LAST_FILL = {"k": FILL_NO["k1"], **{lv: FILL_NO[(lv, BH - 1)] for lv in LEVELS}}

        NSTEP = TB * AH
        ATT_S0 = S_GA

        def wait_slot_used(eng, j):
            if SLOTS[j][0] == "a":
                eng.wait_ge(group_done, FIRST[j] + 2)
            elif j % 2:
                eng.wait_ge(group_done, FIRST[j] + TB)
            else:
                eng.wait_ge(half_used, sum(1 for i in range(0, j + 1, 2) if SLOTS[i][0] == "b"))

        block = ctx.enter_context(nc.Block())

        @block.sync
        def _(sp):
            x_rows = x[0].rearrange("(t p) d -> t p d", p=P)
            sp.dma_start(rel_rows[:], rel_bias.rearrange("b h -> h b"), allow_slow_non_contiguous=True).then_inc(rel_in, 16)
            for t in range(TB):
                sp.dma_start(x_t[:, t, :], x_rows[t]).then_inc(x_in[t], 16)
            sp.dma_start(param_rows[0:CW, :], conv_w[0]).then_inc(params_in, 16)
            for r, v in ((ROW_NE, norm_even), (ROW_NO, norm_odd), (ROW_CB, conv_b), (ROW_LG, conv_ln_g),
                         (ROW_LB, conv_ln_b)):
                sp.dma_start(param_rows[r:r + 1, :], v).then_inc(params_in, 16)
            sp.dma_start(small_rows[0:2, :], b_gla_lr[0].rearrange("(a n) -> a n", a=2)).then_inc(params_in, 16)
            sp.dma_start(small_rows[2:3, :], gla_norm).then_inc(params_in, 16)
            sp.dma_start(w_lr[:], w_gla_lr[0]).then_inc(params_in, 16)

            def load(j):
                kind, ks, pieces = SLOTS[j]
                if j >= 2:
                    sp.wait_ge(lo_ready, j - 1)
                for at, m, c0, n in pieces:
                    if kind == "a":
                        dst = w_raw[j % 2][:].rearrange("p (k n) -> p k n", k=KC)[:, :, at:at + n]
                        src = WSRC[m].rearrange("(k p) n -> p k n", p=P)[:, :, c0:c0 + n]
                    else:
                        dst = w_raw[j % 2][:].rearrange("p (k n) -> p k n", k=4)
                        src = WSRC[m].rearrange("(k p) n -> p k n", p=P)[:, ks[0]:ks[0] + 4, c0:c0 + n]
                    sp.dma_start(dst, src).then_inc(raw_in[j % 2], 16)

            load(0)
            load(1)
            sp.wait_ge(rev_ready, 1)
            sp.wait_ge(normed, TB)
            for h in range(AH):
                row = bias_rev[h:h + 1, 127:127 + S]
                src = bass.AP(row.tensor, row.offset, [list(row.ap[0]), [-1, P], [1, S]])
                sp.dma_start(bias_tab[:, h, :], src).then_inc(table_in, 16)
            for j in range(2, NS):
                if j == S_OE + 2:
                    sp.wait_ge(logit_ready, NSTEP)
                    sp.dma_start(x_t, x[0].rearrange("(t p) d -> p t d", p=P)).then_inc(x_again, 16)
                if j == S_ODD + 4:
                    sp.wait_ge(group_done, FIRST[S_ODD])
                    sp.dma_start(nf_row, norm_f.rearrange("(a n) -> a n", a=1).to_broadcast([P, D])).then_inc(nf_in, 16)
                load(j)
            out_rows = out[0].rearrange("(t p) d -> t p d", p=P)
            for t in range(TB):
                sp.wait_ge(y_ready, t + 1)
                sp.dma_start(out_rows[t], x_t[:, t, :]).then_inc(out_done, 16)
            sp.wait_ge(out_done, 16 * TB)

        @block.gpsimd
        def _(pool):
            chain = [0]

            def link(ins):
                chain[0] += 1
                ins.then_inc(pool_chain, 1)
                pool.wait_ge(pool_chain, chain[0])

            def affine(dst, src, op, fill, step, mult):
                return nc.gpsimd.affine_select(out=dst, in_=src, compare_op=op, fill=fill, base=0,
                                               pattern=[[step, P]], channel_multiplier=mult)

            link(nc.gpsimd.memset(ident[:], 0.0))
            link(affine(ident[:], ident[:], ALU.not_equal, 1.0, -1, 1))
            nc.gpsimd.memset(ones[:], 1.0).then_inc(pool_const, 1)
            link(nc.gpsimd.memset(minus_half[:], -0.5))
            nc.gpsimd.memset(ident_bf[:], 0.0).then_inc(pool_const, 1)
            pool.wait_ge(pool_const, 2)
            affine(ident_bf[:], ident_bf[:], ALU.not_equal, 1.0, -1, 1).then_inc(pool_const, 1)
            link(nc.gpsimd.memset(neg_mask[:, 0:P], 0.0))
            affine(neg_mask[:, 0:P], neg_mask[:, 0:P], ALU.is_ge, NEG, -1, 1).then_inc(pool_const, 1)
            nc.gpsimd.iota(iota_i, [[1, P]], base=0, channel_multiplier=0).then_inc(pool_const, 1)
            nc.gpsimd.iota(iota_p, [[0, P]], base=0, channel_multiplier=1).then_inc(pool_const, 1)

            def rsqrt(first, last, ready, value, done):
                pool.wait_ge(ready, value)
                nc.gpsimd.tensor_tensor(rstd[:, first:last], stat[:, first:last], minus_half[:, first:last],
                                        ALU.pow).then_inc(done, 1)

            def split_lo(j):
                pool.wait_ge(hi_ready, j + 1)
                if j >= 3:
                    wait_slot_used(pool, j - 3)
                if j == 1:
                    v = lambda t: t[:].rearrange("p (k n) -> p k n", k=KC)[:, :, 0:148]
                else:
                    v = lambda t: t[:]
                nc.gpsimd.tensor_tensor(v(w_lo[j % 3]), v(w_raw[j % 2]), v(w_hi[j % 3]).bitcast(F32),
                                        ALU.subtract).then_inc(lo_ready, 1)

            for t in range(TB):
                rsqrt(t, t + 1, var_ready, t + 1, rstd_ready)
            pool.wait_ge(xor_ready, 1)
            affine(ixor_up, ixor, ALU.is_gt, 0.0, 1, -1).then_inc(pool_const, 1)
            split_lo(0)
            split_lo(1)
            pool.wait_ge(params_T, 2)
            pool.wait_ge(squares, TB)
            nc.gpsimd.memset(r_att[:], 0.0).then_inc(att_zero, 1)

            def diff(it):
                n = ITEM_NO[it]
                pool.wait_ge(bsum_ready, 1)
                if n >= 4:
                    pool.wait_ge(fill_done, LAST_FILL[ITEMS[n - 4]] + 1)
                dst = lin[n % 4]
                if it == "k":
                    dv = dst.rearrange("p (b c) -> p b c", c=P)
                    bv = bsum.rearrange("p (b c) -> p b c", c=P)
                    last = bv[:, :, P - 1:P].to_broadcast([P, 8, P])
                    nc.gpsimd.tensor_tensor(dv, last, bv, ALU.subtract).then_inc(diff_ready, 2)
                    return
                nb = D // (2 * it)
                dv = dst.rearrange("p (b c) -> p b c", c=2 * it)
                bv = bsum.rearrange("p (b c) -> p b c", c=2 * it)
                ref = bv[:, :, it - 1:it].to_broadcast([P, nb, it])
                nc.gpsimd.tensor_tensor(dv[:, :, 0:it], ref, bv[:, :, 0:it], ALU.subtract).then_inc(diff_ready, 1)
                nc.gpsimd.tensor_tensor(dv[:, :, it:], bv[:, :, it:], ref, ALU.subtract).then_inc(diff_ready, 1)

            for s_ in range(NS):
                if s_ + 2 < NS:
                    split_lo(s_ + 2)
                if s_ == 2:
                    for n, tb in enumerate((1, 2, 3)):
                        pool.wait_ge(score_step, IH * (n + 1))
                        diag = score[tb][:, P * tb:P * tb + P]
                        affine(diag, diag, ALU.is_ge, HIDDEN, -1, 1).then_inc(causal_ready, 1)
                for it in ITEM_STEP.get(s_ + 1, []):
                    diff(it)
                if s_ == 12:
                    rsqrt(0, 16, ob_var, 1, ob_rstd)
                if s_ == S_OE + 3:
                    for t in range(TB):
                        rsqrt(t, t + 1, var_ready, TB + t + 1, rstd_ready)
            for t in range(TB):
                rsqrt(t, t + 1, var_ready, 2 * TB + t + 1, rstd_ready)

        @block.scalar
        def _(act):
            chain = [0]

            def link(ins):
                chain[0] += 1
                ins.then_inc(act_chain, 1)
                act.wait_ge(act_chain, chain[0])

            def split_hi(j):
                act.wait_ge(raw_in[j % 2], raw_full[j])
                if j >= 3:
                    wait_slot_used(act, j - 3)
                if j == 1:
                    v = lambda t: t[:].rearrange("p (k n) -> p k n", k=KC)[:, :, 0:148]
                else:
                    v = lambda t: t[:]
                nc.scalar.activation(v(w_hi[j % 3]), v(w_raw[j % 2]), ACT.Copy).then_inc(hi_ready, 1)

            def hT_high(rnd, order, scale):
                for n, c in enumerate(order):
                    act.wait_ge(hT_in_bank, KC * rnd + n + 1)
                    nc.scalar.activation(hT_hi[:, c, :], bank[4 + n % 4][:], ACT.Copy,
                                         scale=scale(c)).then_inc(hT_hi_ready, 1)

            def empty(g, dst, rows=P, scale=1.0, func=ACT.Copy):
                act.wait_ge(group_done, g + 1)
                nc.scalar.activation(dst, bank[g % 4][0:rows, :], func, scale=scale).then_inc(act_emptied, 1)

            split_hi(0)
            for t in range(TB):
                act.wait_ge(x_in[t], 16)
                if t:
                    act.wait_ge(squares, t)
                nc.scalar.activation(junk, x_t[:, t, :], ACT.Square, accum_out=stat[:, t:t + 1]).then_inc(squares, 1)
            split_hi(1)
            act.wait_ge(pvec_ready, 2)
            hT_high(0, range(KC), lambda c: pvec[:, c, ROW_NE:ROW_NE + 1])

            def exps(it):
                n = ITEM_NO[it]
                act.wait_ge(diff_ready, 2 * (n + 1))
                nc.scalar.activation(lin[n % 4], lin[n % 4], ACT.Exp, scale=1.0 / TAU).then_inc(exp_ready, 1)

            def soft(n):
                act.wait_ge(max_ready, n + 1)
                if n >= 2:
                    act.wait_ge(probT_done, n - 1)
                w = P * (n // AH + 1)
                nc.scalar.activation(prob[n % 2][:, 0:w], logit[n % 2][:, 0:w], ACT.Exp, bias=neg_max[:, n:n + 1],
                                     accum_out=row_sum[:, n:n + 1]).then_inc(prob_ready, 1)

            for s_ in range(S_OE):
                if s_ + 2 < NS:
                    split_hi(s_ + 2)
                g = FIRST[s_]
                if s_ == 0:
                    empty(g, qiT[:, 0, :])
                    empty(g + 1, qiT[:, 1, :])
                elif s_ == 1:
                    empty(g, kiT)
                    empty(g + 1, lwT[:], rows=RANK + IH)
                elif s_ == 2:
                    empty(g, qbT[:, 0:S], scale=DK ** -0.5)
                    act.wait_ge(wi_T, 1)
                    nc.scalar.activation(wi[:], bank[6][:, 0:TB * (RANK + IH)].rearrange(
                        "p (t c) -> p t c", t=TB)[:, :, RANK:], ACT.Copy,
                        scale=ID ** -0.5 * IH ** -0.5).then_inc(wi_ready, 1)
                    n = 0
                    for tb in (1, 2, 3):
                        for h in range(IH):
                            act.wait_ge(idx_done, n + 1)
                            if n >= 4:
                                act.wait_ge(score_step, n - 3)
                            w = P * (tb + 1)
                            nc.scalar.activation(relu_b[n % 4][:, 0:w], bank[4 + n % 2][:, 0:w],
                                                 ACT.Relu).then_inc(relu_ready, 1)
                            n += 1
                    empty(g + 1, qbT[:, S:], scale=DK ** -0.5)
                    act.wait_ge(z_added, 2)
                    link(nc.scalar.activation(lin[1], lin[0], ACT.Abs))
                    link(nc.scalar.activation(lin[1], lin[1], ACT.Exp, scale=-1.0))
                    nc.scalar.activation(lin[1], lin[1], ACT.Ln, bias=1.0).then_inc(softplus, 1)
                elif s_ == 3:
                    empty(g, kbT[:, 0:S])
                    empty(g + 1, kbT[:, S:])
                    act.wait_ge(bsum_ready, 1)
                    nc.scalar.activation(q_dec, bsum, ACT.Exp, scale=1.0 / TAU).then_inc(exp_ready, 1)
                elif s_ == S_VB + 1:
                    act.wait_ge(table_in, 16 * AH)
                    act.wait_ge(masks_ready, 1)
                    for t in range(TB):
                        empty(g + t, vb[:, t, :])
                    exps("k")
                elif S_QA <= s_ < S_VA:
                    its = ITEM_STEP.get(s_ + 1, [])
                    c = 2 * (s_ - S_QA) if s_ < S_KA else 2 * (s_ - S_KA)
                    if s_ == S_KA:
                        act.wait_ge(score_step, 3 * IH)
                    dst = qaT if s_ < S_KA else kaT
                    sc = AD ** -0.5 if s_ < S_KA else 1.0
                    empty(g, dst[:, c, :], scale=sc)
                    if its:
                        exps(its[0])
                    empty(g + 1, dst[:, c + 1, :], scale=sc)
                    for it in its[1:]:
                        exps(it)
                elif s_ == S_VA + 1:
                    act.wait_ge(mask_ready, 3)
                    for t in range(TB):
                        empty(g + t, va[:, t, :])
                    for t in range(TB):
                        act.wait_ge(fill_emptied, FILL_NO[f"ob{t}1"] + 1)
                        if t >= 2:
                            act.wait_ge(ob_summed, t - 1)
                        nc.scalar.activation(sq_b[t % 2], ob[:, t, :], ACT.Square).then_inc(ob_squared, 1)
                    soft(0)
                elif s_ >= ATT_S0:
                    for u in range(TB):
                        n0 = AH * (s_ - ATT_S0) + 2 * u
                        if n0 + 1 < NSTEP:
                            soft(n0 + 1)
                        if n0 + 2 < NSTEP:
                            soft(n0 + 2)
                        if s_ == S_GA + 1:
                            if u == 0:
                                act.wait_ge(fill_done, len(FILLS))
                            empty(g + u, gate_a[:, u, :])
                        if s_ == S_GB + 1:
                            empty(g + u, gate_b[:, u, :])
                    if s_ == S_GA + 1:
                        act.wait_ge(act_emptied, evacs_through(FIRST[S_GA] + 3, "act"))
                        nc.scalar.activation(r_qkb[:], r_qkb[:], ACT.Silu).then_inc(gates_silu, 1)
            act.wait_ge(act_emptied, evacs_through(FIRST[S_GB] + 3, "act"))
            nc.scalar.activation(r_vb[:], r_vb[:], ACT.Silu).then_inc(gates_silu, 1)
            wait_slot_used(act, S_OE - 1)
            hT_high(1, range(KC), lambda c: 1.0 if c < 4 else pb3[:, 2:3])

            def row_squares(base):
                for t in range(TB):
                    act.wait_ge(dve_emptied, base + t + 1)
                    act.wait_ge(squares, (base - TB) // TB // 2 * TB + TB + t)
                    nc.scalar.activation(sq_junk, x_t[:, t, :], ACT.Square,
                                         accum_out=stat[:, t:t + 1]).then_inc(squares, 1)

            for s_ in range(S_OE, S_ODD):
                split_hi(s_ + 2)
            row_squares(TB)
            wait_slot_used(act, S_ODD - 1)
            hT_high(2, range(KC), lambda c: pvec[:, c, ROW_NO:ROW_NO + 1])

            for s_ in range(S_ODD, S_OO):
                split_hi(s_ + 2)
                g = FIRST[s_]
                if s_ in CHUNK:
                    c = CHUNK[s_]
                    if c >= 2:
                        act.wait_ge(u_ready, c - 1)
                    act.wait_ge(group_done, g + 2)
                    nc.scalar.activation(sgl[c % 2], bank[(g + 1) % 4][:], ACT.Sigmoid).then_inc(act_emptied, 1)
                else:
                    c = GATE[s_]
                    empty(g, gate_s(c))
                    empty(g + 1, gate_s(c + 1))
            act.wait_ge(act_emptied, evacs_through(FIRST[S_OO] - 1, "act"))
            nc.scalar.activation(r_qa[:], r_qa[:], ACT.Silu).then_inc(gates_silu, 1)
            nc.scalar.activation(r_ka[:], r_ka[:], ACT.Silu).then_inc(gates_silu, 1)
            for c in range(KC):
                act.wait_ge(centred, c + 1)
                if c >= 2:
                    act.wait_ge(lnsq_used, c - 1)
                nc.scalar.activation(ln_sq[c % 2], conv_y(c), ACT.Square).then_inc(lnsq_ready, 1)
            act.wait_ge(std_ready, 1)
            nc.scalar.activation(ln_rstd, ln_rstd, ACT.Sqrt).then_inc(std_ready, 1)
            for c in range(KC):
                act.wait_ge(scaled, c + 1)
                nc.scalar.activation(conv_y(c), conv_y(c), ACT.Silu, scale=pvec[:, c, ROW_LG:ROW_LG + 1],
                                     bias=pvec[:, c, ROW_LB:ROW_LB + 1]).then_inc(ln_silu, 1)
                if c >= 1:
                    act.wait_ge(m_ready, c)
                    nc.scalar.activation(hT_hi[:, c - 1, :], m_f32[(c - 1) % 2], ACT.Copy).then_inc(hT_hi_ready, 1)
            act.wait_ge(m_ready, KC)
            nc.scalar.activation(hT_hi[:, KC - 1, :], m_f32[(KC - 1) % 2], ACT.Copy).then_inc(hT_hi_ready, 1)
            for s_ in range(S_OO, NS - 2):
                split_hi(s_ + 2)
            row_squares(3 * TB)

        @block.vector
        def _(dve):
            chain = [0]

            def link(ins):
                chain[0] += 1
                ins.then_inc(dve_chain, 1)
                dve.wait_ge(dve_chain, chain[0])

            dve.wait_ge(rel_in, 16)
            starts = bucket_starts() + [S]
            for b in range(NB):
                lo_d, hi_d = starts[b], starts[b + 1]
                last = nc.vector.tensor_copy(bias_rev[:, S - hi_d:S - lo_d],
                                             rel_rows[:, b:b + 1].to_broadcast([AH, hi_d - lo_d]))
            link(last)
            nc.vector.memset(bias_rev[:, S:S + P], 0.0).then_inc(rev_ready, 1)
            dve.wait_ge(pool_const, 6)
            nc.vector.tensor_tensor(ixor, iota_i, iota_p, ALU.bitwise_xor).then_inc(xor_ready, 1)

            def norm_rows(first_square):
                for t in range(TB):
                    dve.wait_ge(squares, first_square + t + 1)
                    nc.vector.tensor_scalar(stat[:, t:t + 1], stat[:, t:t + 1], 1.0 / D, EPS, ALU.mult,
                                            ALU.add).then_inc(var_ready, 1)
                    dve.wait_ge(rstd_ready, first_square + t + 1)
                    nc.vector.tensor_scalar(oa[:, t, :], x_t[:, t, 0:512], rstd[:, t:t + 1], None, ALU.mult)
                    nc.vector.tensor_scalar(ob[:, t, :], x_t[:, t, 512:], rstd[:, t:t + 1], None,
                                            ALU.mult).then_inc(normed, 1)

            def hT_low(rnd, order, scale):
                for n, c in enumerate(order):
                    dve.wait_ge(hT_hi_ready, KC * rnd + n + 1)
                    nc.vector.scalar_tensor_tensor(
                        out=hT_lo[:, c, :], in0=bank[4 + n % 4][:], scalar=scale(c),
                        in1=hT_hi[:, c, :].bitcast(F32), op0=ALU.mult, op1=ALU.subtract).then_inc(hT_ready, 1)

            norm_rows(0)
            dve.wait_ge(params_T, 2)
            nc.vector.tensor_copy(pvec[:], bank[0][:, 0:KC * NROW].rearrange(
                "p (c r) -> p c r", c=KC)).then_inc(pvec_ready, 1)
            nc.vector.tensor_copy(pb3[:, 0:3], bank[1][:, 0:3]).then_inc(pvec_ready, 1)
            dve.wait_ge(pvec_ready, 2)
            hT_low(0, range(KC), lambda c: pvec[:, c, ROW_NE:ROW_NE + 1])
            dve.wait_ge(pool_const, 7)
            for lg in range(5):
                link(nc.vector.tensor_scalar(ishift, ixor_up, lg, None, ALU.logical_shift_right))
                link(nc.vector.tensor_scalar(level_mask[:, lg, :], ishift, 1, None, ALU.is_equal))
            nc.vector.tensor_copy(level_mask[:, 5, :], ident[:]).then_inc(masks_ready, 1)

            for i in range(2):
                dve.wait_ge(z_done, i + 1)
                nc.vector.tensor_scalar(lin[0][:, S * i:S * i + S], bank[7][:], pb3[:, i:i + 1], None,
                                        ALU.add).then_inc(z_added, 1)
            dve.wait_ge(wi_ready, 1)
            n = 0
            for tb in (1, 2, 3):
                w = P * (tb + 1)
                for h in range(IH):
                    dve.wait_ge(relu_ready, n + 1)
                    if h == 0:
                        ins = nc.vector.tensor_scalar(score[tb], relu_b[n % 4][:, 0:w], wi[:, tb, 0:1], None, ALU.mult)
                    else:
                        dve.wait_ge(score_step, n)
                        ins = nc.vector.scalar_tensor_tensor(out=score[tb], in0=relu_b[n % 4][:, 0:w],
                                                             scalar=wi[:, tb, h:h + 1], in1=score[tb],
                                                             op0=ALU.mult, op1=ALU.add)
                    ins.then_inc(score_step, 1)
                    n += 1
            dve.wait_ge(softplus, 1)
            link(nc.vector.scalar_tensor_tensor(out=lin[2], in0=lin[0], scalar=0.0, in1=lin[1], op0=ALU.min,
                                                op1=ALU.subtract))
            for b in range(8):
                ins = nc.vector.tensor_tensor_scan(bsum[:, P * b:P * b + P], ones[:], lin[2][:, P * b:P * b + P],
                                                   0.0, ALU.mult, ALU.add)
            ins.then_inc(bsum_ready, 1)

            for n, tb in enumerate((1, 2, 3)):
                dve.wait_ge(causal_ready, n + 1)
                w = P * (tb + 1)
                for r in range(TOPK // 8):
                    link(nc.vector.max(top8[:], score[tb]))
                    link(nc.vector.match_replace(score[tb], top8[:], score[tb], TAKEN))
                nc.vector.tensor_scalar(neg_mask[:, MASK_AT[tb]:MASK_AT[tb] + w], score[tb],
                                        0.5 * (HIDDEN + TAKEN), NEG, ALU.is_gt, ALU.mult).then_inc(mask_ready, 1)

            dve.wait_ge(exp_ready, 1)
            link(nc.vector.tensor_copy(chunk_decay[:], q_dec.rearrange("p (i t c) -> p i t c", i=2, c=P)[:, :, :, P - 1]))
            nc.vector.tensor_tensor(q_dec, q_dec, qbT, ALU.mult).then_inc(operand_ready, 1)

            def operand(it):
                n = ITEM_NO[it]
                dve.wait_ge(exp_ready, n + 2)
                v = lin[n % 4]
                if it == "k":
                    nc.vector.tensor_tensor(v, v, kbT, ALU.mult).then_inc(operand_ready, 1)
                    return
                vv, kv, qv = (a.rearrange("p (b c) -> p b c", c=2 * it) for a in (v, kbT, qbT))
                nc.vector.tensor_tensor(vv[:, :, 0:it], vv[:, :, 0:it], kv[:, :, 0:it], ALU.mult)
                nc.vector.tensor_tensor(vv[:, :, it:], vv[:, :, it:], qv[:, :, it:],
                                        ALU.mult).then_inc(operand_ready, 1)

            def empty_fill(f):
                n = FILL_NO[f]
                b = bank[4 + n % 4]
                dve.wait_ge(fill_done, n + 1)
                if f in ("k0", "k1"):
                    w = 2 if f == "k0" else 1
                    t0 = 0 if f == "k0" else 2
                    nc.vector.tensor_copy(k_rows[:, t0:t0 + w, :], b[:, 0:256 * w].rearrange(
                        "p (t c) -> p t c", t=w)).then_inc(fill_emptied, 1)
                    return
                if isinstance(f, tuple):
                    lv, h = f
                    a = attn[:, TB * h:TB * h + TB, :]
                    v = b[:].rearrange("p (t i) -> p t i", t=TB)
                    dve.wait_ge(att_zero, 1)
                    if lv >= 32:
                        for p0 in range(0, P, 2 * lv):
                            ins = nc.vector.tensor_copy(a[p0:p0 + lv, :, p0 + lv:p0 + 2 * lv],
                                                        v[p0:p0 + lv, :, p0 + lv:p0 + 2 * lv])
                    else:
                        lg = {16: 4, 8: 3, 4: 2, 2: 1, 1: 0, 0: 5}[lv]
                        m = level_mask[:, lg:lg + 1, :].to_broadcast([P, TB, P])
                        ins = nc.vector.copy_predicated(a, m, v)
                    ins.then_inc(fill_emptied, 1)
                    return
                t = int(f[2])
                if f[:2] == "kv":
                    if t == 0:
                        nc.vector.tensor_copy(state[:, 1, :], b[:, 0:256]).then_inc(fill_emptied, 1)
                        return
                    dve.wait_ge(fill_emptied, n)
                    for i in range(2):
                        ins = nc.vector.scalar_tensor_tensor(
                            out=state[:, t + 1, DV * i:DV * i + DV], in0=state[:, t, DV * i:DV * i + DV],
                            scalar=chunk_decay[:, i, t:t + 1], in1=b[:, DV * i:DV * i + DV], op0=ALU.mult, op1=ALU.add)
                    ins.then_inc(fill_emptied, 1)
                    return
                par = int(f[3])
                nc.vector.tensor_copy(ob[:, t, :].rearrange("p (i r e) -> p i r e", i=2, r=2)[:, :, par, :],
                                      b[:, 0:2 * DV].rearrange("p (i e) -> p i e", i=2)).then_inc(fill_emptied, 1)

            operand("k")
            operand(64)
            for f in ("k0", "k1"):
                empty_fill(f)
            for s_ in range(7, 11):
                for it in ITEM_STEP[s_]:
                    for h in range(BH):
                        empty_fill((it, h))
                for it in ITEM_STEP.get(s_ + 1, []):
                    operand(it)
            for f in FILLS[FILL_NO[(0, 0)]:]:
                empty_fill(f)
            for t in range(TB):
                dve.wait_ge(ob_squared, t + 1)
                nc.vector.tensor_reduce(stat[:, 4 * t:4 * t + 4], sq_b[t % 2].rearrange("p (h e) -> p h e", h=BH),
                                        AX.X, ALU.add).then_inc(ob_summed, 1)
            def logits(n):
                tb, h = divmod(n, AH)
                w = P * (tb + 1)
                dve.wait_ge(qk_done, n + 1)
                if n >= 2:
                    dve.wait_ge(prob_ready, n - 1)
                nc.vector.tensor_tensor_reduce(out=logit[n % 2][:, 0:w], in0=bank[4 + n % 2][:, 0:w],
                                               in1=bias_tab[:, h, S - w:S], scale=1.0, scalar=-3.0e38, op0=ALU.add,
                                               op1=ALU.max, accum_out=row_max[:, n:n + 1]).then_inc(logit_ready, 1)
                dve.wait_ge(logit_ready, n + 1)
                nc.vector.tensor_scalar(neg_max[:, n:n + 1], row_max[:, n:n + 1], -1.0, None,
                                        ALU.mult).then_inc(max_ready, 1)

            def empty_oa(tb):
                dve.wait_ge(pv_done, AH * (tb + 1))
                link(nc.vector.reciprocal(row_inv[:, AH * tb:AH * tb + AH], row_sum[:, AH * tb:AH * tb + AH]))
                inv = row_inv[:, AH * tb:AH * tb + AH].unsqueeze(2).to_broadcast([P, AH, AD])
                nc.vector.tensor_tensor(oa[:, tb, :].rearrange("p (h d) -> p h d", h=AH),
                                        bank[7][:].rearrange("p (h d) -> p h d", h=AH), inv,
                                        ALU.mult).then_inc(oa_emptied, 1)

            dve.wait_ge(table_in, 16 * AH)
            logits(0)
            for n in range(NSTEP):
                if n + 1 < NSTEP:
                    logits(n + 1)
                w = P * (n // AH + 1)
                dve.wait_ge(probT_done, n + 1)
                if n >= 2:
                    dve.wait_ge(pv_done, n - 1)
                nc.vector.tensor_copy(probT[n % 2][:, 0:w], bank[6][:, 0:w]).then_inc(probT_ready, 1)
                if n % AH == 0 and n:
                    empty_oa(n // AH - 1)
                if n == 2:
                    dve.wait_ge(ob_summed, TB)
                    nc.vector.tensor_scalar(stat[:], stat[:], 1.0 / DV, EPS, ALU.mult, ALU.add).then_inc(ob_var, 1)
                if n == 6:
                    dve.wait_ge(ob_rstd, 1)
                    g16 = r_ob[:].rearrange("p (g e) -> p g e", e=DV)
                    link(nc.vector.tensor_tensor(g16, g16, rstd[:].unsqueeze(2).to_broadcast([P, 16, DV]), ALU.mult))
            empty_oa(TB - 1)
            dve.wait_ge(oa_emptied, TB)
            dve.wait_ge(gates_silu, 1)
            nc.vector.tensor_tensor(r_oa[:], r_oa[:], r_qkb[:], ALU.mult).then_inc(mixed, 1)
            dve.wait_ge(gates_silu, 2)
            nc.vector.tensor_tensor(r_ob[:], r_ob[:], r_vb[:], ALU.mult).then_inc(mixed, 1)
            hT_low(1, range(KC), lambda c: 1.0 if c < 4 else pb3[:, 2:3])

            def residual(s0):
                for half in range(2):
                    for t in range(TB):
                        g = FIRST[s0 + 2 * half] + t
                        dve.wait_ge(group_done, g + 1)
                        xs = x_t[:, t, 512 * half:512 * half + 512]
                        nc.vector.tensor_tensor(xs, bank[g % 4][:], xs, ALU.add).then_inc(dve_emptied, 1)

            dve.wait_ge(x_again, 16)
            residual(S_OE)
            norm_rows(TB)
            hT_low(2, range(KC), lambda c: pvec[:, c, ROW_NO:ROW_NO + 1])

            for i in range(3):
                ins = nc.vector.memset(upad[i][:, 0:CW - 1], 0.0)
            link(ins)
            chunk_slots = sorted(CHUNK, key=lambda j: CHUNK[j])

            def glu(c):
                g = FIRST[chunk_slots[c]]
                dve.wait_ge(act_emptied, evacs_through(g + 1, "act"))
                nc.vector.tensor_tensor(upad[c % 3][:, CW - 1:PADW], bank[g % 4][:], sgl[c % 2],
                                        ALU.mult).then_inc(u_ready, 1)

            glu(0)
            for c in range(KC):
                if c + 1 < KC:
                    glu(c + 1)
                dve.wait_ge(u_ready, c + 1)
                acc = bank[6 + c % 2][:]
                link(nc.vector.tensor_scalar(acc, upad[c % 3][:, 0:S], pvec[:, c, 0:1], pvec[:, c, ROW_CB:ROW_CB + 1],
                                             ALU.mult, ALU.add))
                for k in range(1, CW):
                    ins = nc.vector.scalar_tensor_tensor(
                        out=acc if k < CW - 1 else conv_y(c), in0=upad[c % 3][:, k:k + S], scalar=pvec[:, c, k:k + 1],
                        in1=acc, op0=ALU.mult, op1=ALU.add)
                    if k < CW - 1:
                        link(ins)
                ins.then_inc(conv_done, 1)
            dve.wait_ge(mean_done, 1)
            for c in range(KC):
                nc.vector.scalar_tensor_tensor(out=conv_y(c), in0=bank[4][:], scalar=-1.0 / D, in1=conv_y(c),
                                               op0=ALU.mult, op1=ALU.add).then_inc(centred, 1)
            dve.wait_ge(mean_done, 2)
            nc.vector.tensor_scalar(ln_rstd, bank[5][:], 1.0 / D, EPS, ALU.mult, ALU.add).then_inc(std_ready, 1)
            dve.wait_ge(std_ready, 2)
            link(nc.vector.reciprocal(ln_rstd, ln_rstd))
            dve.wait_ge(gates_silu, 4)
            wait_slot_used(dve, S_OO - 1)

            def low_m(c):
                dve.wait_ge(hT_hi_ready, 3 * KC + c + 1)
                nc.vector.tensor_tensor(hT_lo[:, c, :], m_f32[c % 2], hT_hi[:, c, :].bitcast(F32),
                                        ALU.subtract).then_inc(hT_ready, 1)

            for c in range(KC + 2):
                if c < KC:
                    nc.vector.tensor_tensor(conv_y(c), conv_y(c), ln_rstd, ALU.mult).then_inc(scaled, 1)
                if c >= 2:
                    low_m(c - 2)
                if 1 <= c <= KC:
                    dve.wait_ge(ln_silu, c)
                    nc.vector.tensor_tensor(m_f32[(c - 1) % 2], conv_y(c - 1), gate_s(c - 1), ALU.mult).then_inc(m_ready, 1)
            residual(S_OO)
            dve.wait_ge(nf_in, 16)
            for t in range(TB):
                dve.wait_ge(squares, 2 * TB + t + 1)
                nc.vector.tensor_scalar(stat[:, t:t + 1], stat[:, t:t + 1], 1.0 / D, EPS, ALU.mult,
                                        ALU.add).then_inc(var_ready, 1)
                dve.wait_ge(rstd_ready, 2 * TB + t + 1)
                nc.vector.scalar_tensor_tensor(out=x_t[:, t, :], in0=x_t[:, t, :], scalar=rstd[:, t:t + 1], in1=nf_row,
                                               op0=ALU.mult, op1=ALU.mult).then_inc(y_ready, 1)

        @block.tensor
        def _(pe):
            pe.wait_ge(pool_chain, 2)
            pe.wait_ge(params_in, 16 * 9)
            for c in range(KC):
                ins = nc.tensor.transpose(bank[0][:, NROW * c:NROW * c + NROW], param_rows[0:NROW, P * c:P * c + P],
                                          ident[0:NROW, 0:NROW])
            ins.then_inc(params_T, 1)
            nc.tensor.transpose(bank[1][:, 0:3], small_rows[:], ident[0:3, 0:3]).then_inc(params_T, 1)

            def transpose_rows(rnd, order, ready):
                for n, c in enumerate(order):
                    ready(n)
                    if n >= 4:
                        pe.wait_ge(hT_ready, KC * rnd + n - 3)
                    for t in range(TB):
                        ins = nc.tensor.transpose(bank[4 + n % 4][:, P * t:P * t + P], hx(t, c), ident[:])
                    ins.then_inc(hT_in_bank, 1)

            transpose_rows(0, range(KC), lambda n: pe.wait_ge(normed, TB) if n == 0 else None)

            def bank_free(g):
                if g < 4:
                    pe.wait_ge(pvec_ready, 2)
                    return
                if evac_by[g - 4] == "act":
                    pe.wait_ge(act_emptied, evacs_through(g - 4, "act"))
                elif evac_by[g - 4] == "val":
                    pe.wait_ge(u_ready, evacs_through(g - 4, "val"))
                else:
                    pe.wait_ge(dve_emptied, evacs_through(g - 4, "residual"))

            def slot_ready(j):
                pe.wait_ge(lo_ready, j + 1)

            def group_a(j, i, hT_round=None):
                g = FIRST[j] + i
                bank_free(g)
                m = 128 if j != 1 or i == 0 else RANK + IH
                wh = w_hi[j % 3][:].rearrange("p (k n) -> p k n", k=KC)
                wl = w_lo[j % 3][:].rearrange("p (k n) -> p k n", k=KC)
                for k in range(KC):
                    if hT_round is not None:
                        pe.wait_ge(hT_ready, KC * hT_round + k + 1)
                    for q, (w, h) in enumerate(((wh, hT_hi), (wh, hT_lo), (wl, hT_hi))):
                        ins = nc.tensor.matmul(bank[g % 4][0:m, :], w[:, k, P * i:P * i + m], h[:, k, :],
                                               start=(k == 0 and q == 0), stop=(k == KC - 1 and q == 2))
                ins.then_inc(group_done, 1)

            def unit_b(j, t, part=(0, 4), hT_round=None):
                g = FIRST[j] + t
                ks = SLOTS[j][1]
                first, final = j % 2 == 0, j % 2 == 1
                if first and part[0] == 0:
                    bank_free(g)
                wh = w_hi[j % 3][:].rearrange("p (k n) -> p k n", k=4)
                wl = w_lo[j % 3][:].rearrange("p (k n) -> p k n", k=4)
                for i in range(*part):
                    k = ks[i]
                    if hT_round is not None:
                        pe.wait_ge(hT_ready, KC * hT_round + (i if first else 4 + i) + 1)
                    for q, (h, w) in enumerate(((hT_hi, wh), (hT_hi, wl), (hT_lo, wh))):
                        ins = nc.tensor.matmul(bank[g % 4][:], h[:, k, P * t:P * t + P], w[:, i, :],
                                               start=(first and i == 0 and q == 0), stop=(final and i == 3 and q == 2))
                if part[1] == 4:
                    if final:
                        ins.then_inc(group_done, 1)
                    elif t == TB - 1:
                        ins.then_inc(half_used, 1)

            slot_ready(0)
            group_a(0, 0, hT_round=0)
            group_a(0, 1)
            slot_ready(1)
            group_a(1, 0)
            group_a(1, 1)
            slot_ready(2)
            group_a(2, 0)
            pe.wait_ge(act_emptied, 4)
            pe.wait_ge(hT_ready, KC)
            for t in range(TB):
                ins = nc.tensor.transpose(bank[6][:, (RANK + IH) * t:(RANK + IH) * (t + 1)], lwT[:, P * t:P * t + P],
                                          ident[0:RANK + IH, 0:RANK + IH])
            ins.then_inc(wi_T, 1)
            nc.tensor.matmul(bank[7][:], w_lr[:, 0:P], lwT[0:RANK, :], start=True, stop=True).then_inc(z_done, 1)
            n = 0
            for tb in (1, 2, 3):
                for h in range(IH):
                    if n >= 2:
                        pe.wait_ge(relu_ready, n - 1)
                    p0 = 64 * (h % 2)
                    nc.tensor.matmul(bank[4 + n % 2][:, 0:P * (tb + 1)], qiT[p0:p0 + 64, h // 2, P * tb:P * tb + P],
                                     kiT[p0:p0 + 64, 0:P * (tb + 1)], start=True, stop=True).then_inc(idx_done, 1)
                    n += 1
                if tb == 1:
                    pe.wait_ge(z_added, 1)
                    nc.tensor.matmul(bank[7][:], w_lr[:, P:2 * P], lwT[0:RANK, :], start=True,
                                     stop=True).then_inc(z_done, 1)
            group_a(2, 1)

            def fill(f):
                n = FILL_NO[f]
                b = bank[4 + n % 4]
                if n >= 4:
                    pe.wait_ge(fill_emptied, n - 3)
                if f in ("k0", "k1"):
                    if f == "k0":
                        pe.wait_ge(operand_ready, ITEM_NO["k"] + 2)
                        pe.wait_ge(wi_ready, 1)
                        pe.wait_ge(z_added, 2)
                        pe.wait_ge(relu_ready, 12)
                    for a, t in enumerate((0, 1) if f == "k0" else (2,)):
                        for i in range(2):
                            ins = nc.tensor.transpose(b[:, 256 * a + P * i:256 * a + P * i + P],
                                                      lin[0][:, S * i + P * t:S * i + P * t + P], ident[:])
                    ins.then_inc(fill_done, 1)
                    return
                if isinstance(f, tuple):
                    lv, h = f
                    if h == 0 and lv:
                        pe.wait_ge(operand_ready, ITEM_NO[lv] + 2)
                    p0, at = 64 * (h % 2), S * (h // 2)
                    kk = lin[ITEM_NO[lv] % 4] if lv else kbT
                    qq = lin[ITEM_NO[lv] % 4] if lv else qbT
                    for t in range(TB):
                        cols = slice(at + P * t, at + P * t + P)
                        ins = nc.tensor.matmul(b[:, P * t:P * t + P], kk[p0:p0 + 64, cols], qq[p0:p0 + 64, cols],
                                               start=True, stop=True)
                    ins.then_inc(fill_done, 1)
                    return
                t = int(f[2])
                if f[:2] == "kv":
                    for h in range(BH):
                        p0 = 64 * (h % 2)
                        ins = nc.tensor.matmul(b[p0:p0 + 64, DV * (h // 2):DV * (h // 2) + DV],
                                               k_rows[:, t, 64 * h:64 * h + 64], vb[:, t, DV * h:DV * h + DV],
                                               start=True, stop=True)
                    ins.then_inc(fill_done, 1)
                    return
                pe.wait_ge(fill_emptied, FILL_NO["kv0"] if t == 0 else FILL_NO[f"kv{t - 1}"] + 1)
                pe.wait_ge(fill_emptied, FILL_NO[(0, BH - 1)] + 1)
                for h in (int(f[3]), int(f[3]) + 2):
                    p0 = 64 * (h % 2)
                    o = b[:, DV * (h // 2):DV * (h // 2) + DV]
                    ins = nc.tensor.matmul(o, attn[:, TB * h + t, :], vb[:, t, DV * h:DV * h + DV], start=True,
                                           stop=(t == 0))
                    if t:
                        ins = nc.tensor.matmul(o, q_dec[p0:p0 + 64, S * (h // 2) + P * t:S * (h // 2) + P * t + P],
                                               state[p0:p0 + 64, t, DV * (h // 2):DV * (h // 2) + DV],
                                               start=False, stop=True)
                ins.then_inc(fill_done, 1)

            def fills(s_, half):
                for f in FILL_AT.get((s_, half), []):
                    fill(f)

            def qk(n):
                tb, h = divmod(n, AH)
                w, p0 = P * (tb + 1), 64 * (h % 2)
                if n == 0:
                    pe.wait_ge(fill_emptied, len(FILLS))
                    pe.wait_ge(act_emptied, evacs_through(FIRST[S_VA] - 1, "act"))
                if n >= 2:
                    pe.wait_ge(logit_ready, n - 1)
                b = bank[4 + n % 2][:, 0:w]
                nc.tensor.matmul(b, qaT[p0:p0 + 64, h // 2, P * tb:P * tb + P], kaT[p0:p0 + 64, h // 2, 0:w],
                                 start=True, stop=False)
                if tb and h == 0:
                    pe.wait_ge(mask_ready, tb)
                nc.tensor.matmul(b, ident_bf[:], neg_mask[:, MASK_AT[tb]:MASK_AT[tb] + w], start=False,
                                 stop=True).then_inc(qk_done, 1)

            def prob_transpose(n):
                tb = n // AH
                pe.wait_ge(prob_ready, n + 1)
                if n >= 1:
                    pe.wait_ge(probT_ready, n)
                for i in range(tb + 1):
                    ins = nc.tensor.transpose(bank[6][:, P * i:P * i + P], prob[n % 2][:, P * i:P * i + P], ident[:])
                ins.then_inc(probT_done, 1)

            def pv(n):
                tb, h = divmod(n, AH)
                pe.wait_ge(probT_ready, n + 1)
                if n == 0:
                    pe.wait_ge(act_emptied, evacs_through(FIRST[S_VA] + 3, "act"))
                if h == 0 and tb:
                    pe.wait_ge(oa_emptied, tb)
                for i in range(tb + 1):
                    ins = nc.tensor.matmul(bank[7][:, AD * h:AD * h + AD], probT[n % 2][:, P * i:P * i + P],
                                           va[:, i, AD * h:AD * h + AD], start=(i == 0), stop=(i == tb))
                ins.then_inc(pv_done, 1)

            for s_ in range(3, S_OE):
                slot_ready(s_)
                if SLOTS[s_][0] == "a":
                    for half in range(2):
                        group_a(s_, half)
                        fills(s_, half)
                elif s_ < ATT_S0:
                    for half in range(2):
                        unit_b(s_, 2 * half)
                        unit_b(s_, 2 * half + 1)
                        fills(s_, half)
                    if s_ == ATT_S0 - 1:
                        qk(0)
                else:
                    for t in range(TB):
                        for half in range(2):
                            n = AH * (s_ - ATT_S0) + 2 * t + half
                            if n + 1 < NSTEP:
                                qk(n + 1)
                            unit_b(s_, t, part=(2 * half, 2 * half + 2))
                            prob_transpose(n)
                            if n:
                                pv(n - 1)
            pv(NSTEP - 1)
            transpose_rows(1, range(KC), lambda n: (pe.wait_ge(mixed, 1) if n == 0 else
                                                  pe.wait_ge(mixed, 2) if n == 4 else None))
            for s_ in range(S_OE, S_ODD):
                slot_ready(s_)
                for t in range(TB):
                    unit_b(s_, t, hT_round=1 if s_ < S_OE + 2 and t == 0 else None)
            transpose_rows(2, range(KC), lambda n: pe.wait_ge(normed, 2 * TB) if n == 0 else None)

            def ln_sum(c):
                pe.wait_ge(conv_done, c + 1)
                ins = nc.tensor.matmul(bank[4][:], ones[:], conv_y(c), start=(c == 0), stop=(c == KC - 1))
                if c == KC - 1:
                    ins.then_inc(mean_done, 1)

            for s_ in range(S_ODD, S_OO):
                slot_ready(s_)
                group_a(s_, 0, hT_round=2 if s_ == S_ODD else None)
                group_a(s_, 1)
            for c in range(KC):
                ln_sum(c)
            for c in range(KC):
                pe.wait_ge(lnsq_ready, c + 1)
                ins = nc.tensor.matmul(bank[5][:], ones[:], ln_sq[c % 2], start=(c == 0), stop=(c == KC - 1))
                ins.then_inc(lnsq_used if c < KC - 1 else mean_done, 1)
            for s_ in range(S_OO, NS):
                slot_ready(s_)
                for t in range(TB):
                    unit_b(s_, t, hT_round=3 if s_ < S_OO + 2 and t == 0 else None)


_INS = ["x", "rel_bias", "norm_even", "w_in_even", "w_gla_lr", "b_gla_lr", "gla_norm", "w_out_even", "norm_odd",
        "w_in_odd", "conv_w", "conv_b", "conv_ln_g", "conv_ln_b", "w_out_odd", "norm_f"]
_OUTS = [((1, 512, 1024), "float32")]


def kernel(**inputs):
    import numpy as _np
    import concourse.bacc as _bacc
    from concourse import mybir as _mybir
    from concourse.bass_utils import run_bass_kernel_spmd as _run

    nc = _bacc.Bacc("TRN2", target_bir_lowering=False, num_devices=1)
    arrays, args = {}, []
    for name in _INS:
        a = _np.ascontiguousarray(inputs[name])
        arrays[f"in_{name}_dram"] = a
        args.append(nc.dram_tensor(f"in_{name}_dram", a.shape, _mybir.dt.from_np(a.dtype), kind="ExternalInput").ap())
    for i, (shape, dtype) in enumerate(_OUTS):
        dt = _mybir.dt.from_np(_np.dtype(dtype))
        args.append(nc.dram_tensor(f"out_{i}_dram", shape, dt, kind="ExternalOutput").ap())
    hybrid_trunk(nc, *args)
    r = _run(nc, [arrays], core_ids=[0])
    return r.results[0]["out_0_dram"]
```

```python
from contextlib import ExitStack

import concourse.bass as bass
from concourse import mybir

F32 = mybir.dt.float32
F32R = mybir.dt.float32r
BF16 = mybir.dt.bfloat16
I32 = mybir.dt.int32
U8 = mybir.dt.uint8
ALU = mybir.AluOpType
ACT = mybir.ActivationFunctionType
AX = mybir.AxisListType

P = 128
D = 1024
S = 512
KC = D // P
TB = S // P
EPS = 1e-6
AH, AD = 8, 64
IH, ID = 4, 64
BH, DK, DV = 4, 64, 128
RANK = 16
TAU = 16.0
TOPK = min(256, S // 4)
CW = 31
NB, MAXEX, MAXD = 32, 16, 128
PE_TAPS, POOL_TAPS = 2, 6
NEG = -1.0e30
HIDDEN = -2.0e38
TAKEN = -3.0e38

C_QA, C_KA, C_VA, C_GA = 0, 512, 1024, 1536
C_QI = 2048
C_KI = C_QI + IH * ID
C_WI = C_KI + ID
C_QB = C_WI + IH
C_KB = C_QB + BH * DK
C_VB = C_KB + BH * DK
C_GB = C_VB + BH * DV
C_LR = C_GB + BH * DV


B_FIRST = (4, 5, 6, 7, 0, 1, 2, 3)


def bucket_starts():
    import math
    first = {}
    for d in range(S):
        if d < MAXEX:
            b = d
        else:
            b = min(NB - 1, MAXEX + int(math.log(d / MAXEX) / math.log(MAXD / MAXEX) * (NB - MAXEX) + 1e-6))
        first.setdefault(b, d)
    return [first[b] for b in range(NB)]


def plan_slots():
    a = lambda m, c: ("a", (0,), [(0, m, c, 256)])
    b = lambda m, c, ks: [("b", ks[0:4], [(0, m, c, 512)]), ("b", ks[4:8], [(0, m, c, 512)])]
    up = tuple(range(KC))
    s = [a("e", C_QI),
         ("a", (0,), [(0, "e", C_KI, ID), (ID, "e", C_KI, ID), (128, "e", C_LR, RANK), (144, "e", C_WI, IH)]),
         a("e", C_QB), a("e", C_KB)]
    s += b("e", C_VB, up)
    s += [a("e", C_QA), a("e", C_QA + 256), a("e", C_KA), a("e", C_KA + 256)]
    s += b("e", C_VA, up) + b("e", C_GB, up) + b("e", C_GA, up)
    s += b("oe", 0, B_FIRST) + b("oe", 512, B_FIRST)
    vg = lambda c: ("a", (0,), [(0, "o", c * P, P), (P, "o", D + c * P, P)])
    gate = lambda n: a("o", 2 * D + n * 256)
    s += [vg(0), vg(1), gate(0), vg(2), vg(3), gate(1), vg(4), vg(5), gate(2), vg(6), vg(7), gate(3)]
    s += b("oo", 0, up) + b("oo", 512, up)
    return s


def hybrid_trunk(nc, x, rel_bias, norm_even, w_in_even, w_gla_lr, b_gla_lr, gla_norm, w_out_even,
                 norm_odd, w_in_odd, conv_w, conv_b, conv_ln_g, conv_ln_b, w_out_odd, norm_f, out):
    SLOTS = plan_slots()
    NS = len(SLOTS)
    WSRC = {"e": w_in_even[0], "oe": w_out_even[0], "o": w_in_odd[0], "oo": w_out_odd[0]}
    S_VB, S_QA, S_KA, S_VA, S_GB, S_GA, S_OE, S_ODD, S_OO = 4, 6, 8, 10, 12, 14, 16, 20, 32
    FIRST, evac_by = {}, []
    CHUNK, GATE = {}, {}
    for j, (kind, ks, pieces) in enumerate(SLOTS):
        if kind == "a":
            FIRST[j] = len(evac_by)
            if S_ODD <= j < S_OO:
                c0 = pieces[0][2]
                if c0 < D:
                    CHUNK[j] = c0 // P
                    evac_by += ["val", "act"]
                else:
                    GATE[j] = (c0 - 2 * D) // P
                    evac_by += ["act", "act"]
            else:
                evac_by += ["act", "act"]
        elif j % 2 == 0:
            FIRST[j] = FIRST[j + 1] = len(evac_by)
            evac_by += ["residual" if j >= S_OE else "act"] * TB

    def evacs_through(g, who):
        return sum(1 for e in evac_by[:g + 1] if e == who)

    raw_full, n_in = {}, [0, 0]
    for j, (_, ks, pieces) in enumerate(SLOTS):
        n_in[j % 2] += 16 * len(pieces)
        raw_full[j] = n_in[j % 2]

    ctx = ExitStack()
    with ctx:
        def sb(name, shape, dt=F32):
            return ctx.enter_context(nc.sbuf_tensor(name, shape, dt))

        def sem(name):
            return ctx.enter_context(nc.semaphore(name))

        w_raw = [sb(f"w_raw{i}", [P, 2048]) for i in range(2)]
        w_hi = [sb(f"w_hi{i}", [P, 2048], F32R) for i in range(3)]
        w_lo = [sb(f"w_lo{i}", [P, 2048], F32R) for i in range(3)]
        hT_hi = sb("hT_hi", [P, KC, S], F32R)
        hT_lo = sb("hT_lo", [P, KC, S], F32R)
        r_x = sb("r_x", [P, 4096])
        r_oa = sb("r_oa", [P, 2048])
        r_ob = sb("r_ob", [P, 2048])
        r_qa = sb("r_qa", [P, 2048])
        r_ka = sb("r_ka", [P, 2048])
        r_va = sb("r_va", [P, 2048])
        r_vb = sb("r_vb", [P, 2048])
        r_qkb = sb("r_qkb", [P, 2048])
        r_g = sb("r_g", [P, 4096])
        r_att = sb("r_att", [P, 2048])
        neg_mask = sb("neg_mask", [P, 1280], BF16)
        ident = sb("ident", [P, P])
        ident_bf = sb("ident_bf", [P, P], BF16)
        ones = sb("ones", [P, P])
        level_mask = sb("level_mask", [P, 6, P], U8)
        NROW = CW + 5
        pvec = sb("pvec", [P, KC, NROW])
        pb3 = sb("pb3", [P, 4])
        small_rows = sb("small_rows", [3, P])
        rel_rows = sb("rel_rows", [AH, NB])
        w_lr = sb("w_lr", [RANK, BH * DK])
        lwT = sb("lwT", [RANK + IH, S])
        wi = sb("wi", [P, TB, IH])
        stat = sb("stat", [P, 16])
        half_sq = sb("half_sq", [P, 2 * TB])
        ln_var = sb("ln_var", [P, TB])
        rstd = sb("rstd", [P, 16])
        minus_half = sb("minus_half", [P, 16])
        top8 = sb("top8", [P, 3, 8])
        row_max = sb("row_max", [P, TB * AH])
        neg_max = sb("neg_max", [P, TB * AH])
        row_sum = sb("row_sum", [P, TB * AH])
        row_inv = sb("row_inv", [P, TB * AH])
        chunk_decay = sb("chunk_decay", [P, 2, TB])
        state = sb("state", [P, TB, 2 * DV])

        x_t = r_x[:].rearrange("p (t d) -> p t d", t=TB)
        bias_tab = r_x[:].rearrange("p (h u) -> p h u", h=AH)
        oa = r_oa[:].rearrange("p (t d) -> p t d", t=TB)
        ob = r_ob[:].rearrange("p (t d) -> p t d", t=TB)
        qaT = r_qa[:].rearrange("p (c t) -> p c t", c=4)
        kaT = r_ka[:].rearrange("p (c t) -> p c t", c=4)
        va = r_va[:].rearrange("p (t d) -> p t d", t=TB)
        vb = r_vb[:].rearrange("p (t d) -> p t d", t=TB)
        qbT = r_qkb[:, 0:1024]
        kbT = r_qkb[:, 1024:2048]
        gate_a = r_qkb[:].rearrange("p (t d) -> p t d", t=TB)
        gate_b = vb
        qiT = r_qa[:, 0:1024].rearrange("p (c t) -> p c t", c=2)
        kiT = r_qa[:, 1024:1536]
        relu_b = [r_ka[:, 512 * i:512 * i + 512] for i in range(4)]
        score = {tb: r_va[:, o:o + P * (tb + 1)] for tb, o in ((1, 0), (2, 256), (3, 640))}
        MASK_AT = (0, 128, 384, 768)
        bsum = r_ob[:, 0:1024]
        lin = [r_g[:, 1024 * i:1024 * (i + 1)] for i in range(4)]
        q_dec = r_oa[:, 0:1024]
        k_rows = r_oa[:, 1024:1792].rearrange("p (t c) -> p t c", t=3)
        attn = r_att[:].rearrange("p (g i) -> p g i", g=BH * TB)
        param_rows = r_att[:, 0:D]
        junk = r_att[:, D:2 * D]
        iota_i = r_vb[:, 0:128].bitcast(I32)
        iota_p = r_vb[:, 128:256].bitcast(I32)
        ixor = r_vb[:, 256:384].bitcast(I32)
        ixor_up = r_vb[:, 384:512].bitcast(I32)
        ishift = r_vb[:, 512:640].bitcast(I32)
        bias_rev = r_vb[0:AH, 1024:1664]
        logit = [r_g[:, 512 * i:512 * i + 512] for i in (0, 1)]
        prob = [r_g[:, 1024 + 512 * i:1536 + 512 * i] for i in (0, 1)]
        probT = [r_g[:, 2048 + 512 * i:2560 + 512 * i] for i in (0, 1)]
        sq_b = [r_g[:, 3072 + 512 * i:3584 + 512 * i] for i in (0, 1)]
        conv_y = lambda c: (r_oa if c < 4 else r_ob)[:, 512 * (c % 4):512 * (c % 4) + 512]
        PADW = S + CW - 1
        upad = [r_va[:, 576 * i:576 * i + PADW] for i in range(3)]
        sgl = [r_vb[:, 512 * i:512 * i + 512] for i in (0, 1)]
        m_f32 = [r_g[:, 512 * i:512 * i + 512] for i in range(4)]
        prod = [r_g[:, 1024 + 512 * i:1536 + 512 * i] for i in range(3)]
        pool_acc = [r_g[:, 2560 + 512 * i:3072 + 512 * i] for i in range(3)]
        tap_diag = [[r_vb[:, 1536 + P * (PE_TAPS * i + k):1536 + P * (PE_TAPS * i + k + 1)]
                     for k in range(PE_TAPS)] for i in range(2)]
        ln_diag = r_vb[:, 1024:1024 + S]
        ln_sq = [r_qkb[:, 512 * i:512 * i + 512] for i in (0, 1)]
        gate_s = lambda c: (r_qa if c < 4 else r_ka)[:, 512 * (c % 4):512 * (c % 4) + 512]
        nf_row = r_att[:, 0:D]
        sq_junk = r_att[:, D:2 * D]
        ROW_NE, ROW_NO, ROW_CB, ROW_LG, ROW_LB = CW, CW + 1, CW + 2, CW + 3, CW + 4

        def hx(tb, c):
            return (oa if c < 4 else ob)[:, tb, P * (c % 4):P * (c % 4) + P]

        bank = [ctx.enter_context(nc.psum_tensor(f"bank{i}", [P, 512], F32)) for i in range(8)]

        x_in = [sem(f"x_in{t}") for t in range(TB)]
        params_in = sem("params_in")
        rel_in = sem("rel_in")
        raw_in = [sem(f"raw_in{i}") for i in range(2)]
        table_in = sem("table_in")
        x_again = sem("x_again")
        nf_in = sem("nf_in")
        out_done = sem("out_done")
        pool_const = sem("pool_const")
        pool_chain = sem("pool_chain")
        hi_ready = sem("hi_ready")
        lo_ready = sem("lo_ready")
        squares = sem("squares")
        half_squares = sem("half_squares")
        var_ready = sem("var_ready")
        rstd_ready = sem("rstd_ready")
        normed = sem("normed")
        params_T = sem("params_T")
        pvec_ready = sem("pvec_ready")
        rev_ready = sem("rev_ready")
        xor_ready = sem("xor_ready")
        hT_in_bank = sem("hT_in_bank")
        hT_hi_ready = sem("hT_hi_ready")
        hT_ready = sem("hT_ready")
        half_used = sem("half_used")
        group_done = sem("group_done")
        act_emptied = sem("act_emptied")
        dve_emptied = sem("dve_emptied")
        wi_T = sem("wi_T")
        wi_ready = sem("wi_ready")
        z_done = sem("z_done")
        z_added = sem("z_added")
        softplus = sem("softplus")
        bsum_ready = sem("bsum_ready")
        idx_done = sem("idx_done")
        relu_ready = sem("relu_ready")
        score_step = sem("score_step")
        masks_ready = sem("masks_ready")
        causal_ready = sem("causal_ready")
        mask_ready = sem("mask_ready")
        act_chain = sem("act_chain")
        dve_chain = sem("dve_chain")
        diff_ready = sem("diff_ready")
        exp_ready = sem("exp_ready")
        operand_ready = sem("operand_ready")
        fill_done = sem("fill_done")
        fill_emptied = sem("fill_emptied")
        ob_squared = sem("ob_squared")
        ob_summed = sem("ob_summed")
        ob_var = sem("ob_var")
        ob_rstd = sem("ob_rstd")
        att_zero = sem("att_zero")
        qk_done = sem("qk_done")
        logit_ready = sem("logit_ready")
        max_ready = sem("max_ready")
        prob_ready = sem("prob_ready")
        probT_done = sem("probT_done")
        probT_ready = sem("probT_ready")
        pv_done = sem("pv_done")
        oa_emptied = sem("oa_emptied")
        gates_silu = sem("gates_silu")
        u_ready = sem("u_ready")
        conv_done = sem("conv_done")
        mean_done = sem("mean_done")
        centred = sem("centred")
        lnsq_ready = sem("lnsq_ready")
        lnsq_used = sem("lnsq_used")
        lnvar_done = sem("lnvar_done")
        lnvar_ready = sem("lnvar_ready")
        lnrstd_ready = sem("lnrstd_ready")
        lndiag_ready = sem("lndiag_ready")
        lnrstd_wide = sem("lnrstd_wide")
        topk_step = sem("topk_step")
        diag_ready = sem("diag_ready")
        taps_done = sem("taps_done")
        prod_ready = sem("prod_ready")
        pool_added = sem("pool_added")
        dve_taps_done = sem("dve_taps_done")
        tap_step = sem("tap_step")
        mixed_b = sem("mixed_b")
        mixed_a = sem("mixed_a")
        scaled = sem("scaled")
        ln_silu = sem("ln_silu")
        m_ready = sem("m_ready")
        y_ready = sem("y_ready")

        LEVELS = [64, 32, 16, 8, 4, 2, 1]
        ITEMS = ["k"] + LEVELS
        ITEM_STEP = {6: ["k"], 7: [64], 8: [32, 16], 9: [8, 4], 10: [2, 1]}
        ITEM_NO = {it: n for n, it in enumerate(ITEMS)}
        FILLS = ["k0", "k1"] + [(lv, h) for lv in LEVELS for h in range(BH)] + [(0, h) for h in range(BH)]
        OB_FILLS = [f"ob{t}{par}" for t in range(TB) for par in range(2)]
        FILLS += ["kv0", "kv1", "kv2"] + OB_FILLS
        FILL_NO = {f: n for n, f in enumerate(FILLS)}
        FILL_AT = {}
        for s_, its in ITEM_STEP.items():
            for half, it in enumerate(its):
                FILL_AT[(s_, half if len(its) == 2 else 1)] = ["k0", "k1"] if it == "k" else [(it, h) for h in range(BH)]
        FILL_AT[(11, 0)] = [(0, h) for h in range(BH)] + ["kv0", "kv1", "kv2"]
        FILL_AT[(11, 1)] = OB_FILLS
        LAST_FILL = {"k": FILL_NO["k1"], **{lv: FILL_NO[(lv, BH - 1)] for lv in LEVELS}}

        NSTEP = TB * AH
        ATT_S0 = S_GB

        def wait_slot_used(eng, j):
            if SLOTS[j][0] == "a":
                eng.wait_ge(group_done, FIRST[j] + 2)
            elif j % 2:
                eng.wait_ge(group_done, FIRST[j] + TB)
            else:
                eng.wait_ge(half_used, sum(1 for i in range(0, j + 1, 2) if SLOTS[i][0] == "b"))

        block = ctx.enter_context(nc.Block())

        @block.sync
        def _(sp):
            x_rows = x[0].rearrange("(t p) d -> t p d", p=P)
            sp.dma_start(x_t[:, 0, :], x_rows[0]).then_inc(x_in[0], 16)
            sp.dma_start(param_rows[0:CW, :], conv_w[0]).then_inc(params_in, 16)
            for r, v in ((ROW_NE, norm_even), (ROW_NO, norm_odd), (ROW_CB, conv_b), (ROW_LG, conv_ln_g),
                         (ROW_LB, conv_ln_b)):
                sp.dma_start(param_rows[r:r + 1, :], v).then_inc(params_in, 16)
            sp.dma_start(small_rows[0:2, :], b_gla_lr[0].rearrange("(a n) -> a n", a=2)).then_inc(params_in, 16)
            sp.dma_start(small_rows[2:3, :], gla_norm).then_inc(params_in, 16)
            sp.dma_start(w_lr[:], w_gla_lr[0]).then_inc(params_in, 16)
            for t in range(1, TB):
                sp.dma_start(x_t[:, t, :], x_rows[t]).then_inc(x_in[t], 16)

            def load(j):
                kind, ks, pieces = SLOTS[j]
                if j >= 2:
                    sp.wait_ge(lo_ready, j - 1)
                for at, m, c0, n in pieces:
                    if kind == "a":
                        dst = w_raw[j % 2][:].rearrange("p (k n) -> p k n", k=KC)[:, :, at:at + n]
                        src = WSRC[m].rearrange("(k p) n -> p k n", p=P)[:, :, c0:c0 + n]
                    else:
                        dst = w_raw[j % 2][:].rearrange("p (k n) -> p k n", k=4)
                        src = WSRC[m].rearrange("(k p) n -> p k n", p=P)[:, ks[0]:ks[0] + 4, c0:c0 + n]
                    sp.dma_start(dst, src).then_inc(raw_in[j % 2], 16)

            load(0)
            sp.dma_start(rel_rows[:], rel_bias.rearrange("b h -> h b"),
                         allow_slow_non_contiguous=True).then_inc(rel_in, 16)
            load(1)
            sp.wait_ge(rev_ready, 1)
            sp.wait_ge(normed, TB)
            for h in range(AH):
                row = bias_rev[h:h + 1, 127:127 + S]
                src = bass.AP(row.tensor, row.offset, [list(row.ap[0]), [-1, P], [1, S]])
                sp.dma_start(bias_tab[:, h, :], src).then_inc(table_in, 16)
            for j in range(2, NS):
                if j == S_OE + 2:
                    sp.wait_ge(logit_ready, NSTEP)
                    sp.dma_start(x_t, x[0].rearrange("(t p) d -> p t d", p=P)).then_inc(x_again, 16)
                if j == S_ODD + 4:
                    sp.wait_ge(group_done, FIRST[S_ODD])
                    sp.dma_start(nf_row, norm_f.rearrange("(a n) -> a n", a=1).to_broadcast([P, D])).then_inc(nf_in, 16)
                load(j)
            out_rows = out[0].rearrange("(t p) d -> t p d", p=P)
            for t in range(TB):
                for half in range(2):
                    cols = slice(512 * half, 512 * half + 512)
                    sp.wait_ge(y_ready, 2 * t + half + 1)
                    sp.dma_start(out_rows[t][:, cols], x_t[:, t, cols]).then_inc(out_done, 16)
            sp.wait_ge(out_done, 16 * 2 * TB)

        @block.gpsimd
        def _(pool):
            chain = [0]

            def link(ins):
                chain[0] += 1
                ins.then_inc(pool_chain, 1)
                pool.wait_ge(pool_chain, chain[0])

            def affine(dst, src, op, fill, step, mult):
                return nc.gpsimd.affine_select(out=dst, in_=src, compare_op=op, fill=fill, base=0,
                                               pattern=[[step, P]], channel_multiplier=mult)

            link(nc.gpsimd.memset(ident[:], 0.0))
            link(affine(ident[:], ident[:], ALU.not_equal, 1.0, -1, 1))
            nc.gpsimd.memset(ones[:], 1.0).then_inc(pool_const, 1)
            link(nc.gpsimd.memset(minus_half[:], -0.5))
            nc.gpsimd.memset(ident_bf[:], 0.0).then_inc(pool_const, 1)
            pool.wait_ge(pool_const, 2)
            affine(ident_bf[:], ident_bf[:], ALU.not_equal, 1.0, -1, 1).then_inc(pool_const, 1)
            link(nc.gpsimd.memset(neg_mask[:, 0:P], 0.0))
            affine(neg_mask[:, 0:P], neg_mask[:, 0:P], ALU.is_ge, NEG, -1, 1).then_inc(pool_const, 1)
            nc.gpsimd.iota(iota_i, [[1, P]], base=0, channel_multiplier=0).then_inc(pool_const, 1)
            nc.gpsimd.iota(iota_p, [[0, P]], base=0, channel_multiplier=1).then_inc(pool_const, 1)

            def rsqrt(first, last, ready, value, done):
                pool.wait_ge(ready, value)
                nc.gpsimd.tensor_tensor(rstd[:, first:last], stat[:, first:last], minus_half[:, first:last],
                                        ALU.pow).then_inc(done, 1)

            def split_lo(j):
                pool.wait_ge(hi_ready, j + 1)
                if j >= 3:
                    wait_slot_used(pool, j - 3)
                if j == 1:
                    v = lambda t: t[:].rearrange("p (k n) -> p k n", k=KC)[:, :, 0:148]
                else:
                    v = lambda t: t[:]
                nc.gpsimd.tensor_tensor(v(w_lo[j % 3]), v(w_raw[j % 2]), v(w_hi[j % 3]).bitcast(F32),
                                        ALU.subtract).then_inc(lo_ready, 1)

            for t in range(TB):
                rsqrt(t, t + 1, var_ready, t + 1, rstd_ready)
            pool.wait_ge(xor_ready, 1)
            affine(ixor_up, ixor, ALU.is_gt, 0.0, 1, -1).then_inc(pool_const, 1)
            split_lo(0)
            split_lo(1)
            pool.wait_ge(params_T, 2)
            pool.wait_ge(squares, TB)
            nc.gpsimd.memset(r_att[:], 0.0).then_inc(att_zero, 1)

            def diff(it):
                n = ITEM_NO[it]
                pool.wait_ge(bsum_ready, 1)
                if n >= 4:
                    pool.wait_ge(fill_done, LAST_FILL[ITEMS[n - 4]] + 1)
                dst = lin[n % 4]
                if it == "k":
                    dv = dst.rearrange("p (b c) -> p b c", c=P)
                    bv = bsum.rearrange("p (b c) -> p b c", c=P)
                    last = bv[:, :, P - 1:P].to_broadcast([P, 8, P])
                    nc.gpsimd.tensor_tensor(dv, last, bv, ALU.subtract).then_inc(diff_ready, 2)
                    return
                nb = D // (2 * it)
                dv = dst.rearrange("p (b c) -> p b c", c=2 * it)
                bv = bsum.rearrange("p (b c) -> p b c", c=2 * it)
                ref = bv[:, :, it - 1:it].to_broadcast([P, nb, it])
                nc.gpsimd.tensor_tensor(dv[:, :, 0:it], ref, bv[:, :, 0:it], ALU.subtract).then_inc(diff_ready, 1)
                nc.gpsimd.tensor_tensor(dv[:, :, it:], bv[:, :, it:], ref, ALU.subtract).then_inc(diff_ready, 1)

            def add_products(c):
                for k in range(1, POOL_TAPS):
                    pool.wait_ge(prod_ready, POOL_TAPS * c + k + 1)
                    if k > 1:
                        pool.wait_ge(pool_added, (POOL_TAPS - 1) * c + k - 1)
                    n = (POOL_TAPS - 1) * c + k - 1
                    nc.gpsimd.tensor_tensor(pool_acc[c % 3], pool_acc[c % 3], prod[n % 3], ALU.add).then_inc(pool_added, 1)

            def finish_conv(c):
                pool.wait_ge(dve_taps_done, c + 1)
                pool.wait_ge(pool_added, (POOL_TAPS - 1) * (c + 1))
                nc.gpsimd.tensor_tensor(conv_y(c), conv_y(c), pool_acc[c % 3], ALU.add).then_inc(conv_done, 1)

            for s_ in range(NS):
                if s_ + 2 < NS:
                    split_lo(s_ + 2)
                if s_ == 2:
                    for n, tb in enumerate((1, 2, 3)):
                        pool.wait_ge(score_step, IH * (n + 1))
                        diag = score[tb][:, P * tb:P * tb + P]
                        affine(diag, diag, ALU.is_ge, HIDDEN, -1, 1).then_inc(causal_ready, 1)
                for it in ITEM_STEP.get(s_ + 1, []):
                    diff(it)
                if s_ == 12:
                    rsqrt(0, 16, ob_var, 1, ob_rstd)
                if s_ == S_OE + 3:
                    for t in range(TB):
                        rsqrt(t, t + 1, var_ready, TB + t + 1, rstd_ready)
                if s_ in CHUNK:
                    if CHUNK[s_] >= 1:
                        add_products(CHUNK[s_] - 1)
                    if CHUNK[s_] >= 3:
                        finish_conv(CHUNK[s_] - 3)
                if s_ == S_OO - 1:
                    add_products(KC - 1)
                    for c in range(KC - 3, KC):
                        finish_conv(c)
                    pool.wait_ge(lnvar_ready, 1)
                    nc.gpsimd.tensor_tensor(rstd[:, 0:TB], ln_var[:], minus_half[:, 0:TB], ALU.pow).then_inc(lnrstd_ready, 1)
                    for c in range(KC):
                        pool.wait_ge(hT_hi_ready, 3 * KC + c + 1)
                        nc.gpsimd.tensor_tensor(hT_lo[:, c, :], m_f32[c % 4], hT_hi[:, c, :].bitcast(F32),
                                                ALU.subtract).then_inc(hT_ready, 1)
            for t in range(TB):
                rsqrt(t, t + 1, var_ready, 2 * TB + t + 1, rstd_ready)

        @block.scalar
        def _(act):
            chain = [0]

            def link(ins):
                chain[0] += 1
                ins.then_inc(act_chain, 1)
                act.wait_ge(act_chain, chain[0])

            def split_hi(j):
                act.wait_ge(raw_in[j % 2], raw_full[j])
                if j >= 3:
                    wait_slot_used(act, j - 3)
                if j == 1:
                    v = lambda t: t[:].rearrange("p (k n) -> p k n", k=KC)[:, :, 0:148]
                else:
                    v = lambda t: t[:]
                nc.scalar.activation(v(w_hi[j % 3]), v(w_raw[j % 2]), ACT.Copy).then_inc(hi_ready, 1)

            def hT_high(rnd, order, bank_of, scale):
                for n, c in enumerate(order):
                    act.wait_ge(hT_in_bank, KC * rnd + n + 1)
                    nc.scalar.activation(hT_hi[:, c, :], bank[bank_of(n)][:], ACT.Copy,
                                         scale=scale(c)).then_inc(hT_hi_ready, 1)

            def empty(g, dst, rows=P, scale=1.0, func=ACT.Copy):
                act.wait_ge(group_done, g + 1)
                nc.scalar.activation(dst, bank[g % 4][0:rows, :], func, scale=scale).then_inc(act_emptied, 1)

            for t in range(TB):
                act.wait_ge(x_in[t], 16)
                if t:
                    act.wait_ge(squares, t)
                nc.scalar.activation(junk, x_t[:, t, :], ACT.Square, accum_out=stat[:, t:t + 1]).then_inc(squares, 1)
            split_hi(0)
            act.wait_ge(pvec_ready, 2)
            hT_high(0, range(KC), lambda n: n, lambda c: pvec[:, c, ROW_NE:ROW_NE + 1])
            split_hi(1)

            def exps(it):
                n = ITEM_NO[it]
                act.wait_ge(diff_ready, 2 * (n + 1))
                nc.scalar.activation(lin[n % 4], lin[n % 4], ACT.Exp, scale=1.0 / TAU).then_inc(exp_ready, 1)

            def soft(n):
                act.wait_ge(max_ready, n + 1)
                if n >= 2:
                    act.wait_ge(probT_done, n - 1)
                w = P * (n // AH + 1)
                nc.scalar.activation(prob[n % 2][:, 0:w], logit[n % 2][:, 0:w], ACT.Exp, bias=neg_max[:, n:n + 1],
                                     accum_out=row_sum[:, n:n + 1]).then_inc(prob_ready, 1)

            for s_ in range(S_OE):
                if s_ + 2 < NS:
                    split_hi(s_ + 2)
                g = FIRST[s_]
                if s_ == 0:
                    empty(g, qiT[:, 0, :])
                    empty(g + 1, qiT[:, 1, :])
                elif s_ == 1:
                    empty(g, kiT)
                    empty(g + 1, lwT[:], rows=RANK + IH)
                elif s_ == 2:
                    empty(g, qbT[:, 0:S], scale=DK ** -0.5)
                    act.wait_ge(wi_T, 1)
                    nc.scalar.activation(wi[:], bank[6][:, 0:TB * (RANK + IH)].rearrange(
                        "p (t c) -> p t c", t=TB)[:, :, RANK:], ACT.Copy,
                        scale=ID ** -0.5 * IH ** -0.5).then_inc(wi_ready, 1)
                    n = 0
                    for tb in (1, 2, 3):
                        for h in range(IH):
                            act.wait_ge(idx_done, n + 1)
                            if n >= 4:
                                act.wait_ge(score_step, n - 3)
                            w = P * (tb + 1)
                            nc.scalar.activation(relu_b[n % 4][:, 0:w], bank[4 + n % 2][:, 0:w],
                                                 ACT.Relu).then_inc(relu_ready, 1)
                            n += 1
                    empty(g + 1, qbT[:, S:], scale=DK ** -0.5)
                    act.wait_ge(z_added, 2)
                    link(nc.scalar.activation(lin[1], lin[0], ACT.Abs))
                    link(nc.scalar.activation(lin[1], lin[1], ACT.Exp, scale=-1.0))
                    nc.scalar.activation(lin[1], lin[1], ACT.Ln, bias=1.0).then_inc(softplus, 1)
                elif s_ == 3:
                    empty(g, kbT[:, 0:S])
                    empty(g + 1, kbT[:, S:])
                    act.wait_ge(bsum_ready, 1)
                    nc.scalar.activation(q_dec, bsum, ACT.Exp, scale=1.0 / TAU).then_inc(exp_ready, 1)
                elif s_ == S_VB + 1:
                    act.wait_ge(table_in, 16 * AH)
                    act.wait_ge(masks_ready, 1)
                    for t in range(TB):
                        empty(g + t, vb[:, t, :])
                    exps("k")
                elif S_QA <= s_ < S_VA:
                    its = ITEM_STEP.get(s_ + 1, [])
                    c = 2 * (s_ - S_QA) if s_ < S_KA else 2 * (s_ - S_KA)
                    if s_ == S_KA:
                        act.wait_ge(score_step, 3 * IH)
                    dst = qaT if s_ < S_KA else kaT
                    sc = AD ** -0.5 if s_ < S_KA else 1.0
                    empty(g, dst[:, c, :], scale=sc)
                    if its:
                        exps(its[0])
                    empty(g + 1, dst[:, c + 1, :], scale=sc)
                    for it in its[1:]:
                        exps(it)
                elif s_ == S_VA + 1:
                    act.wait_ge(mask_ready, 3)
                    for t in range(TB):
                        empty(g + t, va[:, t, :])
                    for t in range(TB):
                        act.wait_ge(fill_emptied, FILL_NO[f"ob{t}1"] + 1)
                        if t >= 2:
                            act.wait_ge(ob_summed, t - 1)
                        nc.scalar.activation(sq_b[t % 2], ob[:, t, :], ACT.Square).then_inc(ob_squared, 1)
                    soft(0)
                elif s_ >= ATT_S0:
                    for u in range(TB):
                        n0 = AH * (s_ - ATT_S0) + 2 * u
                        if n0 + 1 < NSTEP:
                            soft(n0 + 1)
                        if n0 + 2 < NSTEP:
                            soft(n0 + 2)
                        if s_ == S_GB + 1:
                            if u == 0:
                                act.wait_ge(fill_done, len(FILLS))
                            empty(g + u, gate_b[:, u, :])
                        if s_ == S_GA + 1 and u < TB - 1:
                            empty(g + u, gate_a[:, u, :])
                    if s_ == S_GB + 1:
                        act.wait_ge(act_emptied, evacs_through(FIRST[S_GB] + 3, "act"))
                        nc.scalar.activation(r_vb[:], r_vb[:], ACT.Silu).then_inc(gates_silu, 1)
            act.wait_ge(act_emptied, evacs_through(FIRST[S_GA] + 2, "act"))
            nc.scalar.activation(gate_a[:, 0:TB - 1, :], gate_a[:, 0:TB - 1, :], ACT.Silu).then_inc(gates_silu, 1)
            empty(FIRST[S_GA] + TB - 1, gate_a[:, TB - 1, :], func=ACT.Silu)
            wait_slot_used(act, S_OE - 1)
            hT_high(1, B_FIRST, lambda n: n, lambda c: 1.0 if c < 4 else pb3[:, 2:3])

            def row_squares(base, n0):
                for half in range(2):
                    for t in range(TB):
                        act.wait_ge(dve_emptied, base + TB * half + t + 1)
                        n = TB * half + t
                        if n0 + n:
                            act.wait_ge(half_squares, n0 + n)
                        nc.scalar.activation(sq_junk[:, 0:512], x_t[:, t, 512 * half:512 * half + 512], ACT.Square,
                                             accum_out=half_sq[:, n:n + 1]).then_inc(half_squares, 1)

            for s_ in range(S_OE, S_ODD):
                split_hi(s_ + 2)
            row_squares(0, 0)
            wait_slot_used(act, S_ODD - 1)
            hT_high(2, range(KC), lambda n: 4 + n % 4, lambda c: pvec[:, c, ROW_NO:ROW_NO + 1])

            def products(c):
                act.wait_ge(u_ready, c + 1)
                for k in range(POOL_TAPS):
                    tap = PE_TAPS + k
                    src = upad[c % 3][:, tap:tap + S]
                    if k == 0:
                        if c >= 3:
                            act.wait_ge(conv_done, c - 2)
                        nc.scalar.activation(pool_acc[c % 3], src, ACT.Identity, scale=pvec[:, c, tap:tap + 1],
                                             bias=pvec[:, c, ROW_CB:ROW_CB + 1]).then_inc(prod_ready, 1)
                    else:
                        n = (POOL_TAPS - 1) * c + k - 1
                        if n >= 3:
                            act.wait_ge(pool_added, n - 2)
                        nc.scalar.activation(prod[n % 3], src, ACT.Copy,
                                             scale=pvec[:, c, tap:tap + 1]).then_inc(prod_ready, 1)

            def centre_squares():
                for c in range(KC):
                    act.wait_ge(centred, c + 1)
                    if c >= 2:
                        act.wait_ge(lnsq_used, c - 1)
                    nc.scalar.activation(ln_sq[c % 2], conv_y(c), ACT.Square).then_inc(lnsq_ready, 1)

            for s_ in range(S_ODD, S_OO):
                split_hi(s_ + 2)
                g = FIRST[s_]
                if s_ in CHUNK:
                    c = CHUNK[s_]
                    if c >= 2:
                        act.wait_ge(taps_done, c - 1)
                    for k in range(PE_TAPS):
                        nc.scalar.activation(tap_diag[c % 2][k], ident[:], ACT.Copy,
                                             scale=pvec[:, c, k:k + 1]).then_inc(diag_ready, 1)
                    if c >= 2:
                        act.wait_ge(u_ready, c - 1)
                    act.wait_ge(group_done, g + 2)
                    nc.scalar.activation(sgl[c % 2], bank[(g + 1) % 4][:], ACT.Sigmoid).then_inc(act_emptied, 1)
                    if c >= 1:
                        products(c - 1)
                else:
                    c = GATE[s_]
                    empty(g, gate_s(c))
                    if s_ == S_OO - 1:
                        products(KC - 1)
                        centre_squares()
                    empty(g + 1, gate_s(c + 1))
            act.wait_ge(act_emptied, evacs_through(FIRST[S_OO] - 1, "act"))
            nc.scalar.activation(r_qa[:], r_qa[:], ACT.Silu).then_inc(gates_silu, 1)
            nc.scalar.activation(r_ka[:], r_ka[:], ACT.Silu).then_inc(gates_silu, 1)
            for c in range(KC):
                act.wait_ge(scaled, c + 1)
                nc.scalar.activation(conv_y(c), conv_y(c), ACT.Silu, scale=pvec[:, c, ROW_LG:ROW_LG + 1],
                                     bias=pvec[:, c, ROW_LB:ROW_LB + 1]).then_inc(ln_silu, 1)
                if c >= 1:
                    act.wait_ge(m_ready, c)
                    nc.scalar.activation(hT_hi[:, c - 1, :], m_f32[(c - 1) % 4], ACT.Copy).then_inc(hT_hi_ready, 1)
            act.wait_ge(m_ready, KC)
            nc.scalar.activation(hT_hi[:, KC - 1, :], m_f32[(KC - 1) % 4], ACT.Copy).then_inc(hT_hi_ready, 1)
            for s_ in range(S_OO, NS - 2):
                split_hi(s_ + 2)
            row_squares(2 * TB, 2 * TB)

        @block.vector
        def _(dve):
            chain = [0]

            def link(ins):
                chain[0] += 1
                ins.then_inc(dve_chain, 1)
                dve.wait_ge(dve_chain, chain[0])

            def scale_rows(t, count):
                dve.wait_ge(rstd_ready, count)
                nc.vector.tensor_scalar(oa[:, t, :], x_t[:, t, 0:512], rstd[:, t:t + 1], None, ALU.mult)
                nc.vector.tensor_scalar(ob[:, t, :], x_t[:, t, 512:], rstd[:, t:t + 1], None,
                                        ALU.mult).then_inc(normed, 1)

            def row_variance(t, n0):
                dve.wait_ge(half_squares, n0 + t + 1)
                link(nc.vector.tensor_scalar(stat[:, t:t + 1], half_sq[:, t:t + 1], 1.0 / D, EPS, ALU.mult, ALU.add))
                dve.wait_ge(half_squares, n0 + TB + t + 1)
                nc.vector.scalar_tensor_tensor(out=stat[:, t:t + 1], in0=half_sq[:, TB + t:TB + t + 1], scalar=1.0 / D,
                                               in1=stat[:, t:t + 1], op0=ALU.mult, op1=ALU.add).then_inc(var_ready, 1)

            def hT_low(rnd, order, bank_of, scale):
                for n, c in enumerate(order):
                    dve.wait_ge(hT_hi_ready, KC * rnd + n + 1)
                    nc.vector.scalar_tensor_tensor(
                        out=hT_lo[:, c, :], in0=bank[bank_of(n)][:], scalar=scale(c),
                        in1=hT_hi[:, c, :].bitcast(F32), op0=ALU.mult, op1=ALU.subtract).then_inc(hT_ready, 1)

            dve.wait_ge(params_T, 2)
            nc.vector.tensor_copy(pvec[:], bank[0][:, 0:KC * NROW].rearrange(
                "p (c r) -> p c r", c=KC)).then_inc(pvec_ready, 1)
            nc.vector.tensor_copy(pb3[:, 0:3], bank[1][:, 0:3]).then_inc(pvec_ready, 1)
            for t in range(TB + 1):
                if t < TB:
                    dve.wait_ge(squares, t + 1)
                    nc.vector.tensor_scalar(stat[:, t:t + 1], stat[:, t:t + 1], 1.0 / D, EPS, ALU.mult,
                                            ALU.add).then_inc(var_ready, 1)
                if t:
                    scale_rows(t - 1, t)
            dve.wait_ge(pvec_ready, 2)
            hT_low(0, range(KC), lambda n: n, lambda c: pvec[:, c, ROW_NE:ROW_NE + 1])
            dve.wait_ge(rel_in, 16)
            starts = bucket_starts() + [S]
            for b in range(NB):
                lo_d, hi_d = starts[b], starts[b + 1]
                last = nc.vector.tensor_copy(bias_rev[:, S - hi_d:S - lo_d],
                                             rel_rows[:, b:b + 1].to_broadcast([AH, hi_d - lo_d]))
            link(last)
            nc.vector.memset(bias_rev[:, S:S + P], 0.0).then_inc(rev_ready, 1)
            dve.wait_ge(pool_const, 6)
            nc.vector.tensor_tensor(ixor, iota_i, iota_p, ALU.bitwise_xor).then_inc(xor_ready, 1)
            dve.wait_ge(pool_const, 7)
            for lg in range(5):
                link(nc.vector.tensor_scalar(ishift, ixor_up, lg, None, ALU.logical_shift_right))
                link(nc.vector.tensor_scalar(level_mask[:, lg, :], ishift, 1, None, ALU.is_equal))
            nc.vector.tensor_copy(level_mask[:, 5, :], ident[:]).then_inc(masks_ready, 1)

            for i in range(2):
                dve.wait_ge(z_done, i + 1)
                nc.vector.tensor_scalar(lin[0][:, S * i:S * i + S], bank[7][:], pb3[:, i:i + 1], None,
                                        ALU.add).then_inc(z_added, 1)
            dve.wait_ge(wi_ready, 1)
            n = 0
            for tb in (1, 2, 3):
                w = P * (tb + 1)
                for h in range(IH):
                    dve.wait_ge(relu_ready, n + 1)
                    if h == 0:
                        ins = nc.vector.tensor_scalar(score[tb], relu_b[n % 4][:, 0:w], wi[:, tb, 0:1], None, ALU.mult)
                    else:
                        dve.wait_ge(score_step, n)
                        ins = nc.vector.scalar_tensor_tensor(out=score[tb], in0=relu_b[n % 4][:, 0:w],
                                                             scalar=wi[:, tb, h:h + 1], in1=score[tb],
                                                             op0=ALU.mult, op1=ALU.add)
                    ins.then_inc(score_step, 1)
                    n += 1
            dve.wait_ge(softplus, 1)
            link(nc.vector.scalar_tensor_tensor(out=lin[2], in0=lin[0], scalar=0.0, in1=lin[1], op0=ALU.min,
                                                op1=ALU.subtract))
            for b in range(8):
                ins = nc.vector.tensor_tensor_scan(bsum[:, P * b:P * b + P], ones[:], lin[2][:, P * b:P * b + P],
                                                   0.0, ALU.mult, ALU.add)
            ins.then_inc(bsum_ready, 1)

            dve.wait_ge(causal_ready, 3)
            n = 0
            for r in range(TOPK // 8):
                for step in range(2):
                    for tb in (1, 2, 3):
                        if n >= 3:
                            dve.wait_ge(topk_step, n - 2)
                        if step == 0:
                            ins = nc.vector.max(top8[:, tb - 1, :], score[tb])
                        else:
                            ins = nc.vector.match_replace(score[tb], top8[:, tb - 1, :], score[tb], TAKEN)
                        ins.then_inc(topk_step, 1)
                        n += 1
            dve.wait_ge(topk_step, n)
            for tb in (1, 2, 3):
                w = P * (tb + 1)
                nc.vector.tensor_scalar(neg_mask[:, MASK_AT[tb]:MASK_AT[tb] + w], score[tb],
                                        0.5 * (HIDDEN + TAKEN), NEG, ALU.is_gt, ALU.mult).then_inc(mask_ready, 1)

            dve.wait_ge(exp_ready, 1)
            link(nc.vector.tensor_copy(chunk_decay[:], q_dec.rearrange("p (i t c) -> p i t c", i=2, c=P)[:, :, :, P - 1]))
            nc.vector.tensor_tensor(q_dec, q_dec, qbT, ALU.mult).then_inc(operand_ready, 1)

            def operand(it):
                n = ITEM_NO[it]
                dve.wait_ge(exp_ready, n + 2)
                v = lin[n % 4]
                if it == "k":
                    nc.vector.tensor_tensor(v, v, kbT, ALU.mult).then_inc(operand_ready, 1)
                    return
                vv, kv, qv = (a.rearrange("p (b c) -> p b c", c=2 * it) for a in (v, kbT, qbT))
                nc.vector.tensor_tensor(vv[:, :, 0:it], vv[:, :, 0:it], kv[:, :, 0:it], ALU.mult)
                nc.vector.tensor_tensor(vv[:, :, it:], vv[:, :, it:], qv[:, :, it:],
                                        ALU.mult).then_inc(operand_ready, 1)

            def empty_fill(f):
                n = FILL_NO[f]
                b = bank[4 + n % 4]
                dve.wait_ge(fill_done, n + 1)
                if f in ("k0", "k1"):
                    w = 2 if f == "k0" else 1
                    t0 = 0 if f == "k0" else 2
                    nc.vector.tensor_copy(k_rows[:, t0:t0 + w, :], b[:, 0:256 * w].rearrange(
                        "p (t c) -> p t c", t=w)).then_inc(fill_emptied, 1)
                    return
                if isinstance(f, tuple):
                    lv, h = f
                    a = attn[:, TB * h:TB * h + TB, :]
                    v = b[:].rearrange("p (t i) -> p t i", t=TB)
                    dve.wait_ge(att_zero, 1)
                    if lv >= 32:
                        for p0 in range(0, P, 2 * lv):
                            ins = nc.vector.tensor_copy(a[p0:p0 + lv, :, p0 + lv:p0 + 2 * lv],
                                                        v[p0:p0 + lv, :, p0 + lv:p0 + 2 * lv])
                    else:
                        lg = {16: 4, 8: 3, 4: 2, 2: 1, 1: 0, 0: 5}[lv]
                        m = level_mask[:, lg:lg + 1, :].to_broadcast([P, TB, P])
                        ins = nc.vector.copy_predicated(a, m, v)
                    ins.then_inc(fill_emptied, 1)
                    return
                t = int(f[2])
                if f[:2] == "kv":
                    if t == 0:
                        nc.vector.tensor_copy(state[:, 1, :], b[:, 0:256]).then_inc(fill_emptied, 1)
                        return
                    dve.wait_ge(fill_emptied, n)
                    for i in range(2):
                        ins = nc.vector.scalar_tensor_tensor(
                            out=state[:, t + 1, DV * i:DV * i + DV], in0=state[:, t, DV * i:DV * i + DV],
                            scalar=chunk_decay[:, i, t:t + 1], in1=b[:, DV * i:DV * i + DV], op0=ALU.mult, op1=ALU.add)
                    ins.then_inc(fill_emptied, 1)
                    return
                par = int(f[3])
                nc.vector.tensor_copy(ob[:, t, :].rearrange("p (i r e) -> p i r e", i=2, r=2)[:, :, par, :],
                                      b[:, 0:2 * DV].rearrange("p (i e) -> p i e", i=2)).then_inc(fill_emptied, 1)

            operand("k")
            operand(64)
            for f in ("k0", "k1"):
                empty_fill(f)
            for s_ in range(7, 11):
                for it in ITEM_STEP[s_]:
                    for h in range(BH):
                        empty_fill((it, h))
                for it in ITEM_STEP.get(s_ + 1, []):
                    operand(it)
            for f in FILLS[FILL_NO[(0, 0)]:]:
                empty_fill(f)
            for t in range(TB):
                dve.wait_ge(ob_squared, t + 1)
                nc.vector.tensor_reduce(stat[:, 4 * t:4 * t + 4], sq_b[t % 2].rearrange("p (h e) -> p h e", h=BH),
                                        AX.X, ALU.add).then_inc(ob_summed, 1)
            def logits(n):
                tb, h = divmod(n, AH)
                w = P * (tb + 1)
                dve.wait_ge(qk_done, n + 1)
                if n >= 2:
                    dve.wait_ge(prob_ready, n - 1)
                nc.vector.tensor_tensor_reduce(out=logit[n % 2][:, 0:w], in0=bank[4 + n % 2][:, 0:w],
                                               in1=bias_tab[:, h, S - w:S], scale=1.0, scalar=-3.0e38, op0=ALU.add,
                                               op1=ALU.max, accum_out=row_max[:, n:n + 1]).then_inc(logit_ready, 1)
                dve.wait_ge(logit_ready, n + 1)
                nc.vector.tensor_scalar(neg_max[:, n:n + 1], row_max[:, n:n + 1], -1.0, None,
                                        ALU.mult).then_inc(max_ready, 1)

            def empty_oa(tb):
                dve.wait_ge(pv_done, AH * (tb + 1))
                link(nc.vector.reciprocal(row_inv[:, AH * tb:AH * tb + AH], row_sum[:, AH * tb:AH * tb + AH]))
                inv = row_inv[:, AH * tb:AH * tb + AH].unsqueeze(2).to_broadcast([P, AH, AD])
                nc.vector.tensor_tensor(oa[:, tb, :].rearrange("p (h d) -> p h d", h=AH),
                                        bank[7][:].rearrange("p (h d) -> p h d", h=AH), inv,
                                        ALU.mult).then_inc(oa_emptied, 1)

            dve.wait_ge(table_in, 16 * AH)
            logits(0)
            for n in range(NSTEP):
                if n + 1 < NSTEP:
                    logits(n + 1)
                w = P * (n // AH + 1)
                dve.wait_ge(probT_done, n + 1)
                if n >= 2:
                    dve.wait_ge(pv_done, n - 1)
                nc.vector.tensor_copy(probT[n % 2][:, 0:w], bank[6][:, 0:w]).then_inc(probT_ready, 1)
                if n % AH == 0 and n:
                    empty_oa(n // AH - 1)
                if n == 2:
                    dve.wait_ge(ob_summed, TB)
                    nc.vector.tensor_scalar(stat[:], stat[:], 1.0 / DV, EPS, ALU.mult, ALU.add).then_inc(ob_var, 1)
                if n == 20:
                    dve.wait_ge(gates_silu, 1)
                    nc.vector.tensor_tensor(r_ob[:], r_ob[:], r_vb[:], ALU.mult).then_inc(mixed_b, 1)
                if n == 6:
                    dve.wait_ge(ob_rstd, 1)
                    g16 = r_ob[:].rearrange("p (g e) -> p g e", e=DV)
                    link(nc.vector.tensor_tensor(g16, g16, rstd[:].unsqueeze(2).to_broadcast([P, 16, DV]), ALU.mult))
            dve.wait_ge(gates_silu, 2)
            dve.wait_ge(oa_emptied, TB - 1)
            nc.vector.tensor_tensor(oa[:, 0:TB - 1, :], oa[:, 0:TB - 1, :], gate_a[:, 0:TB - 1, :],
                                    ALU.mult).then_inc(mixed_a, 1)
            empty_oa(TB - 1)
            dve.wait_ge(oa_emptied, TB)
            dve.wait_ge(act_emptied, evacs_through(FIRST[S_GA] + TB - 1, "act"))
            nc.vector.tensor_tensor(oa[:, TB - 1, :], oa[:, TB - 1, :], gate_a[:, TB - 1, :],
                                    ALU.mult).then_inc(mixed_a, 1)
            hT_low(1, B_FIRST, lambda n: n, lambda c: 1.0 if c < 4 else pb3[:, 2:3])

            def residual(s0, variance, scaled_rows):
                for half in range(2):
                    for t in range(TB):
                        g = FIRST[s0 + 2 * half] + t
                        dve.wait_ge(group_done, g + 1)
                        xs = x_t[:, t, 512 * half:512 * half + 512]
                        nc.vector.tensor_tensor(xs, bank[g % 4][:], xs, ALU.add).then_inc(dve_emptied, 1)
                        if half and t:
                            variance(t - 1)
                            scaled_rows(t - 1)
                variance(TB - 1)
                scaled_rows(TB - 1)

            dve.wait_ge(x_again, 16)
            residual(S_OE, lambda t: row_variance(t, 0), lambda t: scale_rows(t, TB + t + 1))
            hT_low(2, range(KC), lambda n: 4 + n % 4, lambda c: pvec[:, c, ROW_NO:ROW_NO + 1])

            for i in range(3):
                ins = nc.vector.memset(upad[i][:, 0:CW - 1], 0.0)
            link(ins)
            chunk_slots = sorted(CHUNK, key=lambda j: CHUNK[j])

            def glu(c):
                g = FIRST[chunk_slots[c]]
                dve.wait_ge(act_emptied, evacs_through(g + 1, "act"))
                nc.vector.tensor_tensor(upad[c % 3][:, CW - 1:PADW], bank[g % 4][:], sgl[c % 2],
                                        ALU.mult).then_inc(u_ready, 1)

            FIRST_TAP = PE_TAPS + POOL_TAPS
            taps = list(range(FIRST_TAP, CW))
            n_first = (len(taps) + 1) // 2
            tap_no = {}
            count = [0]

            def tap(c, i):
                acc = bank[4 + c % 3][:]
                k = taps[i]
                if i == 0:
                    dve.wait_ge(taps_done, c + 1)
                else:
                    dve.wait_ge(tap_step, tap_no[c, i - 1])
                nc.vector.scalar_tensor_tensor(
                    out=acc if i < len(taps) - 1 else conv_y(c), in0=upad[c % 3][:, k:k + S],
                    scalar=pvec[:, c, k:k + 1], in1=acc, op0=ALU.mult,
                    op1=ALU.add).then_inc(tap_step if i < len(taps) - 1 else dve_taps_done, 1)
                if i < len(taps) - 1:
                    count[0] += 1
                    tap_no[c, i] = count[0]

            glu(0)
            for c in range(KC + 1):
                for i in range(n_first):
                    if c < KC:
                        tap(c, i)
                    if c and n_first + i < len(taps):
                        tap(c - 1, n_first + i)
                    if i == n_first // 2 and c + 1 < KC:
                        glu(c + 1)
            dve.wait_ge(mean_done, 1)
            for c in range(KC):
                nc.vector.scalar_tensor_tensor(out=conv_y(c), in0=bank[7][:], scalar=-1.0 / D, in1=conv_y(c),
                                               op0=ALU.mult, op1=ALU.add).then_inc(centred, 1)
            dve.wait_ge(lnvar_done, 1)
            nc.vector.tensor_scalar(ln_var[:], bank[4][:, 0:TB], 1.0 / D, EPS, ALU.mult, ALU.add).then_inc(lnvar_ready, 1)
            dve.wait_ge(lnrstd_ready, 1)
            for t in range(TB):
                ins = nc.vector.tensor_scalar(ln_diag[:, P * t:P * t + P], ident[:], rstd[:, t:t + 1], None, ALU.mult)
            ins.then_inc(lndiag_ready, 1)
            dve.wait_ge(lnrstd_wide, 1)
            dve.wait_ge(gates_silu, 4)
            wait_slot_used(dve, S_OO - 1)
            for c in range(KC + 1):
                if c < KC:
                    nc.vector.tensor_tensor(conv_y(c), conv_y(c), bank[5][:], ALU.mult).then_inc(scaled, 1)
                if c >= 1:
                    dve.wait_ge(ln_silu, c)
                    if c >= 5:
                        dve.wait_ge(hT_ready, 3 * KC + c - 4)
                    nc.vector.tensor_tensor(m_f32[(c - 1) % 4], conv_y(c - 1), gate_s(c - 1), ALU.mult).then_inc(m_ready, 1)
            dve.wait_ge(nf_in, 16)

            def final_rows(t):
                dve.wait_ge(rstd_ready, 2 * TB + t + 1)
                for half in range(2):
                    cols = slice(512 * half, 512 * half + 512)
                    nc.vector.scalar_tensor_tensor(out=x_t[:, t, cols], in0=x_t[:, t, cols], scalar=rstd[:, t:t + 1],
                                                   in1=nf_row[:, cols], op0=ALU.mult, op1=ALU.mult).then_inc(y_ready, 1)

            residual(S_OO, lambda t: row_variance(t, 2 * TB), final_rows)

        @block.tensor
        def _(pe):
            pe.wait_ge(pool_chain, 2)
            pe.wait_ge(params_in, 16 * 9)
            for c in range(KC):
                ins = nc.tensor.transpose(bank[0][:, NROW * c:NROW * c + NROW], param_rows[0:NROW, P * c:P * c + P],
                                          ident[0:NROW, 0:NROW])
            ins.then_inc(params_T, 1)
            nc.tensor.transpose(bank[1][:, 0:3], small_rows[:], ident[0:3, 0:3]).then_inc(params_T, 1)

            def transpose_rows(rnd, order, ready, bank_of, reuse):
                for first in (0, 4):
                    for t in range(TB):
                        for n in range(first, first + 4):
                            ready(n, t)
                            if t == 0 and n >= 4 and reuse:
                                pe.wait_ge(hT_ready, KC * rnd + n - 3)
                            ins = nc.tensor.transpose(bank[bank_of(n)][:, P * t:P * t + P], hx(t, order[n]), ident[:])
                            if t == TB - 1:
                                ins.then_inc(hT_in_bank, 1)

            pe.wait_ge(pvec_ready, 2)
            transpose_rows(0, range(KC), lambda n, t: pe.wait_ge(normed, t + 1), lambda n: n, False)

            def bank_free(g):
                if g < 4:
                    pe.wait_ge(hT_ready, g + 1)
                    return
                if evac_by[g - 4] == "act":
                    pe.wait_ge(act_emptied, evacs_through(g - 4, "act"))
                elif evac_by[g - 4] == "val":
                    pe.wait_ge(u_ready, evacs_through(g - 4, "val"))
                else:
                    pe.wait_ge(dve_emptied, evacs_through(g - 4, "residual"))

            def slot_ready(j):
                pe.wait_ge(lo_ready, j + 1)

            def group_a(j, i, hT_round=None):
                g = FIRST[j] + i
                bank_free(g)
                m = 128 if j != 1 or i == 0 else RANK + IH
                wh = w_hi[j % 3][:].rearrange("p (k n) -> p k n", k=KC)
                wl = w_lo[j % 3][:].rearrange("p (k n) -> p k n", k=KC)
                for k in range(KC):
                    if hT_round is not None:
                        pe.wait_ge(hT_ready, KC * hT_round + k + 1)
                    for q, (w, h) in enumerate(((wh, hT_hi), (wh, hT_lo), (wl, hT_hi))):
                        ins = nc.tensor.matmul(bank[g % 4][0:m, :], w[:, k, P * i:P * i + m], h[:, k, :],
                                               start=(k == 0 and q == 0), stop=(k == KC - 1 and q == 2))
                ins.then_inc(group_done, 1)

            def unit_b(j, t, part=(0, 4), hT_round=None):
                g = FIRST[j] + t
                ks = SLOTS[j][1]
                first, final = j % 2 == 0, j % 2 == 1
                if first and part[0] == 0:
                    bank_free(g)
                wh = w_hi[j % 3][:].rearrange("p (k n) -> p k n", k=4)
                wl = w_lo[j % 3][:].rearrange("p (k n) -> p k n", k=4)
                for i in range(*part):
                    k = ks[i]
                    if hT_round is not None:
                        pe.wait_ge(hT_ready, KC * hT_round + (i if first else 4 + i) + 1)
                    for q, (h, w) in enumerate(((hT_hi, wh), (hT_hi, wl), (hT_lo, wh))):
                        ins = nc.tensor.matmul(bank[g % 4][:], h[:, k, P * t:P * t + P], w[:, i, :],
                                               start=(first and i == 0 and q == 0), stop=(final and i == 3 and q == 2))
                if part[1] == 4:
                    if final:
                        ins.then_inc(group_done, 1)
                    elif t == TB - 1:
                        ins.then_inc(half_used, 1)

            slot_ready(0)
            group_a(0, 0, hT_round=0)
            group_a(0, 1)
            slot_ready(1)
            group_a(1, 0)
            group_a(1, 1)
            slot_ready(2)
            group_a(2, 0)
            pe.wait_ge(act_emptied, 4)
            pe.wait_ge(hT_ready, KC)
            for t in range(TB):
                ins = nc.tensor.transpose(bank[6][:, (RANK + IH) * t:(RANK + IH) * (t + 1)], lwT[:, P * t:P * t + P],
                                          ident[0:RANK + IH, 0:RANK + IH])
            ins.then_inc(wi_T, 1)
            nc.tensor.matmul(bank[7][:], w_lr[:, 0:P], lwT[0:RANK, :], start=True, stop=True).then_inc(z_done, 1)
            n = 0
            for tb in (1, 2, 3):
                for h in range(IH):
                    if n >= 2:
                        pe.wait_ge(relu_ready, n - 1)
                    p0 = 64 * (h % 2)
                    nc.tensor.matmul(bank[4 + n % 2][:, 0:P * (tb + 1)], qiT[p0:p0 + 64, h // 2, P * tb:P * tb + P],
                                     kiT[p0:p0 + 64, 0:P * (tb + 1)], start=True, stop=True).then_inc(idx_done, 1)
                    n += 1
                if tb == 1:
                    pe.wait_ge(z_added, 1)
                    nc.tensor.matmul(bank[7][:], w_lr[:, P:2 * P], lwT[0:RANK, :], start=True,
                                     stop=True).then_inc(z_done, 1)
            group_a(2, 1)

            def fill(f):
                n = FILL_NO[f]
                b = bank[4 + n % 4]
                if n >= 4:
                    pe.wait_ge(fill_emptied, n - 3)
                if f in ("k0", "k1"):
                    if f == "k0":
                        pe.wait_ge(operand_ready, ITEM_NO["k"] + 2)
                        pe.wait_ge(wi_ready, 1)
                        pe.wait_ge(z_added, 2)
                        pe.wait_ge(relu_ready, 12)
                    for a, t in enumerate((0, 1) if f == "k0" else (2,)):
                        for i in range(2):
                            ins = nc.tensor.transpose(b[:, 256 * a + P * i:256 * a + P * i + P],
                                                      lin[0][:, S * i + P * t:S * i + P * t + P], ident[:])
                    ins.then_inc(fill_done, 1)
                    return
                if isinstance(f, tuple):
                    lv, h = f
                    if h == 0 and lv:
                        pe.wait_ge(operand_ready, ITEM_NO[lv] + 2)
                    p0, at = 64 * (h % 2), S * (h // 2)
                    kk = lin[ITEM_NO[lv] % 4] if lv else kbT
                    qq = lin[ITEM_NO[lv] % 4] if lv else qbT
                    for t in range(TB):
                        cols = slice(at + P * t, at + P * t + P)
                        ins = nc.tensor.matmul(b[:, P * t:P * t + P], kk[p0:p0 + 64, cols], qq[p0:p0 + 64, cols],
                                               start=True, stop=True)
                    ins.then_inc(fill_done, 1)
                    return
                t = int(f[2])
                if f[:2] == "kv":
                    for h in range(BH):
                        p0 = 64 * (h % 2)
                        ins = nc.tensor.matmul(b[p0:p0 + 64, DV * (h // 2):DV * (h // 2) + DV],
                                               k_rows[:, t, 64 * h:64 * h + 64], vb[:, t, DV * h:DV * h + DV],
                                               start=True, stop=True)
                    ins.then_inc(fill_done, 1)
                    return
                pe.wait_ge(fill_emptied, FILL_NO["kv0"] if t == 0 else FILL_NO[f"kv{t - 1}"] + 1)
                pe.wait_ge(fill_emptied, FILL_NO[(0, BH - 1)] + 1)
                for h in (int(f[3]), int(f[3]) + 2):
                    p0 = 64 * (h % 2)
                    o = b[:, DV * (h // 2):DV * (h // 2) + DV]
                    ins = nc.tensor.matmul(o, attn[:, TB * h + t, :], vb[:, t, DV * h:DV * h + DV], start=True,
                                           stop=(t == 0))
                    if t:
                        ins = nc.tensor.matmul(o, q_dec[p0:p0 + 64, S * (h // 2) + P * t:S * (h // 2) + P * t + P],
                                               state[p0:p0 + 64, t, DV * (h // 2):DV * (h // 2) + DV],
                                               start=False, stop=True)
                ins.then_inc(fill_done, 1)

            def fills(s_, half):
                for f in FILL_AT.get((s_, half), []):
                    fill(f)

            def qk(n):
                tb, h = divmod(n, AH)
                w, p0 = P * (tb + 1), 64 * (h % 2)
                if n == 0:
                    pe.wait_ge(fill_emptied, len(FILLS))
                    pe.wait_ge(act_emptied, evacs_through(FIRST[S_VA] - 1, "act"))
                if n >= 2:
                    pe.wait_ge(logit_ready, n - 1)
                b = bank[4 + n % 2][:, 0:w]
                nc.tensor.matmul(b, qaT[p0:p0 + 64, h // 2, P * tb:P * tb + P], kaT[p0:p0 + 64, h // 2, 0:w],
                                 start=True, stop=False)
                if tb and h == 0:
                    pe.wait_ge(mask_ready, tb)
                nc.tensor.matmul(b, ident_bf[:], neg_mask[:, MASK_AT[tb]:MASK_AT[tb] + w], start=False,
                                 stop=True).then_inc(qk_done, 1)

            def prob_transpose(n):
                tb = n // AH
                pe.wait_ge(prob_ready, n + 1)
                if n >= 1:
                    pe.wait_ge(probT_ready, n)
                for i in range(tb + 1):
                    ins = nc.tensor.transpose(bank[6][:, P * i:P * i + P], prob[n % 2][:, P * i:P * i + P], ident[:])
                ins.then_inc(probT_done, 1)

            def pv(n):
                tb, h = divmod(n, AH)
                pe.wait_ge(probT_ready, n + 1)
                if n == 0:
                    pe.wait_ge(act_emptied, evacs_through(FIRST[S_VA] + 3, "act"))
                if h == 0 and tb:
                    pe.wait_ge(oa_emptied, tb)
                for i in range(tb + 1):
                    ins = nc.tensor.matmul(bank[7][:, AD * h:AD * h + AD], probT[n % 2][:, P * i:P * i + P],
                                           va[:, i, AD * h:AD * h + AD], start=(i == 0), stop=(i == tb))
                ins.then_inc(pv_done, 1)

            for s_ in range(3, S_OE):
                slot_ready(s_)
                if SLOTS[s_][0] == "a":
                    for half in range(2):
                        group_a(s_, half)
                        fills(s_, half)
                elif s_ < ATT_S0:
                    for half in range(2):
                        unit_b(s_, 2 * half)
                        unit_b(s_, 2 * half + 1)
                        fills(s_, half)
                    if s_ == ATT_S0 - 1:
                        qk(0)
                else:
                    for t in range(TB):
                        for half in range(2):
                            n = AH * (s_ - ATT_S0) + 2 * t + half
                            if n + 1 < NSTEP:
                                qk(n + 1)
                            unit_b(s_, t, part=(2 * half, 2 * half + 2))
                            prob_transpose(n)
                            if n:
                                pv(n - 1)
            pv(NSTEP - 1)
            pe.wait_ge(act_emptied, evacs_through(FIRST[S_OE] - 1, "act"))
            pe.wait_ge(mixed_b, 1)

            def rows_mixed(n, t):
                if n >= 4:
                    pe.wait_ge(mixed_a, 1 if t < TB - 1 else 2)
                if n == 7:
                    pe.wait_ge(oa_emptied, TB)

            transpose_rows(1, B_FIRST, rows_mixed, lambda n: n, False)
            for s_ in range(S_OE, S_ODD):
                slot_ready(s_)
                for t in range(TB):
                    unit_b(s_, t, hT_round=1 if s_ < S_OE + 2 and t == 0 else None)
            transpose_rows(2, range(KC), lambda n, t: pe.wait_ge(normed, TB + t + 1), lambda n: 4 + n % 4, True)

            def pe_taps(c):
                pe.wait_ge(diag_ready, PE_TAPS * (c + 1))
                pe.wait_ge(u_ready, c + 1)
                if c >= 3:
                    pe.wait_ge(dve_taps_done, c - 2)
                for k in range(PE_TAPS):
                    ins = nc.tensor.matmul(bank[4 + c % 3][:], tap_diag[c % 2][k], upad[c % 3][:, k:k + S],
                                           start=(k == 0), stop=(k == PE_TAPS - 1))
                ins.then_inc(taps_done, 1)

            def ln_sum(c):
                pe.wait_ge(conv_done, c + 1)
                ins = nc.tensor.matmul(bank[7][:], ones[:], conv_y(c), start=(c == 0), stop=(c == KC - 1))
                if c == KC - 1:
                    ins.then_inc(mean_done, 1)

            for s_ in range(S_ODD, S_OO):
                slot_ready(s_)
                group_a(s_, 0, hT_round=2 if s_ == S_ODD else None)
                if s_ in CHUNK and CHUNK[s_]:
                    pe_taps(CHUNK[s_] - 1)
                if s_ == S_OO - 1:
                    pe_taps(KC - 1)
                    for c in range(KC):
                        ln_sum(c)
                group_a(s_, 1)
            for c in range(KC):
                pe.wait_ge(lnsq_ready, c + 1)
                for t in range(TB):
                    ins = nc.tensor.matmul(bank[4][:, t:t + 1], ln_sq[c % 2][:, P * t:P * t + P], ones[:, 0:1],
                                           start=(c == 0 and t == 0), stop=(c == KC - 1), skip_group_check=True)
                ins.then_inc(lnsq_used if c < KC - 1 else lnvar_done, 1)
            pe.wait_ge(lndiag_ready, 1)
            for t in range(TB):
                ins = nc.tensor.matmul(bank[5][:, P * t:P * t + P], ones[:], ln_diag[:, P * t:P * t + P],
                                       start=True, stop=True)
            ins.then_inc(lnrstd_wide, 1)
            for s_ in range(S_OO, NS):
                slot_ready(s_)
                for t in range(TB):
                    unit_b(s_, t, hT_round=3 if s_ < S_OO + 2 and t == 0 else None)


_INS = ["x", "rel_bias", "norm_even", "w_in_even", "w_gla_lr", "b_gla_lr", "gla_norm", "w_out_even", "norm_odd",
        "w_in_odd", "conv_w", "conv_b", "conv_ln_g", "conv_ln_b", "w_out_odd", "norm_f"]
_OUTS = [((1, 512, 1024), "float32")]


def kernel(**inputs):
    import numpy as _np
    import concourse.bacc as _bacc
    from concourse import mybir as _mybir
    from concourse.bass_utils import run_bass_kernel_spmd as _run

    nc = _bacc.Bacc("TRN2", target_bir_lowering=False, num_devices=1)
    arrays, args = {}, []
    for name in _INS:
        a = _np.ascontiguousarray(inputs[name])
        arrays[f"in_{name}_dram"] = a
        args.append(nc.dram_tensor(f"in_{name}_dram", a.shape, _mybir.dt.from_np(a.dtype), kind="ExternalInput").ap())
    for i, (shape, dtype) in enumerate(_OUTS):
        dt = _mybir.dt.from_np(_np.dtype(dtype))
        args.append(nc.dram_tensor(f"out_{i}_dram", shape, dt, kind="ExternalOutput").ap())
    hybrid_trunk(nc, *args)
    r = _run(nc, [arrays], core_ids=[0])
    return r.results[0]["out_0_dram"]
```

```python
from contextlib import ExitStack

import concourse.bass as bass
from concourse import mybir

F32 = mybir.dt.float32
F32R = mybir.dt.float32r
BF16 = mybir.dt.bfloat16
I32 = mybir.dt.int32
U8 = mybir.dt.uint8
ALU = mybir.AluOpType
ACT = mybir.ActivationFunctionType
AX = mybir.AxisListType

P = 128
D = 1024
S = 512
KC = D // P
TB = S // P
EPS = 1e-6
AH, AD = 8, 64
IH, ID = 4, 64
BH, DK, DV = 4, 64, 128
RANK = 16
TAU = 16.0
TOPK = min(256, S // 4)
CW = 31
NB, MAXEX, MAXD = 32, 16, 128
PE_TAPS, POOL_TAPS = 4, 5
WARM_START, WARM_LN = 30, 40
NEG = -1.0e30
HIDDEN = -2.0e38
TAKEN = -3.0e38

C_QA, C_KA, C_VA, C_GA = 0, 512, 1024, 1536
C_QI = 2048
C_KI = C_QI + IH * ID
C_WI = C_KI + ID
C_QB = C_WI + IH
C_KB = C_QB + BH * DK
C_VB = C_KB + BH * DK
C_GB = C_VB + BH * DV
C_LR = C_GB + BH * DV
M_KI = ID + RANK + IH


B_FIRST = (4, 5, 6, 7, 0, 1, 2, 3)


def bucket_starts():
    import math
    first = {}
    for d in range(S):
        if d < MAXEX:
            b = d
        else:
            b = min(NB - 1, MAXEX + int(math.log(d / MAXEX) / math.log(MAXD / MAXEX) * (NB - MAXEX) + 1e-6))
        first.setdefault(b, d)
    return [first[b] for b in range(NB)]


def plan_slots():
    a = lambda m, c: ("a", (0,), [(0, m, c, 256)])
    b = lambda m, c, ks: [("b", ks[0:4], [(0, m, c, 512)]), ("b", ks[4:8], [(0, m, c, 512)])]
    up = tuple(range(KC))
    s = [a("e", C_QI),
         ("a", (0,), [(0, "e", C_KI, ID), (ID, "e", C_LR, RANK), (ID + RANK, "e", C_WI, IH)]),
         a("e", C_QB), a("e", C_KB)]
    s += b("e", C_VB, up)
    s += [a("e", C_QA), a("e", C_QA + 256), a("e", C_KA), a("e", C_KA + 256)]
    s += b("e", C_VA, up) + b("e", C_GB, up) + b("e", C_GA, up)
    s += b("oe", 0, B_FIRST) + b("oe", 512, B_FIRST)
    vg = lambda c: ("a", (0,), [(0, "o", c * P, P), (P, "o", D + c * P, P)])
    gate = lambda n: a("o", 2 * D + n * 256)
    s += [vg(c) for c in range(KC)] + [gate(n) for n in range(4)]
    s += b("oo", 0, up) + b("oo", 512, up)
    return s


def hybrid_trunk(nc, x, rel_bias, norm_even, w_in_even, w_gla_lr, b_gla_lr, gla_norm, w_out_even,
                 norm_odd, w_in_odd, conv_w, conv_b, conv_ln_g, conv_ln_b, w_out_odd, norm_f, out):
    SLOTS = plan_slots()
    NS = len(SLOTS)
    WSRC = {"e": w_in_even[0], "oe": w_out_even[0], "o": w_in_odd[0], "oo": w_out_odd[0]}
    S_VB, S_QA, S_KA, S_VA, S_GB, S_GA, S_OE, S_ODD, S_OO = 4, 6, 8, 10, 12, 14, 16, 20, 32
    FIRST, evac_by = {}, []
    CHUNK, GATE = {}, {}
    for j, (kind, ks, pieces) in enumerate(SLOTS):
        if kind == "a":
            FIRST[j] = len(evac_by)
            if S_ODD <= j < S_OO:
                c0 = pieces[0][2]
                if c0 < D:
                    CHUNK[j] = c0 // P
                    evac_by += ["val", "act"]
                else:
                    GATE[j] = (c0 - 2 * D) // P
                    evac_by += ["act", "act"]
            else:
                evac_by += ["act"] if j == 1 else ["act", "act"]
        elif j % 2 == 0:
            FIRST[j] = FIRST[j + 1] = len(evac_by)
            evac_by += ["residual" if j >= S_OE else "act"] * TB

    def evacs_through(g, who):
        return sum(1 for e in evac_by[:g + 1] if e == who)

    raw_full, n_in = {}, [0, 0]
    for j, (_, ks, pieces) in enumerate(SLOTS):
        n_in[j % 2] += 16 * len(pieces)
        raw_full[j] = n_in[j % 2]

    ctx = ExitStack()
    with ctx:
        def sb(name, shape, dt=F32):
            return ctx.enter_context(nc.sbuf_tensor(name, shape, dt))

        def sem(name):
            return ctx.enter_context(nc.semaphore(name))

        w_raw = [sb(f"w_raw{i}", [P, 2048]) for i in range(2)]
        w_hi = [sb(f"w_hi{i}", [P, 2048], F32R) for i in range(3)]
        w_lo = [sb(f"w_lo{i}", [P, 2048], F32R) for i in range(3)]
        hT_hi = sb("hT_hi", [P, KC, S], F32R)
        hT_lo = sb("hT_lo", [P, KC, S], F32R)
        r_x = sb("r_x", [P, 4096])
        r_oa = sb("r_oa", [P, 2048])
        r_ob = sb("r_ob", [P, 2048])
        r_qa = sb("r_qa", [P, 2048])
        r_ka = sb("r_ka", [P, 2048])
        r_va = sb("r_va", [P, 2048])
        r_vb = sb("r_vb", [P, 2048])
        r_qkb = sb("r_qkb", [P, 2048])
        r_g = sb("r_g", [P, 4096])
        r_att = sb("r_att", [P, 2048])
        neg_mask = sb("neg_mask", [P, 1280], BF16)
        ident = sb("ident", [P, P])
        ident_bf = sb("ident_bf", [P, P], BF16)
        ones = sb("ones", [P, P])
        level_mask = sb("level_mask", [P, 6, P], U8)
        NROW = CW + 5
        pvec = sb("pvec", [P, KC, NROW])
        pb3 = sb("pb3", [P, 4])
        small_rows = sb("small_rows", [3, P])
        rel_rows = sb("rel_rows", [AH, NB])
        w_lr = sb("w_lr", [ID + RANK, BH * DK])
        lwT = sb("lwT", [M_KI, S])
        wi = sb("wi", [P, TB, IH])
        stat = sb("stat", [P, 16])
        half_sq = sb("half_sq", [P, 2 * TB])
        ln_var = sb("ln_var", [P, TB])
        rstd = sb("rstd", [P, 16])
        minus_half = sb("minus_half", [P, 16])
        top8 = sb("top8", [P, 3, 8])
        row_max = sb("row_max", [P, TB * AH])
        neg_max = sb("neg_max", [P, TB * AH])
        row_sum = sb("row_sum", [P, TB * AH])
        row_inv = sb("row_inv", [P, TB * AH])
        chunk_decay = sb("chunk_decay", [P, 2, TB])
        state = sb("state", [P, TB, 2 * DV])

        x_t = r_x[:].rearrange("p (t d) -> p t d", t=TB)
        bias_tab = r_x[:].rearrange("p (h u) -> p h u", h=AH)
        oa = r_oa[:].rearrange("p (t d) -> p t d", t=TB)
        ob = r_ob[:].rearrange("p (t d) -> p t d", t=TB)
        qaT = r_qa[:].rearrange("p (c t) -> p c t", c=4)
        kaT = r_ka[:].rearrange("p (c t) -> p c t", c=4)
        va = r_va[:].rearrange("p (t d) -> p t d", t=TB)
        vb = r_vb[:].rearrange("p (t d) -> p t d", t=TB)
        qbT = r_qkb[:, 0:1024]
        kbT = r_qkb[:, 1024:2048]
        gate_a = r_qkb[:].rearrange("p (t d) -> p t d", t=TB)
        gate_b = vb
        qiT = r_qa[:, 0:1024].rearrange("p (c t) -> p c t", c=2)
        kiT = r_qa[:, 1024:1536]
        relu_b = [r_ka[:, 512 * i:512 * i + 512] for i in range(4)]
        score = {tb: r_va[:, o:o + P * (tb + 1)] for tb, o in ((1, 0), (2, 256), (3, 640))}
        MASK_AT = (0, 128, 384, 768)
        bsum = r_ob[:, 0:1024]
        lin = [r_g[:, 1024 * i:1024 * (i + 1)] for i in range(4)]
        q_dec = r_oa[:, 0:1024]
        k_rows = r_oa[:, 1024:1792].rearrange("p (t c) -> p t c", t=3)
        attn = r_att[:].rearrange("p (g i) -> p g i", g=BH * TB)
        param_rows = r_att[:, 0:D]
        junk = [r_att[:, D:2 * D], r_qkb[:, 0:D]]
        iota_i = r_vb[:, 0:128].bitcast(I32)
        iota_p = r_vb[:, 128:256].bitcast(I32)
        ixor = r_vb[:, 256:384].bitcast(I32)
        ixor_up = r_vb[:, 384:512].bitcast(I32)
        ishift = r_vb[:, 512:640].bitcast(I32)
        bias_rev = r_vb[0:AH, 1024:1664]
        logit = [r_g[:, 512 * i:512 * i + 512] for i in (0, 1)]
        prob = [r_g[:, 1024 + 512 * i:1536 + 512 * i] for i in (0, 1)]
        probT = [r_g[:, 2048 + 512 * i:2560 + 512 * i] for i in (0, 1)]
        sq_b = [r_att[:, 512 * i:512 * i + 512] for i in range(TB)]
        conv_y = lambda c: (r_oa if c < 4 else r_ob)[:, 512 * (c % 4):512 * (c % 4) + 512]
        PADW = S + CW - 1
        upad = [r_va[:, 576 * i:576 * i + PADW] for i in range(3)]
        sgl = [r_vb[:, 512 * i:512 * i + 512] for i in (0, 1)]
        m_f32 = [r_g[:, 512 * i:512 * i + 512] for i in range(KC)]
        prod = [r_g[:, 1024 + 512 * i:1536 + 512 * i] for i in range(3)]
        pool_acc = [r_g[:, 2560 + 512 * i:3072 + 512 * i] for i in range(3)]
        tap_diag = [[r_vb[:, 1024 + P * (PE_TAPS * i + k):1024 + P * (PE_TAPS * i + k + 1)]
                     for k in range(PE_TAPS)] for i in range(2)]
        ln_diag = r_vb[:, 1024:1024 + S]
        ln_sq = [(r_qkb if c < 4 else r_va)[:, 512 * (c % 4):512 * (c % 4) + 512] for c in range(KC)]
        gate_s = lambda c: (r_qa if c < 4 else r_ka)[:, 512 * (c % 4):512 * (c % 4) + 512]
        nf_row = r_att[:, 0:D]
        sq_junk = r_att[:, D:2 * D]
        ROW_NE, ROW_NO, ROW_CB, ROW_LG, ROW_LB = CW, CW + 1, CW + 2, CW + 3, CW + 4

        def hx(tb, c):
            return (oa if c < 4 else ob)[:, tb, P * (c % 4):P * (c % 4) + P]

        bank = [ctx.enter_context(nc.psum_tensor(f"bank{i}", [P, 512], F32)) for i in range(8)]

        x_in = [sem(f"x_in{t}") for t in range(TB)]
        params_in = sem("params_in")
        rel_in = sem("rel_in")
        raw_in = [sem(f"raw_in{i}") for i in range(2)]
        table_in = sem("table_in")
        x_again = sem("x_again")
        nf_in = sem("nf_in")
        out_done = sem("out_done")
        pool_const = sem("pool_const")
        pool_chain = sem("pool_chain")
        hi_ready = sem("hi_ready")
        lo_ready = sem("lo_ready")
        squares = sem("squares")
        half_squares = sem("half_squares")
        var_ready = sem("var_ready")
        rstd_ready = sem("rstd_ready")
        normed = sem("normed")
        params_T = sem("params_T")
        pvec_ready = sem("pvec_ready")
        rev_ready = sem("rev_ready")
        xor_ready = sem("xor_ready")
        hT_in_bank = sem("hT_in_bank")
        hT_hi_ready = sem("hT_hi_ready")
        hT_ready = sem("hT_ready")
        half_used = sem("half_used")
        group_done = sem("group_done")
        act_emptied = sem("act_emptied")
        dve_emptied = sem("dve_emptied")
        ki_ready = sem("ki_ready")
        ki_twice = sem("ki_twice")
        wi_T = sem("wi_T")
        wi_ready = sem("wi_ready")
        z_done = sem("z_done")
        z_added = sem("z_added")
        softplus = sem("softplus")
        bsum_ready = sem("bsum_ready")
        idx_done = sem("idx_done")
        relu_ready = sem("relu_ready")
        score_step = sem("score_step")
        masks_ready = sem("masks_ready")
        causal_ready = sem("causal_ready")
        mask_ready = sem("mask_ready")
        act_chain = sem("act_chain")
        dve_chain = sem("dve_chain")
        diff_ready = sem("diff_ready")
        exp_ready = sem("exp_ready")
        operand_ready = sem("operand_ready")
        fill_done = sem("fill_done")
        fill_emptied = sem("fill_emptied")
        ob_squared = sem("ob_squared")
        ob_summed = sem("ob_summed")
        ob_var = sem("ob_var")
        ob_rstd = sem("ob_rstd")
        att_zero = sem("att_zero")
        qk_done = sem("qk_done")
        logit_ready = sem("logit_ready")
        max_ready = sem("max_ready")
        prob_ready = sem("prob_ready")
        probT_done = sem("probT_done")
        probT_ready = sem("probT_ready")
        pv_done = sem("pv_done")
        oa_emptied = sem("oa_emptied")
        gates_silu = sem("gates_silu")
        u_ready = sem("u_ready")
        conv_done = sem("conv_done")
        mean_done = sem("mean_done")
        centred = sem("centred")
        lnsq_ready = sem("lnsq_ready")
        lnsq_paired = sem("lnsq_paired")
        lnvar_done = sem("lnvar_done")
        lnvar_ready = sem("lnvar_ready")
        lnrstd_ready = sem("lnrstd_ready")
        lndiag_ready = sem("lndiag_ready")
        lnrstd_wide = sem("lnrstd_wide")
        topk_step = sem("topk_step")
        diag_ready = sem("diag_ready")
        taps_done = sem("taps_done")
        prod_ready = sem("prod_ready")
        sum_begun = sem("sum_begun")
        pool_added = sem("pool_added")
        dve_taps_done = sem("dve_taps_done")
        tap_step = sem("tap_step")
        mixed_b = sem("mixed_b")
        mixed_a = sem("mixed_a")
        scaled = sem("scaled")
        ln_silu = sem("ln_silu")
        m_ready = sem("m_ready")
        m_low_dve = sem("m_low_dve")
        y_ready = sem("y_ready")

        LEVELS = [64, 32, 16, 8, 4, 2, 1]
        ITEMS = ["k"] + LEVELS
        ITEM_STEP = {6: ["k"], 7: [64], 8: [32, 16], 9: [8, 4], 10: [2, 1]}
        ITEM_NO = {it: n for n, it in enumerate(ITEMS)}
        FILLS = ["k0", "k1"] + [(lv, h) for lv in LEVELS for h in range(BH)] + [(0, h) for h in range(BH)]
        OB_FILLS = [f"ob{t}{par}" for t in range(TB) for par in range(2)]
        FILLS += ["kv0", "kv1", "kv2"] + OB_FILLS
        FILL_NO = {f: n for n, f in enumerate(FILLS)}
        FILL_AT = {}
        for s_, its in ITEM_STEP.items():
            for half, it in enumerate(its):
                FILL_AT[(s_, half if len(its) == 2 else 1)] = ["k0", "k1"] if it == "k" else [(it, h) for h in range(BH)]
        FILL_AT[(11, 0)] = [(0, h) for h in range(BH)] + ["kv0", "kv1", "kv2"]
        FILL_AT[(11, 1)] = OB_FILLS
        LAST_FILL = {"k": FILL_NO["k1"], **{lv: FILL_NO[(lv, BH - 1)] for lv in LEVELS}}

        NSTEP = TB * AH
        ATT_S0 = S_GB

        def wait_slot_used(eng, j):
            if SLOTS[j][0] == "a":
                eng.wait_ge(group_done, FIRST[j] + (1 if j == 1 else 2))
            elif j % 2:
                eng.wait_ge(group_done, FIRST[j] + TB)
            else:
                eng.wait_ge(half_used, sum(1 for i in range(0, j + 1, 2) if SLOTS[i][0] == "b"))

        def proj_bank(g):
            return bank[g % 4 + (4 if g >= FIRST[S_ODD] else 0)]

        def odd_bank(n):
            return 4 + (FIRST[S_ODD] + n) % 4 if n < 4 else n - 4

        def mixed_bank(n):
            return (FIRST[S_OE] + n) % 4 if n < 4 else n

        M_LOW_DVE = (0, 2)

        def wait_m(eng, c):
            by_dve = sum(1 for k in M_LOW_DVE if k <= c)
            if c in M_LOW_DVE:
                eng.wait_ge(m_low_dve, by_dve)
            else:
                eng.wait_ge(hT_ready, 3 * KC + c + 1 - by_dve)

        JOB = {S_ODD + 1 + c: c for c in range(KC)}

        block = ctx.enter_context(nc.Block())

        @block.sync
        def _(sp):
            x_rows = x[0].rearrange("(t p) d -> t p d", p=P)
            for t in range(TB):
                sp.dma_start(x_t[:, t, :], x_rows[t]).then_inc(x_in[t], 16)
            sp.dma_start(param_rows[0:CW, :], conv_w[0]).then_inc(params_in, 16)
            for r, v in ((ROW_NE, norm_even), (ROW_NO, norm_odd), (ROW_CB, conv_b), (ROW_LG, conv_ln_g),
                         (ROW_LB, conv_ln_b)):
                sp.dma_start(param_rows[r:r + 1, :], v).then_inc(params_in, 16)
            sp.dma_start(small_rows[0:2, :], b_gla_lr[0].rearrange("(a n) -> a n", a=2)).then_inc(params_in, 16)
            sp.dma_start(small_rows[2:3, :], gla_norm).then_inc(params_in, 16)
            sp.dma_start(w_lr[ID:ID + RANK, :], w_gla_lr[0]).then_inc(params_in, 16)

            def load(j):
                kind, ks, pieces = SLOTS[j]
                if j >= 2:
                    sp.wait_ge(lo_ready, j - 1)
                for at, m, c0, n in pieces:
                    if kind == "a":
                        dst = w_raw[j % 2][:].rearrange("p (k n) -> p k n", k=KC)[:, :, at:at + n]
                        src = WSRC[m].rearrange("(k p) n -> p k n", p=P)[:, :, c0:c0 + n]
                    else:
                        dst = w_raw[j % 2][:].rearrange("p (k n) -> p k n", k=4)
                        src = WSRC[m].rearrange("(k p) n -> p k n", p=P)[:, ks[0]:ks[0] + 4, c0:c0 + n]
                    sp.dma_start(dst, src).then_inc(raw_in[j % 2], 16)

            load(0)
            sp.dma_start(rel_rows[:], rel_bias.rearrange("b h -> h b"),
                         allow_slow_non_contiguous=True).then_inc(rel_in, 16)
            load(1)
            for j in range(2, NS):
                if j == 4:
                    sp.wait_ge(ki_ready, 1)
                    sp.dma_start(kiT[ID:2 * ID, :], kiT[0:ID, :]).then_inc(ki_twice, 16)
                if j == 5:
                    sp.wait_ge(rev_ready, 1)
                    sp.wait_ge(normed, TB)
                    for h in range(AH):
                        row = bias_rev[h:h + 1, 127:127 + S]
                        src = bass.AP(row.tensor, row.offset, [list(row.ap[0]), [-1, P], [1, S]])
                        sp.dma_start(bias_tab[:, h, :], src).then_inc(table_in, 16)
                if j == S_OE + 2:
                    sp.wait_ge(logit_ready, NSTEP)
                    sp.dma_start(x_t, x[0].rearrange("(t p) d -> p t d", p=P)).then_inc(x_again, 16)
                if j == S_ODD + 4:
                    sp.wait_ge(half_squares, 2 * TB)
                    sp.dma_start(nf_row, norm_f.rearrange("(a n) -> a n", a=1).to_broadcast([P, D])).then_inc(nf_in, 16)
                load(j)
            out_rows = out[0].rearrange("(t p) d -> t p d", p=P)
            for t in range(TB):
                for half in range(2):
                    cols = slice(512 * half, 512 * half + 512)
                    sp.wait_ge(y_ready, 2 * t + half + 1)
                    sp.dma_start(out_rows[t][:, cols], x_t[:, t, cols]).then_inc(out_done, 16)
            sp.wait_ge(out_done, 16 * 2 * TB)

        @block.gpsimd
        def _(pool):
            chain = [0]

            def link(ins):
                chain[0] += 1
                ins.then_inc(pool_chain, 1)
                pool.wait_ge(pool_chain, chain[0])

            def affine(dst, src, op, fill, step, mult):
                return nc.gpsimd.affine_select(out=dst, in_=src, compare_op=op, fill=fill, base=0,
                                               pattern=[[step, P]], channel_multiplier=mult)

            link(nc.gpsimd.memset(ident[:], 0.0))
            link(affine(ident[:], ident[:], ALU.not_equal, 1.0, -1, 1))
            nc.gpsimd.memset(ones[:], 1.0).then_inc(pool_const, 1)
            link(nc.gpsimd.memset(minus_half[:], -0.5))
            nc.gpsimd.memset(ident_bf[:], 0.0).then_inc(pool_const, 1)
            pool.wait_ge(pool_const, 2)
            affine(ident_bf[:], ident_bf[:], ALU.not_equal, 1.0, -1, 1).then_inc(pool_const, 1)
            link(nc.gpsimd.memset(neg_mask[:, 0:P], 0.0))
            affine(neg_mask[:, 0:P], neg_mask[:, 0:P], ALU.is_ge, NEG, -1, 1).then_inc(pool_const, 1)
            nc.gpsimd.iota(iota_i, [[1, P]], base=0, channel_multiplier=0).then_inc(pool_const, 1)
            nc.gpsimd.iota(iota_p, [[0, P]], base=0, channel_multiplier=1).then_inc(pool_const, 1)

            def rsqrt(first, last, ready, value, done):
                pool.wait_ge(ready, value)
                nc.gpsimd.tensor_tensor(rstd[:, first:last], stat[:, first:last], minus_half[:, first:last],
                                        ALU.pow).then_inc(done, 1)

            def split_lo(j):
                pool.wait_ge(hi_ready, j + 1)
                if j >= 3:
                    wait_slot_used(pool, j - 3)
                if j == 1:
                    v = lambda t: t[:].rearrange("p (k n) -> p k n", k=KC)[:, :, 0:M_KI]
                else:
                    v = lambda t: t[:]
                nc.gpsimd.tensor_tensor(v(w_lo[j % 3]), v(w_raw[j % 2]), v(w_hi[j % 3]).bitcast(F32),
                                        ALU.subtract).then_inc(lo_ready, 1)

            for t in range(TB):
                rsqrt(t, t + 1, var_ready, t + 1, rstd_ready)
            split_lo(0)
            pool.wait_ge(xor_ready, 1)
            affine(ixor_up, ixor, ALU.is_gt, 0.0, 1, -1).then_inc(pool_const, 1)
            split_lo(1)
            pool.wait_ge(params_T, 1)
            pool.wait_ge(squares, TB)
            nc.gpsimd.memset(r_att[:], 0.0).then_inc(att_zero, 1)

            def diff(it):
                n = ITEM_NO[it]
                pool.wait_ge(bsum_ready, 1)
                if n >= 4:
                    pool.wait_ge(fill_done, LAST_FILL[ITEMS[n - 4]] + 1)
                dst = lin[n % 4]
                if it == "k":
                    dv = dst.rearrange("p (b c) -> p b c", c=P)
                    bv = bsum.rearrange("p (b c) -> p b c", c=P)
                    last = bv[:, :, P - 1:P].to_broadcast([P, 8, P])
                    nc.gpsimd.tensor_tensor(dv, last, bv, ALU.subtract).then_inc(diff_ready, 2)
                    return
                nb = D // (2 * it)
                dv = dst.rearrange("p (b c) -> p b c", c=2 * it)
                bv = bsum.rearrange("p (b c) -> p b c", c=2 * it)
                ref = bv[:, :, it - 1:it].to_broadcast([P, nb, it])
                nc.gpsimd.tensor_tensor(dv[:, :, 0:it], ref, bv[:, :, 0:it], ALU.subtract).then_inc(diff_ready, 1)
                nc.gpsimd.tensor_tensor(dv[:, :, it:], bv[:, :, it:], ref, ALU.subtract).then_inc(diff_ready, 1)

            def add_products(c):
                for k in range(POOL_TAPS):
                    n = POOL_TAPS * c + k
                    pool.wait_ge(sum_begun, c + 1)
                    pool.wait_ge(prod_ready, n + 1)
                    if k:
                        pool.wait_ge(pool_added, n)
                    nc.gpsimd.tensor_tensor(pool_acc[c % 3], pool_acc[c % 3], prod[n % 3], ALU.add).then_inc(pool_added, 1)

            def finish_conv(c):
                pool.wait_ge(dve_taps_done, c + 1)
                pool.wait_ge(pool_added, POOL_TAPS * (c + 1))
                nc.gpsimd.tensor_tensor(conv_y(c), conv_y(c), pool_acc[c % 3], ALU.add).then_inc(conv_done, 1)

            for s_ in range(NS):
                if s_ == S_OE + 3:
                    for t in range(TB):
                        rsqrt(t, t + 1, var_ready, TB + t + 1, rstd_ready)
                if s_ == S_OO - 2:
                    finish_conv(KC - 2)
                if s_ == S_OO - 1:
                    finish_conv(KC - 1)
                    pool.wait_ge(lnvar_ready, 1)
                    nc.gpsimd.tensor_tensor(rstd[:, 0:TB], ln_var[:], minus_half[:, 0:TB], ALU.pow).then_inc(lnrstd_ready, 1)
                if s_ + 2 < NS and s_ != 2:
                    split_lo(s_ + 2)
                if s_ == 2:
                    for n, tb in enumerate((1, 2, 3)):
                        pool.wait_ge(score_step, IH * (n + 1))
                        diag = score[tb][:, P * tb:P * tb + P]
                        affine(diag, diag, ALU.is_ge, HIDDEN, -1, 1).then_inc(causal_ready, 1)
                    split_lo(s_ + 2)
                for it in ITEM_STEP.get(s_ + 1, []):
                    diff(it)
                if s_ == 12:
                    rsqrt(0, 16, ob_var, 1, ob_rstd)
                if s_ in JOB:
                    add_products(JOB[s_])
                    if JOB[s_] >= 2:
                        finish_conv(JOB[s_] - 2)
                if s_ == S_OO - 1:
                    for c in range(KC):
                        if c not in M_LOW_DVE:
                            pool.wait_ge(hT_hi_ready, 3 * KC + c + 1)
                            nc.gpsimd.tensor_tensor(hT_lo[:, c, :], m_f32[c], hT_hi[:, c, :].bitcast(F32),
                                                    ALU.subtract).then_inc(hT_ready, 1)
            for t in range(TB):
                rsqrt(t, t + 1, var_ready, 2 * TB + t + 1, rstd_ready)

        @block.scalar
        def _(act):
            chain = [0]

            def link(ins):
                chain[0] += 1
                ins.then_inc(act_chain, 1)
                act.wait_ge(act_chain, chain[0])

            def split_hi(j):
                act.wait_ge(raw_in[j % 2], raw_full[j])
                if j >= 3:
                    wait_slot_used(act, j - 3)
                if j == 1:
                    v = lambda t: t[:].rearrange("p (k n) -> p k n", k=KC)[:, :, 0:M_KI]
                else:
                    v = lambda t: t[:]
                nc.scalar.activation(v(w_hi[j % 3]), v(w_raw[j % 2]), ACT.Copy).then_inc(hi_ready, 1)

            def hT_high(rnd, order, bank_of, scale):
                for n, c in enumerate(order):
                    act.wait_ge(hT_in_bank, KC * rnd + n + 1)
                    nc.scalar.activation(hT_hi[:, c, :], bank[bank_of(n)][:], ACT.Copy,
                                         scale=scale(c)).then_inc(hT_hi_ready, 1)

            def empty(g, dst, rows=P, scale=1.0, func=ACT.Copy):
                act.wait_ge(group_done, g + 1)
                nc.scalar.activation(dst, proj_bank(g)[0:rows, :], func, scale=scale).then_inc(act_emptied, 1)

            for t in range(TB):
                act.wait_ge(x_in[t], 16)
                if t >= 2:
                    act.wait_ge(squares, t - 1)
                nc.scalar.activation(junk[t % 2], x_t[:, t, :], ACT.Square, accum_out=stat[:, t:t + 1]).then_inc(squares, 1)
            split_hi(0)
            act.wait_ge(pvec_ready, 2)
            hT_high(0, range(KC), lambda n: n, lambda c: pvec[:, c, ROW_NE:ROW_NE + 1])
            split_hi(1)

            def exps(it):
                n = ITEM_NO[it]
                act.wait_ge(diff_ready, 2 * (n + 1))
                nc.scalar.activation(lin[n % 4], lin[n % 4], ACT.Exp, scale=1.0 / TAU).then_inc(exp_ready, 1)

            def soft(n):
                act.wait_ge(max_ready, n + 1)
                if n >= 2:
                    act.wait_ge(probT_done, n - 1)
                w = P * (n // AH + 1)
                nc.scalar.activation(prob[n % 2][:, 0:w], logit[n % 2][:, 0:w], ACT.Exp, bias=neg_max[:, n:n + 1],
                                     accum_out=row_sum[:, n:n + 1]).then_inc(prob_ready, 1)

            for s_ in range(S_OE):
                if s_ != 2:
                    split_hi(s_ + 2)
                g = FIRST[s_]
                if s_ == 0:
                    empty(g, qiT[:, 0, :])
                    empty(g + 1, qiT[:, 1, :])
                elif s_ == 1:
                    act.wait_ge(group_done, g + 1)
                    nc.scalar.activation(kiT[0:ID, :], proj_bank(g)[0:ID, :], ACT.Copy).then_inc(ki_ready, 1)
                    nc.scalar.activation(lwT[ID:M_KI, :], proj_bank(g)[ID:M_KI, :], ACT.Copy).then_inc(act_emptied, 1)
                elif s_ == 2:
                    empty(g, qbT[:, 0:S], scale=DK ** -0.5)
                    act.wait_ge(wi_T, 1)
                    nc.scalar.activation(wi[:], bank[6][:, 0:TB * (RANK + IH)].rearrange(
                        "p (t c) -> p t c", t=TB)[:, :, RANK:], ACT.Copy,
                        scale=ID ** -0.5 * IH ** -0.5).then_inc(wi_ready, 1)
                    n = 0
                    for tb in (1, 2, 3):
                        for h in range(IH):
                            act.wait_ge(idx_done, n + 1)
                            if n >= 4:
                                act.wait_ge(score_step, n - 3)
                            w = P * (tb + 1)
                            nc.scalar.activation(relu_b[n % 4][:, 0:w], bank[4 + n % 2][:, 0:w],
                                                 ACT.Relu).then_inc(relu_ready, 1)
                            n += 1
                    split_hi(s_ + 2)
                    empty(g + 1, qbT[:, S:], scale=DK ** -0.5)
                    act.wait_ge(z_added, 2)
                    link(nc.scalar.activation(lin[1], lin[0], ACT.Abs))
                    link(nc.scalar.activation(lin[1], lin[1], ACT.Exp, scale=-1.0))
                    nc.scalar.activation(lin[1], lin[1], ACT.Ln, bias=1.0).then_inc(softplus, 1)
                elif s_ == 3:
                    empty(g, kbT[:, 0:S])
                    empty(g + 1, kbT[:, S:])
                    act.wait_ge(bsum_ready, 1)
                    nc.scalar.activation(q_dec, bsum, ACT.Exp, scale=1.0 / TAU).then_inc(exp_ready, 1)
                elif s_ == S_VB + 1:
                    act.wait_ge(table_in, 16 * AH)
                    act.wait_ge(masks_ready, 1)
                    for t in range(TB):
                        empty(g + t, vb[:, t, :])
                    exps("k")
                elif S_QA <= s_ < S_VA:
                    its = ITEM_STEP.get(s_ + 1, [])
                    c = 2 * (s_ - S_QA) if s_ < S_KA else 2 * (s_ - S_KA)
                    if s_ == S_KA:
                        act.wait_ge(score_step, 3 * IH)
                    dst = qaT if s_ < S_KA else kaT
                    sc = AD ** -0.5 if s_ < S_KA else 1.0
                    empty(g, dst[:, c, :], scale=sc)
                    if its:
                        exps(its[0])
                    empty(g + 1, dst[:, c + 1, :], scale=sc)
                    for it in its[1:]:
                        exps(it)
                elif s_ == S_VA + 1:
                    act.wait_ge(mask_ready, 3)
                    for t in range(TB):
                        empty(g + t, va[:, t, :])
                    act.wait_ge(fill_emptied, len(FILLS))
                    soft(0)
                    soft(1)
                    for t in range(TB):
                        nc.scalar.activation(sq_b[t], ob[:, t, :], ACT.Square).then_inc(ob_squared, 1)
                elif s_ >= ATT_S0:
                    for u in range(TB):
                        n0 = AH * (s_ - ATT_S0) + 2 * u
                        for n in (n0 + 2, n0 + 3):
                            if n < NSTEP:
                                soft(n)
                        if s_ == S_GB + 1:
                            if u == 0:
                                act.wait_ge(fill_done, len(FILLS))
                            empty(g + u, gate_b[:, u, :])
                        if s_ == S_GA + 1 and u < TB - 1:
                            empty(g + u, gate_a[:, u, :])
                    if s_ == S_GB + 1:
                        act.wait_ge(act_emptied, evacs_through(FIRST[S_GB] + 3, "act"))
                        nc.scalar.activation(r_vb[:], r_vb[:], ACT.Silu).then_inc(gates_silu, 1)
            act.wait_ge(act_emptied, evacs_through(FIRST[S_GA] + 2, "act"))
            nc.scalar.activation(gate_a[:, 0:TB - 1, :], gate_a[:, 0:TB - 1, :], ACT.Silu).then_inc(gates_silu, 1)
            empty(FIRST[S_GA] + TB - 1, gate_a[:, TB - 1, :], func=ACT.Silu)
            wait_slot_used(act, S_OE - 1)
            hT_high(1, B_FIRST, mixed_bank, lambda c: 1.0 if c < 4 else pb3[:, 2:3])

            def row_squares(base, n0, half):
                for t in range(TB):
                    act.wait_ge(dve_emptied, base + TB * half + t + 1)
                    n = TB * half + t
                    if n0 + n:
                        act.wait_ge(half_squares, n0 + n)
                    nc.scalar.activation(sq_junk[:, 0:512], x_t[:, t, 512 * half:512 * half + 512], ACT.Square,
                                         accum_out=half_sq[:, n:n + 1]).then_inc(half_squares, 1)

            for s_ in range(S_OE, S_ODD):
                split_hi(s_ + 2)
                if s_ >= S_ODD - 2:
                    row_squares(0, 0, s_ - (S_ODD - 2))
            wait_slot_used(act, S_ODD - 1)
            hT_high(2, range(KC), odd_bank, lambda c: pvec[:, c, ROW_NO:ROW_NO + 1])

            def products(c):
                if c >= 3:
                    act.wait_ge(conv_done, c - 2)
                act.wait_ge(taps_done, c + 1)
                nc.scalar.activation(pool_acc[c % 3], bank[c % 3][:], ACT.Identity,
                                     bias=pvec[:, c, ROW_CB:ROW_CB + 1]).then_inc(sum_begun, 1)
                for k in range(POOL_TAPS):
                    tap, n = PE_TAPS + k, POOL_TAPS * c + k
                    if n >= 3:
                        act.wait_ge(pool_added, n - 2)
                    nc.scalar.activation(prod[n % 3], upad[c % 3][:, tap:tap + S], ACT.Copy,
                                         scale=pvec[:, c, tap:tap + 1]).then_inc(prod_ready, 1)

            def centre_squares():
                for c in range(KC):
                    act.wait_ge(centred, c + 1)
                    nc.scalar.activation(ln_sq[c], conv_y(c), ACT.Square).then_inc(lnsq_ready, 1)

            for s_ in range(S_ODD, S_OO):
                split_hi(s_ + 2)
                g = FIRST[s_]
                if s_ in CHUNK:
                    c = CHUNK[s_]
                    if c >= 2:
                        act.wait_ge(taps_done, c - 1)
                    for k in range(PE_TAPS):
                        nc.scalar.activation(tap_diag[c % 2][k], ident[:], ACT.Copy,
                                             scale=pvec[:, c, k:k + 1]).then_inc(diag_ready, 1)
                    if c >= 2:
                        act.wait_ge(u_ready, c - 1)
                    act.wait_ge(group_done, g + 2)
                    nc.scalar.activation(sgl[c % 2], proj_bank(g + 1)[:], ACT.Sigmoid).then_inc(act_emptied, 1)
                    if s_ in JOB:
                        products(JOB[s_])
                else:
                    if s_ in JOB:
                        products(JOB[s_])
                    c = GATE[s_]
                    empty(g, gate_s(c), func=ACT.Silu)
                    if s_ == S_OO - 2:
                        centre_squares()
                    if s_ < S_OO - 1:
                        empty(g + 1, gate_s(c + 1), func=ACT.Silu)

            def norm_silu(c):
                act.wait_ge(scaled, c + 1)
                nc.scalar.activation(conv_y(c), conv_y(c), ACT.Silu, scale=pvec[:, c, ROW_LG:ROW_LG + 1],
                                     bias=pvec[:, c, ROW_LB:ROW_LB + 1]).then_inc(ln_silu, 1)

            def m_high(c):
                act.wait_ge(m_ready, c + 1)
                nc.scalar.activation(hT_hi[:, c, :], m_f32[c], ACT.Copy).then_inc(hT_hi_ready, 1)

            for c in range(4):
                norm_silu(c)
            wait_slot_used(act, S_OO - 1)
            for c in range(4):
                m_high(c)
            norm_silu(4)
            norm_silu(5)
            empty(FIRST[S_OO - 1] + 1, gate_s(KC - 1), func=ACT.Silu)
            norm_silu(6)
            norm_silu(7)
            for c in range(4, KC):
                m_high(c)
            for s_ in range(S_OO, NS - 2):
                split_hi(s_ + 2)
            for half in range(2):
                row_squares(2 * TB, 2 * TB, half)

        @block.vector
        def _(dve):
            chain = [0]

            def link(ins):
                chain[0] += 1
                ins.then_inc(dve_chain, 1)
                dve.wait_ge(dve_chain, chain[0])

            def scale_rows(t, count):
                dve.wait_ge(rstd_ready, count)
                nc.vector.tensor_scalar(oa[:, t, :], x_t[:, t, 0:512], rstd[:, t:t + 1], None, ALU.mult)
                nc.vector.tensor_scalar(ob[:, t, :], x_t[:, t, 512:], rstd[:, t:t + 1], None,
                                        ALU.mult).then_inc(normed, 1)

            def row_variance(t, n0, half):
                dve.wait_ge(half_squares, n0 + TB * half + t + 1)
                v = stat[:, t:t + 1]
                if half == 0:
                    link(nc.vector.tensor_scalar(v, half_sq[:, t:t + 1], 1.0 / D, EPS, ALU.mult, ALU.add))
                else:
                    nc.vector.scalar_tensor_tensor(out=v, in0=half_sq[:, TB + t:TB + t + 1], scalar=1.0 / D,
                                                   in1=v, op0=ALU.mult, op1=ALU.add).then_inc(var_ready, 1)

            def hT_low(rnd, order, bank_of, scale):
                for n, c in enumerate(order):
                    dve.wait_ge(hT_hi_ready, KC * rnd + n + 1)
                    nc.vector.scalar_tensor_tensor(
                        out=hT_lo[:, c, :], in0=bank[bank_of(n)][:], scalar=scale(c),
                        in1=hT_hi[:, c, :].bitcast(F32), op0=ALU.mult, op1=ALU.subtract).then_inc(hT_ready, 1)

            for t in range(TB + 1):
                if t == TB:
                    scale_rows(t - 1, t)
                    dve.wait_ge(params_T, 1)
                    nc.vector.tensor_copy(pvec[:], bank[7][:, 0:KC * NROW].rearrange(
                        "p (c r) -> p c r", c=KC)).then_inc(pvec_ready, 1)
                    nc.vector.tensor_copy(pb3[:, 0:3], bank[7][:, KC * NROW:KC * NROW + 3]).then_inc(pvec_ready, 1)
                if t < TB:
                    dve.wait_ge(squares, t + 1)
                    nc.vector.tensor_scalar(stat[:, t:t + 1], stat[:, t:t + 1], 1.0 / D, EPS, ALU.mult,
                                            ALU.add).then_inc(var_ready, 1)
                if 0 < t < TB:
                    scale_rows(t - 1, t)
            dve.wait_ge(pvec_ready, 2)
            hT_low(0, range(KC), lambda n: n, lambda c: pvec[:, c, ROW_NE:ROW_NE + 1])
            dve.wait_ge(rel_in, 16)
            starts = bucket_starts() + [S]
            for b in range(NB):
                lo_d, hi_d = starts[b], starts[b + 1]
                last = nc.vector.tensor_copy(bias_rev[:, S - hi_d:S - lo_d],
                                             rel_rows[:, b:b + 1].to_broadcast([AH, hi_d - lo_d]))
            link(last)
            nc.vector.memset(bias_rev[:, S:S + P], 0.0).then_inc(rev_ready, 1)
            dve.wait_ge(pool_const, 6)
            nc.vector.tensor_tensor(ixor, iota_i, iota_p, ALU.bitwise_xor).then_inc(xor_ready, 1)
            dve.wait_ge(pool_const, 7)
            for lg in range(5):
                link(nc.vector.tensor_scalar(ishift, ixor_up, lg, None, ALU.logical_shift_right))
                link(nc.vector.tensor_scalar(level_mask[:, lg, :], ishift, 1, None, ALU.is_equal))
            nc.vector.tensor_copy(level_mask[:, 5, :], ident[:]).then_inc(masks_ready, 1)

            for i in range(2):
                dve.wait_ge(z_done, i + 1)
                nc.vector.tensor_scalar(lin[0][:, S * i:S * i + S], bank[7][:], pb3[:, i:i + 1], None,
                                        ALU.add).then_inc(z_added, 1)
            dve.wait_ge(wi_ready, 1)
            n = 0
            for tb in (1, 2, 3):
                w = P * (tb + 1)
                for h in range(IH):
                    dve.wait_ge(relu_ready, n + 1)
                    if h == 0:
                        ins = nc.vector.tensor_scalar(score[tb], relu_b[n % 4][:, 0:w], wi[:, tb, 0:1], None, ALU.mult)
                    else:
                        dve.wait_ge(score_step, n)
                        ins = nc.vector.scalar_tensor_tensor(out=score[tb], in0=relu_b[n % 4][:, 0:w],
                                                             scalar=wi[:, tb, h:h + 1], in1=score[tb],
                                                             op0=ALU.mult, op1=ALU.add)
                    ins.then_inc(score_step, 1)
                    n += 1
            dve.wait_ge(softplus, 1)
            link(nc.vector.scalar_tensor_tensor(out=lin[2], in0=lin[0], scalar=0.0, in1=lin[1], op0=ALU.min,
                                                op1=ALU.subtract))
            for b in range(8):
                ins = nc.vector.tensor_tensor_scan(bsum[:, P * b:P * b + P], ones[:], lin[2][:, P * b:P * b + P],
                                                   0.0, ALU.mult, ALU.add)
            ins.then_inc(bsum_ready, 1)

            dve.wait_ge(causal_ready, 3)
            def topk_round(r):
                n = 6 * r
                for step in range(2):
                    for tb in (1, 2, 3):
                        if n >= 3:
                            dve.wait_ge(topk_step, n - 2)
                        if step == 0:
                            ins = nc.vector.max(top8[:, tb - 1, :], score[tb])
                        else:
                            ins = nc.vector.match_replace(score[tb], top8[:, tb - 1, :], score[tb], TAKEN)
                        ins.then_inc(topk_step, 1)
                        n += 1

            def topk_masks():
                dve.wait_ge(topk_step, 6 * ROUNDS)
                for tb in (1, 2, 3):
                    w = P * (tb + 1)
                    nc.vector.tensor_scalar(neg_mask[:, MASK_AT[tb]:MASK_AT[tb] + w], score[tb],
                                            0.5 * (HIDDEN + TAKEN), NEG, ALU.is_gt, ALU.mult).then_inc(mask_ready, 1)

            ROUNDS = TOPK // 8
            EARLY_ROUNDS = ROUNDS - 8
            for r in range(EARLY_ROUNDS):
                topk_round(r)

            dve.wait_ge(exp_ready, 1)
            link(nc.vector.tensor_copy(chunk_decay[:], q_dec.rearrange("p (i t c) -> p i t c", i=2, c=P)[:, :, :, P - 1]))
            nc.vector.tensor_tensor(q_dec, q_dec, qbT, ALU.mult).then_inc(operand_ready, 1)

            def operand(it):
                n = ITEM_NO[it]
                dve.wait_ge(exp_ready, n + 2)
                v = lin[n % 4]
                if it == "k":
                    nc.vector.tensor_tensor(v, v, kbT, ALU.mult).then_inc(operand_ready, 1)
                    return
                vv, kv, qv = (a.rearrange("p (b c) -> p b c", c=2 * it) for a in (v, kbT, qbT))
                nc.vector.tensor_tensor(vv[:, :, 0:it], vv[:, :, 0:it], kv[:, :, 0:it], ALU.mult)
                nc.vector.tensor_tensor(vv[:, :, it:], vv[:, :, it:], qv[:, :, it:],
                                        ALU.mult).then_inc(operand_ready, 1)

            def empty_fill(f):
                n = FILL_NO[f]
                b = bank[4 + n % 4]
                dve.wait_ge(fill_done, n + 1)
                if f in ("k0", "k1"):
                    w = 2 if f == "k0" else 1
                    t0 = 0 if f == "k0" else 2
                    nc.vector.tensor_copy(k_rows[:, t0:t0 + w, :], b[:, 0:256 * w].rearrange(
                        "p (t c) -> p t c", t=w)).then_inc(fill_emptied, 1)
                    return
                if isinstance(f, tuple):
                    lv, h = f
                    a = attn[:, TB * h:TB * h + TB, :]
                    dve.wait_ge(att_zero, 1)
                    if lv == 0:
                        m = level_mask[:, 5:6, :].to_broadcast([P, TB, P])
                        ins = nc.vector.copy_predicated(a, m, b[:].rearrange("p (t i) -> p t i", t=TB))
                    elif lv >= 32:
                        v = b[:, 0:TB * P // 2].rearrange("p (t i) -> p t i", t=TB)
                        for p0 in range(0, P, 2 * lv):
                            ins = nc.vector.tensor_copy(a[p0:p0 + lv, :, p0 + lv:p0 + 2 * lv],
                                                        v[p0:p0 + lv, :, p0 // 2:p0 // 2 + lv])
                    else:
                        lg = lv.bit_length() - 1
                        m = level_mask[:, lg:lg + 1, :].rearrange("p t (a c) -> p t a c", c=2 * lv)[:, :, :, lv:]
                        ins = nc.vector.copy_predicated(
                            a.rearrange("p t (a c) -> p t a c", c=2 * lv)[:, :, :, lv:],
                            m.to_broadcast([P, TB, P // (2 * lv), lv]),
                            b[:, 0:TB * P // 2].rearrange("p (t a c) -> p t a c", t=TB, c=lv))
                    ins.then_inc(fill_emptied, 1)
                    return
                t = int(f[2])
                if f[:2] == "kv":
                    if t == 0:
                        nc.vector.tensor_copy(state[:, 1, :], b[:, 0:256]).then_inc(fill_emptied, 1)
                        return
                    dve.wait_ge(fill_emptied, n)
                    for i in range(2):
                        ins = nc.vector.scalar_tensor_tensor(
                            out=state[:, t + 1, DV * i:DV * i + DV], in0=state[:, t, DV * i:DV * i + DV],
                            scalar=chunk_decay[:, i, t:t + 1], in1=b[:, DV * i:DV * i + DV], op0=ALU.mult, op1=ALU.add)
                    ins.then_inc(fill_emptied, 1)
                    return
                par = int(f[3])
                nc.vector.tensor_copy(ob[:, t, :].rearrange("p (i r e) -> p i r e", i=2, r=2)[:, :, par, :],
                                      b[:, 0:2 * DV].rearrange("p (i e) -> p i e", i=2)).then_inc(fill_emptied, 1)

            operand("k")
            operand(64)
            for f in ("k0", "k1"):
                empty_fill(f)
            late = EARLY_ROUNDS
            for s_ in range(7, 11):
                for it in ITEM_STEP[s_]:
                    for h in range(BH):
                        empty_fill((it, h))
                    if late < ROUNDS:
                        topk_round(late)
                        late += 1
                for it in ITEM_STEP.get(s_ + 1, []):
                    operand(it)
            for r in range(late, ROUNDS):
                topk_round(r)
            topk_masks()
            for f in FILLS[FILL_NO[(0, 0)]:]:
                empty_fill(f)
            def logits(n):
                tb, h = divmod(n, AH)
                w = P * (tb + 1)
                dve.wait_ge(qk_done, n + 1)
                if n >= 2:
                    dve.wait_ge(prob_ready, n - 1)
                nc.vector.tensor_tensor_reduce(out=logit[n % 2][:, 0:w], in0=bank[4 + n % 2][:, 0:w],
                                               in1=bias_tab[:, h, S - w:S], scale=1.0, scalar=-3.0e38, op0=ALU.add,
                                               op1=ALU.max, accum_out=row_max[:, n:n + 1]).then_inc(logit_ready, 1)
                dve.wait_ge(logit_ready, n + 1)
                nc.vector.tensor_scalar(neg_max[:, n:n + 1], row_max[:, n:n + 1], -1.0, None,
                                        ALU.mult).then_inc(max_ready, 1)

            def empty_oa(tb):
                dve.wait_ge(pv_done, AH * (tb + 1))
                link(nc.vector.reciprocal(row_inv[:, AH * tb:AH * tb + AH], row_sum[:, AH * tb:AH * tb + AH]))
                inv = row_inv[:, AH * tb:AH * tb + AH].unsqueeze(2).to_broadcast([P, AH, AD])
                nc.vector.tensor_tensor(oa[:, tb, :].rearrange("p (h d) -> p h d", h=AH),
                                        bank[7][:].rearrange("p (h d) -> p h d", h=AH), inv,
                                        ALU.mult).then_inc(oa_emptied, 1)

            dve.wait_ge(table_in, 16 * AH)
            logits(0)
            logits(1)
            for n in range(NSTEP):
                if n + 2 < NSTEP:
                    logits(n + 2)
                w = P * (n // AH + 1)
                dve.wait_ge(probT_done, n + 1)
                if n >= 2:
                    dve.wait_ge(pv_done, n - 1)
                nc.vector.tensor_copy(probT[n % 2][:, 0:w], bank[6][:, 0:w]).then_inc(probT_ready, 1)
                if n % AH == 0 and n:
                    empty_oa(n // AH - 1)
                if n < TB:
                    dve.wait_ge(ob_squared, n + 1)
                    nc.vector.tensor_reduce(stat[:, 4 * n:4 * n + 4], sq_b[n].rearrange("p (h e) -> p h e", h=BH),
                                            AX.X, ALU.add).then_inc(ob_summed, 1)
                if n == TB:
                    dve.wait_ge(ob_summed, TB)
                    nc.vector.tensor_scalar(stat[:], stat[:], 1.0 / DV, EPS, ALU.mult, ALU.add).then_inc(ob_var, 1)
                if n in range(20, 20 + TB):
                    t = n - 20
                    dve.wait_ge(gates_silu, 1)
                    nc.vector.tensor_tensor(ob[:, t, :], ob[:, t, :], gate_b[:, t, :], ALU.mult).then_inc(mixed_b, 1)
                if n in range(10, 10 + TB):
                    t = n - 10
                    dve.wait_ge(ob_rstd, 1)
                    heads = ob[:, t, :].rearrange("p (h e) -> p h e", h=BH)
                    link(nc.vector.tensor_tensor(heads, heads, rstd[:, BH * t:BH * t + BH].unsqueeze(2).to_broadcast(
                        [P, BH, DV]), ALU.mult))
            dve.wait_ge(gates_silu, 2)
            dve.wait_ge(oa_emptied, TB - 1)
            nc.vector.tensor_tensor(oa[:, 0:TB - 1, :], oa[:, 0:TB - 1, :], gate_a[:, 0:TB - 1, :],
                                    ALU.mult).then_inc(mixed_a, 1)
            empty_oa(TB - 1)
            dve.wait_ge(oa_emptied, TB)
            dve.wait_ge(act_emptied, evacs_through(FIRST[S_GA] + TB - 1, "act"))
            nc.vector.tensor_tensor(oa[:, TB - 1, :], oa[:, TB - 1, :], gate_a[:, TB - 1, :],
                                    ALU.mult).then_inc(mixed_a, 1)
            hT_low(1, B_FIRST, mixed_bank, lambda c: 1.0 if c < 4 else pb3[:, 2:3])

            def residual(s0, variance, scaled_rows):
                for half in range(2):
                    for t in range(TB):
                        g = FIRST[s0 + 2 * half] + t
                        dve.wait_ge(group_done, g + 1)
                        xs = x_t[:, t, 512 * half:512 * half + 512]
                        nc.vector.tensor_tensor(xs, proj_bank(g)[:], xs, ALU.add).then_inc(dve_emptied, 1)
                        if half and t:
                            scaled_rows(t - 1)
                        if half:
                            if t == 0:
                                for u in range(TB):
                                    variance(u, 0)
                            variance(t, 1)
                scaled_rows(TB - 1)

            dve.wait_ge(x_again, 16)
            residual(S_OE, lambda t, half: row_variance(t, 0, half), lambda t: scale_rows(t, TB + t + 1))
            hT_low(2, range(KC), odd_bank, lambda c: pvec[:, c, ROW_NO:ROW_NO + 1])

            for i in range(3):
                ins = nc.vector.memset(upad[i][:, 0:CW - 1], 0.0)
            link(ins)
            chunk_slots = sorted(CHUNK, key=lambda j: CHUNK[j])

            def glu(c):
                g = FIRST[chunk_slots[c]]
                dve.wait_ge(act_emptied, evacs_through(g + 1, "act"))
                if c >= 3:
                    dve.wait_ge(prod_ready, POOL_TAPS * (c - 2))
                nc.vector.tensor_tensor(upad[c % 3][:, CW - 1:PADW], proj_bank(g)[:], sgl[c % 2],
                                        ALU.mult).then_inc(u_ready, 1)

            FIRST_TAP = PE_TAPS + POOL_TAPS
            taps = list(range(FIRST_TAP, CW))
            n_first = (len(taps) + 1) // 2
            tap_no = {}
            count = [0]

            def tap(c, i):
                acc, k = conv_y(c), taps[i]
                src, w = upad[c % 3][:, k:k + S], pvec[:, c, k:k + 1]
                if i == 0:
                    dve.wait_ge(u_ready, c + 1)
                    ins = nc.vector.tensor_scalar(acc, src, w, None, ALU.mult)
                else:
                    dve.wait_ge(tap_step, tap_no[c, i - 1])
                    ins = nc.vector.scalar_tensor_tensor(out=acc, in0=src, scalar=w, in1=acc, op0=ALU.mult, op1=ALU.add)
                if i < len(taps) - 1:
                    ins.then_inc(tap_step, 1)
                    count[0] += 1
                    tap_no[c, i] = count[0]
                else:
                    ins.then_inc(dve_taps_done, 1)

            glu(0)
            for c in range(KC + 1):
                for i in range(n_first):
                    if c < KC:
                        tap(c, i)
                    if c and n_first + i < len(taps):
                        tap(c - 1, n_first + i)
                    if i == (n_first // 2 if c else n_first - 1) and c + 1 < KC:
                        glu(c + 1)
            dve.wait_ge(mean_done, 1)
            for c in range(KC + 1):
                if c < KC:
                    nc.vector.scalar_tensor_tensor(out=conv_y(c), in0=bank[3][:], scalar=-1.0 / D, in1=conv_y(c),
                                                   op0=ALU.mult, op1=ALU.add).then_inc(centred, 1)
                if c >= 2 and c % 2 == 0:
                    dve.wait_ge(lnsq_ready, c)
                    nc.vector.tensor_tensor(ln_sq[c - 2], ln_sq[c - 2], ln_sq[c - 1], ALU.add).then_inc(lnsq_paired, 1)
            dve.wait_ge(lnvar_done, 1)
            nc.vector.tensor_scalar(ln_var[:], bank[0][:, 0:TB], 1.0 / D, EPS, ALU.mult, ALU.add).then_inc(lnvar_ready, 1)
            dve.wait_ge(lnrstd_ready, 1)
            for t in range(TB):
                ins = nc.vector.tensor_scalar(ln_diag[:, P * t:P * t + P], ident[:], rstd[:, t:t + 1], None, ALU.mult)
            ins.then_inc(lndiag_ready, 1)
            dve.wait_ge(lnrstd_wide, 1)

            def m_low(c):
                dve.wait_ge(hT_hi_ready, 3 * KC + c + 1)
                nc.vector.tensor_tensor(hT_lo[:, c, :], m_f32[c], hT_hi[:, c, :].bitcast(F32),
                                        ALU.subtract).then_inc(m_low_dve, 1)

            for c in range(KC + 1):
                if c < KC:
                    nc.vector.tensor_tensor(conv_y(c), conv_y(c), bank[1][:], ALU.mult).then_inc(scaled, 1)
                if c >= 1:
                    dve.wait_ge(ln_silu, c)
                    if c - 4 in M_LOW_DVE:
                        m_low(c - 4)
                    dve.wait_ge(act_emptied, evacs_through(FIRST[S_OO] - (1 if c == KC else 2), "act"))
                    nc.vector.tensor_tensor(m_f32[c - 1], conv_y(c - 1), gate_s(c - 1), ALU.mult).then_inc(m_ready, 1)
            dve.wait_ge(nf_in, 16)

            def final_rows(t):
                dve.wait_ge(rstd_ready, 2 * TB + t + 1)
                for half in range(2):
                    cols = slice(512 * half, 512 * half + 512)
                    nc.vector.scalar_tensor_tensor(out=x_t[:, t, cols], in0=x_t[:, t, cols], scalar=rstd[:, t:t + 1],
                                                   in1=nf_row[:, cols], op0=ALU.mult, op1=ALU.mult).then_inc(y_ready, 1)

            residual(S_OO, lambda t, half: row_variance(t, 2 * TB, half), final_rows)

        @block.tensor
        def _(pe):
            pe.wait_ge(pool_chain, 2)
            def transpose_blocks(order, blocks, ready, bank_of):
                for n, t in blocks:
                    ready(n, t)
                    ins = nc.tensor.transpose(bank[bank_of(n)][:, P * t:P * t + P], hx(t, order[n]), ident[:])
                    if t == TB - 1:
                        ins.then_inc(hT_in_bank, 1)

            LOW, HIGH = range(4), range(4, KC)
            ROWS_0 = [(n, t) for t in range(TB) for n in range(7)] + [(7, t) for t in range(TB)]
            ROWS_1 = [(n, t) for part in (LOW, HIGH) for t in range(TB) for n in part]
            ROWS_2 = [(n, t) for part in (LOW, HIGH) for t in range(TB - 1) for n in part] + \
                     [(n, TB - 1) for n in range(KC)]

            def keep_clock(n, b):
                for _ in range(n):
                    nc.tensor.matmul(bank[b][:, 0:P], ident_bf[:], ident_bf[:], start=True, stop=True)

            def rows_normed(n, t):
                pe.wait_ge(normed, t + 1)
                if n == 7:
                    pe.wait_ge(pvec_ready, 2)

            pe.wait_ge(pool_const, 3)
            keep_clock(WARM_START, 7)
            transpose_blocks(range(KC), ROWS_0[0:21], rows_normed, lambda n: n)
            pe.wait_ge(params_in, 16 * 9)
            for c in range(KC):
                nc.tensor.transpose(bank[7][:, NROW * c:NROW * c + NROW], param_rows[0:NROW, P * c:P * c + P],
                                    ident[0:NROW, 0:NROW])
            nc.tensor.transpose(bank[7][:, KC * NROW:KC * NROW + 3], small_rows[:],
                                ident[0:3, 0:3]).then_inc(params_T, 1)
            transpose_blocks(range(KC), ROWS_0[21:], rows_normed, lambda n: n)

            def bank_free(g):
                if g < 4:
                    pe.wait_ge(hT_ready, g + 1)
                    return
                if FIRST[S_ODD] <= g < FIRST[S_ODD] + 4:
                    pe.wait_ge(hT_ready, 2 * KC + g - FIRST[S_ODD] + 1)
                    return
                if evac_by[g - 4] == "act":
                    pe.wait_ge(act_emptied, evacs_through(g - 4, "act"))
                elif evac_by[g - 4] == "val":
                    pe.wait_ge(u_ready, evacs_through(g - 4, "val"))
                else:
                    pe.wait_ge(dve_emptied, evacs_through(g - 4, "residual"))

            def slot_ready(j):
                pe.wait_ge(lo_ready, j + 1)

            def group_a(j, i, hT_round=None, between={}):
                g = FIRST[j] + i
                bank_free(g)
                m = M_KI if j == 1 else P
                wh = w_hi[j % 3][:].rearrange("p (k n) -> p k n", k=KC)
                wl = w_lo[j % 3][:].rearrange("p (k n) -> p k n", k=KC)
                passes = ((wh, hT_hi), (wh, hT_lo), (wl, hT_hi))
                if j == 0 and i == 0:
                    order = [(k, q) for k in range(KC) for q in (0, 1)] + [(k, 2) for k in range(KC)]
                else:
                    order = [(k, q) for k in range(KC) for q in range(3)]
                for n, (k, q) in enumerate(order):
                    if hT_round is not None and q == 0:
                        pe.wait_ge(hT_ready, KC * hT_round + k + 1)
                    if j == 0 and i == 0 and (k, q) == (0, 2):
                        pe.wait_ge(lo_ready, 1)
                    if n in between:
                        between[n]()
                    w, h = passes[q]
                    ins = nc.tensor.matmul(proj_bank(g)[0:m, :], w[:, k, P * i:P * i + m], h[:, k, :],
                                           start=(n == 0), stop=(n == 3 * KC - 1))
                ins.then_inc(group_done, 1)

            def unit_b(j, t, part=(0, 4), hT_round=None):
                g = FIRST[j] + t
                ks = SLOTS[j][1]
                first, final = j % 2 == 0, j % 2 == 1
                if first and part[0] == 0:
                    bank_free(g)
                wh = w_hi[j % 3][:].rearrange("p (k n) -> p k n", k=4)
                wl = w_lo[j % 3][:].rearrange("p (k n) -> p k n", k=4)
                for i in range(*part):
                    k = ks[i]
                    if hT_round == 3:
                        wait_m(pe, k)
                    elif hT_round is not None:
                        pe.wait_ge(hT_ready, KC * hT_round + (i if first else 4 + i) + 1)
                    for q, (h, w) in enumerate(((hT_hi, wh), (hT_hi, wl), (hT_lo, wh))):
                        ins = nc.tensor.matmul(proj_bank(g)[:], h[:, k, P * t:P * t + P], w[:, i, :],
                                               start=(first and i == 0 and q == 0), stop=(final and i == 3 and q == 2))
                if part[1] == 4:
                    if final:
                        ins.then_inc(group_done, 1)
                    elif t == TB - 1:
                        ins.then_inc(half_used, 1)

            pe.wait_ge(hi_ready, 1)
            group_a(0, 0, hT_round=0)
            group_a(0, 1)
            slot_ready(1)
            group_a(1, 0)
            slot_ready(2)
            group_a(2, 0)
            pe.wait_ge(act_emptied, 3)
            pe.wait_ge(hT_ready, KC)
            for t in range(TB):
                ins = nc.tensor.transpose(bank[6][:, (RANK + IH) * t:(RANK + IH) * (t + 1)],
                                          lwT[ID:M_KI, P * t:P * t + P], ident[ID:M_KI, ID:M_KI])
            ins.then_inc(wi_T, 1)
            nc.tensor.matmul(bank[7][:], w_lr[ID:ID + RANK, 0:P], lwT[ID:ID + RANK, :], start=True,
                             stop=True).then_inc(z_done, 1)
            pe.wait_ge(ki_twice, 16)
            n = 0
            for tb in (1, 2, 3):
                for h in range(IH):
                    if n >= 2:
                        pe.wait_ge(relu_ready, n - 1)
                    p0 = 64 * (h % 2)
                    nc.tensor.matmul(bank[4 + n % 2][:, 0:P * (tb + 1)], qiT[p0:p0 + 64, h // 2, P * tb:P * tb + P],
                                     kiT[p0:p0 + 64, 0:P * (tb + 1)], start=True, stop=True).then_inc(idx_done, 1)
                    n += 1
                if tb == 1:
                    pe.wait_ge(z_added, 1)
                    nc.tensor.matmul(bank[7][:], w_lr[ID:ID + RANK, P:2 * P], lwT[ID:ID + RANK, :], start=True,
                                     stop=True).then_inc(z_done, 1)
            group_a(2, 1)

            def fill(f):
                n = FILL_NO[f]
                b = bank[4 + n % 4]
                if n >= 4:
                    pe.wait_ge(fill_emptied, n - 3)
                if f in ("k0", "k1"):
                    if f == "k0":
                        pe.wait_ge(operand_ready, ITEM_NO["k"] + 2)
                        pe.wait_ge(wi_ready, 1)
                        pe.wait_ge(z_added, 2)
                        pe.wait_ge(relu_ready, 12)
                    for a, t in enumerate((0, 1) if f == "k0" else (2,)):
                        for i in range(2):
                            ins = nc.tensor.transpose(b[:, 256 * a + P * i:256 * a + P * i + P],
                                                      lin[0][:, S * i + P * t:S * i + P * t + P], ident[:])
                    ins.then_inc(fill_done, 1)
                    return
                if isinstance(f, tuple):
                    lv, h = f
                    if h == 0 and lv:
                        pe.wait_ge(operand_ready, ITEM_NO[lv] + 2)
                    p0, at = 64 * (h % 2), S * (h // 2)
                    kk = lin[ITEM_NO[lv] % 4] if lv else kbT
                    qq = lin[ITEM_NO[lv] % 4] if lv else qbT
                    for t in range(TB):
                        cols = slice(at + P * t, at + P * t + P)
                        keys, queries, n_q = kk[p0:p0 + 64, cols], qq[p0:p0 + 64, cols], P
                        if lv:
                            queries = queries.rearrange("p (a c) -> p a c", c=2 * lv)[:, :, lv:]
                            n_q = P // 2
                        ins = nc.tensor.matmul(b[:, n_q * t:n_q * t + n_q], keys, queries, start=True, stop=True)
                    ins.then_inc(fill_done, 1)
                    return
                t = int(f[2])
                if f[:2] == "kv":
                    for h in range(BH):
                        p0 = 64 * (h % 2)
                        ins = nc.tensor.matmul(b[p0:p0 + 64, DV * (h // 2):DV * (h // 2) + DV],
                                               k_rows[:, t, 64 * h:64 * h + 64], vb[:, t, DV * h:DV * h + DV],
                                               start=True, stop=True)
                    ins.then_inc(fill_done, 1)
                    return
                pe.wait_ge(fill_emptied, FILL_NO["kv0"] if t == 0 else FILL_NO[f"kv{t - 1}"] + 1)
                pe.wait_ge(fill_emptied, FILL_NO[(0, BH - 1)] + 1)
                for h in (int(f[3]), int(f[3]) + 2):
                    p0 = 64 * (h % 2)
                    o = b[:, DV * (h // 2):DV * (h // 2) + DV]
                    ins = nc.tensor.matmul(o, attn[:, TB * h + t, :], vb[:, t, DV * h:DV * h + DV], start=True,
                                           stop=(t == 0))
                    if t:
                        ins = nc.tensor.matmul(o, q_dec[p0:p0 + 64, S * (h // 2) + P * t:S * (h // 2) + P * t + P],
                                               state[p0:p0 + 64, t, DV * (h // 2):DV * (h // 2) + DV],
                                               start=False, stop=True)
                ins.then_inc(fill_done, 1)

            def fills(s_, half):
                for f in FILL_AT.get((s_, half), []):
                    fill(f)

            def qk(n):
                tb, h = divmod(n, AH)
                w, p0 = P * (tb + 1), 64 * (h % 2)
                if n == 0:
                    pe.wait_ge(fill_emptied, len(FILLS))
                    pe.wait_ge(act_emptied, evacs_through(FIRST[S_VA] - 1, "act"))
                if n >= 2:
                    pe.wait_ge(logit_ready, n - 1)
                b = bank[4 + n % 2][:, 0:w]
                nc.tensor.matmul(b, qaT[p0:p0 + 64, h // 2, P * tb:P * tb + P], kaT[p0:p0 + 64, h // 2, 0:w],
                                 start=True, stop=False)
                if tb and h == 0:
                    pe.wait_ge(mask_ready, tb)
                nc.tensor.matmul(b, ident_bf[:], neg_mask[:, MASK_AT[tb]:MASK_AT[tb] + w], start=False,
                                 stop=True).then_inc(qk_done, 1)

            def prob_transpose(n):
                tb = n // AH
                pe.wait_ge(prob_ready, n + 1)
                if n >= 1:
                    pe.wait_ge(probT_ready, n)
                for i in range(tb + 1):
                    ins = nc.tensor.transpose(bank[6][:, P * i:P * i + P], prob[n % 2][:, P * i:P * i + P], ident[:])
                ins.then_inc(probT_done, 1)

            def pv(n):
                tb, h = divmod(n, AH)
                pe.wait_ge(probT_ready, n + 1)
                if n == 0:
                    pe.wait_ge(act_emptied, evacs_through(FIRST[S_VA] + 3, "act"))
                if h == 0 and tb:
                    pe.wait_ge(oa_emptied, tb)
                for i in range(tb + 1):
                    ins = nc.tensor.matmul(bank[7][:, AD * h:AD * h + AD], probT[n % 2][:, P * i:P * i + P],
                                           va[:, i, AD * h:AD * h + AD], start=(i == 0), stop=(i == tb))
                ins.then_inc(pv_done, 1)

            for s_ in range(3, S_OE):
                slot_ready(s_)
                if SLOTS[s_][0] == "a":
                    for half in range(2):
                        group_a(s_, half)
                        fills(s_, half)
                elif s_ < ATT_S0:
                    for half in range(2):
                        unit_b(s_, 2 * half)
                        unit_b(s_, 2 * half + 1)
                        fills(s_, half)
                    if s_ == ATT_S0 - 1:
                        qk(0)
                        qk(1)
                else:
                    for t in range(TB):
                        for half in range(2):
                            n = AH * (s_ - ATT_S0) + 2 * t + half
                            if n + 2 < NSTEP:
                                qk(n + 2)
                            unit_b(s_, t, part=(2 * half, 2 * half + 2))
                            prob_transpose(n)
                            if n:
                                pv(n - 1)
            pv(NSTEP - 1)
            pe.wait_ge(act_emptied, evacs_through(FIRST[S_OE] - 1, "act"))
            pe.wait_ge(mixed_b, TB)

            def rows_mixed(n, t):
                if n >= 4:
                    pe.wait_ge(mixed_a, 1 if t < TB - 1 else 2)
                if n == 7:
                    pe.wait_ge(oa_emptied, TB)

            transpose_blocks(B_FIRST, ROWS_1, rows_mixed, mixed_bank)
            for s_ in range(S_OE, S_ODD):
                slot_ready(s_)
                for t in range(TB):
                    unit_b(s_, t, hT_round=1 if s_ < S_OE + 2 and t == 0 else None)
            def odd_rows(n, t):
                pe.wait_ge(normed, TB + t + 1)
                if n >= 4:
                    pe.wait_ge(dve_emptied, 2 * TB)

            transpose_blocks(range(KC), ROWS_2, odd_rows, odd_bank)

            def pe_taps(c):
                pe.wait_ge(diag_ready, PE_TAPS * (c + 1))
                pe.wait_ge(u_ready, c + 1)
                if c >= 3:
                    pe.wait_ge(sum_begun, c - 2)
                for k in range(PE_TAPS):
                    ins = nc.tensor.matmul(bank[c % 3][:], tap_diag[c % 2][k], upad[c % 3][:, k:k + S],
                                           start=(k == 0), stop=(k == PE_TAPS - 1))
                ins.then_inc(taps_done, 1)

            def ln_sum(c):
                pe.wait_ge(conv_done, c + 1)
                ins = nc.tensor.matmul(bank[3][:], ones[:], conv_y(c), start=(c == 0), stop=(c == KC - 1))
                if c == KC - 1:
                    ins.then_inc(mean_done, 1)

            def square_sum(i):
                pe.wait_ge(lnsq_paired, i + 1)
                for t in range(TB):
                    ins = nc.tensor.matmul(bank[0][:, t:t + 1], ln_sq[2 * i][:, P * t:P * t + P], ones[:, 0:1],
                                           start=(i == 0 and t == 0), stop=(i == KC // 2 - 1),
                                           skip_group_check=True)
                if i == KC // 2 - 1:
                    ins.then_inc(lnvar_done, 1)

            def spread_rstd():
                pe.wait_ge(lndiag_ready, 1)
                for t in range(TB):
                    ins = nc.tensor.matmul(bank[1][:, P * t:P * t + P], ones[:], ln_diag[:, P * t:P * t + P],
                                           start=True, stop=True)
                ins.then_inc(lnrstd_wide, 1)

            def last_sums():
                ln_sum(KC - 2)
                ln_sum(KC - 1)

            LN_SUMS = {S_OO - 4: (0, 1, 2, 3), S_OO - 3: (4,), S_OO - 2: (5,)}
            for s_ in range(S_ODD, S_OO):
                slot_ready(s_)
                for c in LN_SUMS.get(s_, ()):
                    ln_sum(c)
                if s_ < S_OO - 1:
                    group_a(s_, 0, hT_round=2 if s_ == S_ODD else None)
                    if s_ - S_ODD in range(1, KC + 1):
                        pe_taps(s_ - S_ODD - 1)
                    group_a(s_, 1, between={3 * KC // 2: last_sums} if s_ == S_OO - 2 else {})
                else:
                    pe.wait_ge(sum_begun, KC)
                    group_a(s_, 0, between={4: lambda: square_sum(0), 12: lambda: square_sum(1),
                                            20: lambda: square_sum(2)})
                    square_sum(3)
                    group_a(s_, 1, between={10: spread_rstd})
            keep_clock(WARM_LN, 2)
            for s_ in range(S_OO, NS):
                slot_ready(s_)
                for t in range(TB):
                    unit_b(s_, t, hT_round=3 if s_ < S_OO + 2 and t == 0 else None)


_INS = ["x", "rel_bias", "norm_even", "w_in_even", "w_gla_lr", "b_gla_lr", "gla_norm", "w_out_even", "norm_odd",
        "w_in_odd", "conv_w", "conv_b", "conv_ln_g", "conv_ln_b", "w_out_odd", "norm_f"]
_OUTS = [((1, 512, 1024), "float32")]


def kernel(**inputs):
    import numpy as _np
    import concourse.bacc as _bacc
    from concourse import mybir as _mybir
    from concourse.bass_utils import run_bass_kernel_spmd as _run

    nc = _bacc.Bacc("TRN2", target_bir_lowering=False, num_devices=1)
    arrays, args = {}, []
    for name in _INS:
        a = _np.ascontiguousarray(inputs[name])
        arrays[f"in_{name}_dram"] = a
        args.append(nc.dram_tensor(f"in_{name}_dram", a.shape, _mybir.dt.from_np(a.dtype), kind="ExternalInput").ap())
    for i, (shape, dtype) in enumerate(_OUTS):
        dt = _mybir.dt.from_np(_np.dtype(dtype))
        args.append(nc.dram_tensor(f"out_{i}_dram", shape, dt, kind="ExternalOutput").ap())
    hybrid_trunk(nc, *args)
    r = _run(nc, [arrays], core_ids=[0])
    return r.results[0]["out_0_dram"]
```
